# Optimizing a Trainium2 kernel written in Bass

```python
import math
import jax
import jax.numpy as jnp
from jax import lax
import numpy as np

D_MODEL = 1024
BATCH = 1
SEQ = 512
DEPTH = 2
DEC_BATCH = 8
DEC_SEQ = 8
PAST_LEN = 2048
PAGE_SIZE = 128

N_A_LAYERS = DEPTH // 2
N_B_LAYERS = DEPTH - N_A_LAYERS
SSM_GROUP = 16
SSM_GROUPS = D_MODEL // SSM_GROUP
SSM_STATE = 64
N_HEADS = 8
HEAD_DK = 64
HEAD_DV = 2 * HEAD_DK
D_FF = -(-(-(-8 * D_MODEL // 3)) // 256) * 256
Q_BLOCK = 128
EPS = 1e-6
DT_MIN = 1e-3
DT_MAX = 1e-1
ATTN_SCALE = HEAD_DK ** -0.5
F32 = jnp.float32

kernel_name = 'yoco_s5_diffattn_adaln_step'

def rms_norm(x, g):
    xf = x.astype(F32)
    y = xf * lax.rsqrt(jnp.mean(xf * xf, axis=-1, keepdims=True) + EPS)
    return (y * g.astype(F32)).astype(x.dtype)

def ada_mod(c, w, b, n):
    m = jax.nn.silu(c) @ w + b
    return jnp.split(m[:, None, :], n, axis=-1)

def modulate(x, g, shift, scale):
    return rms_norm(x, g) * (1.0 + scale) + shift

def ssm_discretize(lam_re, lam_im, log_step, b_re, b_im):
    dt = jnp.exp(log_step.astype(F32))[:, None]
    lr, li = lam_re.astype(F32), lam_im.astype(F32)
    mag = jnp.exp(lr * dt)
    a_re, a_im = mag * jnp.cos(li * dt), mag * jnp.sin(li * dt)
    nr, ni = a_re - 1.0, a_im
    den = lr * lr + li * li
    f_re = (nr * lr + ni * li) / den
    f_im = (ni * lr - nr * li) / den
    br, bi = b_re.astype(F32), b_im.astype(F32)
    bb_re = f_re[..., None] * br - f_im[..., None] * bi
    bb_im = f_re[..., None] * bi + f_im[..., None] * br
    return a_re, a_im, bb_re, bb_im

def _ssm_combine(e1, e2):
    a1r, a1i, b1r, b1i = e1
    a2r, a2i, b2r, b2i = e2
    return (a2r * a1r - a2i * a1i,
            a2r * a1i + a2i * a1r,
            a2r * b1r - a2i * b1i + b2r,
            a2r * b1i + a2i * b1r + b2i)

def s5_mixer(u, h0_re, h0_im, lam_re, lam_im, log_step, b_re, b_im, c_re, c_im, d_skip, w_glu):
    bsz, L, _ = u.shape
    uf = u.astype(F32)
    ug = uf.reshape(bsz, L, SSM_GROUPS, SSM_GROUP)
    a_re, a_im, bb_re, bb_im = ssm_discretize(lam_re, lam_im, log_step, b_re, b_im)
    bu_re = jnp.einsum('blgp,gnp->blgn', ug, bb_re)
    bu_im = jnp.einsum('blgp,gnp->blgn', ug, bb_im)
    bu_re = bu_re.at[:, 0].add(a_re * h0_re - a_im * h0_im)
    bu_im = bu_im.at[:, 0].add(a_re * h0_im + a_im * h0_re)
    shape = bu_re.shape
    _, _, h_re, h_im = lax.associative_scan(
        _ssm_combine,
        (jnp.broadcast_to(a_re, shape), jnp.broadcast_to(a_im, shape), bu_re, bu_im),
        axis=1)
    y = (jnp.einsum('blgn,gpn->blgp', h_re, c_re.astype(F32))
         - jnp.einsum('blgn,gpn->blgp', h_im, c_im.astype(F32)))
    y = y.reshape(bsz, L, D_MODEL) + d_skip.astype(F32) * uf
    g = jax.nn.gelu(y)
    za, zb = jnp.split(g @ w_glu.astype(F32), 2, axis=-1)
    out = za * jax.nn.sigmoid(zb)
    return out.astype(u.dtype), h_re[:, -1], h_im[:, -1]

def swiglu_ffn(h, w13, w2):
    a, b = jnp.split(h @ w13, 2, axis=-1)
    return (jax.nn.silu(a) * b) @ w2

def shared_kv(x, c, norm_kv, w_ada_kv, b_ada_kv, w_kv, k_norm):
    bsz, L, _ = x.shape
    shift, scale = ada_mod(c, w_ada_kv, b_ada_kv, 2)
    h = modulate(x, norm_kv, shift, scale)
    k, v = jnp.split(h @ w_kv, [N_HEADS * 2 * HEAD_DK], axis=-1)
    k = rms_norm(k.reshape(bsz, L, N_HEADS, 2, HEAD_DK), k_norm)
    return k, v.reshape(bsz, L, N_HEADS, HEAD_DV)

def diff_attn_prompt(q, k, v, lam):
    bsz, L = q.shape[:2]
    nb = L // Q_BLOCK
    qb = q.reshape(bsz, nb, Q_BLOCK, N_HEADS, 2, HEAD_DK).transpose(1, 0, 2, 3, 4, 5)
    kpos = jnp.arange(L)

    def block(args):
        qi, i = args
        s = jnp.einsum('bqhmd,bkhmd->bhmqk', qi, k, preferred_element_type=F32) * ATTN_SCALE
        qpos = i * Q_BLOCK + jnp.arange(Q_BLOCK)
        s = jnp.where(kpos[None, :] <= qpos[:, None], s, -jnp.inf)
        p = jax.nn.softmax(s, axis=-1)
        w = p[:, :, 0] - lam * p[:, :, 1]
        return jnp.einsum('bhqk,bkhd->bqhd', w.astype(v.dtype), v)

    o = lax.map(block, (qb, jnp.arange(nb)))
    return o.transpose(1, 0, 2, 3, 4).reshape(bsz, L, N_HEADS, HEAD_DV)

def diff_attn_sample(q, k_past, v_past, k_new, v_new, lam):
    T = q.shape[1]
    P = k_past.shape[1]
    s_past = jnp.einsum('bqhmd,bkhmd->bhmqk', q, k_past, preferred_element_type=F32) * ATTN_SCALE
    s_new = jnp.einsum('bqhmd,bkhmd->bhmqk', q, k_new, preferred_element_type=F32) * ATTN_SCALE
    causal = jnp.arange(T)[None, :] <= jnp.arange(T)[:, None]
    s_new = jnp.where(causal, s_new, -jnp.inf)
    p = jax.nn.softmax(jnp.concatenate([s_past, s_new], axis=-1), axis=-1)
    w = (p[:, :, 0] - lam * p[:, :, 1]).astype(v_new.dtype)
    return (jnp.einsum('bhqk,bkhd->bqhd', w[..., :P], v_past)
            + jnp.einsum('bhqk,bkhd->bqhd', w[..., P:], v_new))

def diff_attention_layer(h, k, v, past, w_q, q_norm, lam_p, subln, w_o, lam_init):
    bsz, L, _ = h.shape
    q = rms_norm((h @ w_q).reshape(bsz, L, N_HEADS, 2, HEAD_DK), q_norm)
    lp = lam_p.astype(F32)
    lam = jnp.exp(jnp.sum(lp[0] * lp[1])) - jnp.exp(jnp.sum(lp[2] * lp[3])) + lam_init
    if past is None:
        o = diff_attn_prompt(q, k, v, lam)
    else:
        o = diff_attn_sample(q, past[0], past[1], k, v, lam)
    o = rms_norm(o, subln) * (1.0 - lam_init)
    return o.reshape(bsz, L, N_HEADS * HEAD_DV) @ w_o

def run_group(x, c, h0_re, h0_im, past, p):
    new_re, new_im = [], []
    k = v = None
    for layer in range(DEPTH):
        sh, sc, gt = ada_mod(c, p['w_ada_mix'][layer], p['b_ada_mix'][layer], 3)
        h = modulate(x, p['norm_mix'][layer], sh, sc)
        if layer < N_A_LAYERS:
            a = layer
            out, hr, hi = s5_mixer(h, h0_re[a], h0_im[a], p['ssm_lam_re'][a], p['ssm_lam_im'][a],
                                   p['ssm_log_step'][a], p['ssm_b_re'][a], p['ssm_b_im'][a],
                                   p['ssm_c_re'][a], p['ssm_c_im'][a], p['ssm_d'][a], p['ssm_w_glu'][a])
            new_re.append(hr)
            new_im.append(hi)
        else:
            j = layer - N_A_LAYERS
            lam_init = 0.8 - 0.6 * math.exp(-0.3 * layer)
            out = diff_attention_layer(h, k, v, past, p['w_q'][j], p['q_norm'][j], p['diff_lambda'][j],
                                       p['subln'][j], p['w_o'][j], lam_init)
        x = x + gt * out
        sh, sc, gt = ada_mod(c, p['w_ada_ffn'][layer], p['b_ada_ffn'][layer], 3)
        h = modulate(x, p['norm_ffn'][layer], sh, sc)
        x = x + gt * swiglu_ffn(h, p['ffn_w13'][layer], p['ffn_w2'][layer])
        if layer == N_A_LAYERS - 1:
            k, v = shared_kv(x, c, p['norm_kv'], p['w_ada_kv'], p['b_ada_kv'], p['w_kv'], p['k_norm'])
    return x, jnp.stack(new_re), jnp.stack(new_im), k, v

def setup_inputs(seed: int = 0) -> dict:
    key = jax.random.key(seed)
    ks = iter(jax.random.split(key, 48))

    def nrm(shape, s):
        return jax.random.normal(next(ks), shape, F32) * s

    D, G, N, P, H = D_MODEL, SSM_GROUPS, SSM_STATE, SSM_GROUP, N_HEADS
    n_pages = PAST_LEN // PAGE_SIZE
    n_used = DEC_BATCH * n_pages
    n_pool = n_used + max(1, n_used // 4)
    ada_s = 0.5 * D ** -0.5
    inp = {}
    inp['x_prompt'] = nrm((BATCH, SEQ, D), 1.0)
    inp['x_sample'] = nrm((DEC_BATCH, DEC_SEQ, D), 1.0)
    inp['state_ssm_re'] = nrm((N_A_LAYERS, DEC_BATCH, G, N), 0.3)
    inp['state_ssm_im'] = nrm((N_A_LAYERS, DEC_BATCH, G, N), 0.3)
    inp['cache_k'] = nrm((n_pool, PAGE_SIZE, H, 2, HEAD_DK), 1.0)
    inp['cache_v'] = nrm((n_pool, PAGE_SIZE, H, HEAD_DV), 1.0)
    inp['page_table'] = jax.random.permutation(next(ks), n_pool)[:n_used].reshape(
        DEC_BATCH, n_pages).astype(jnp.int32)
    inp['c_prompt'] = nrm((BATCH, D), 1.0)
    inp['c_sample'] = nrm((DEC_BATCH, D), 1.0)
    inp['norm_mix'] = 1.0 + nrm((DEPTH, D), 0.02)
    inp['w_ada_mix'] = nrm((DEPTH, D, 3 * D), ada_s)
    inp['b_ada_mix'] = nrm((DEPTH, 3 * D), 0.02)
    inp['norm_ffn'] = 1.0 + nrm((DEPTH, D), 0.02)
    inp['w_ada_ffn'] = nrm((DEPTH, D, 3 * D), ada_s)
    inp['b_ada_ffn'] = nrm((DEPTH, 3 * D), 0.02)
    inp['ffn_w13'] = nrm((DEPTH, D, 2 * D_FF), D ** -0.5)
    inp['ffn_w2'] = nrm((DEPTH, D_FF, D), D_FF ** -0.5)
    inp['ssm_lam_re'] = -0.5 + nrm((N_A_LAYERS, G, N), 0.01)
    inp['ssm_lam_im'] = jnp.pi * jnp.arange(N, dtype=F32) + nrm((N_A_LAYERS, G, N), 0.01)
    inp['ssm_log_step'] = jax.random.uniform(next(ks), (N_A_LAYERS, G), F32,
                                             math.log(DT_MIN), math.log(DT_MAX))
    inp['ssm_b_re'] = nrm((N_A_LAYERS, G, N, P), (2 * P) ** -0.5)
    inp['ssm_b_im'] = nrm((N_A_LAYERS, G, N, P), (2 * P) ** -0.5)
    inp['ssm_c_re'] = nrm((N_A_LAYERS, G, P, N), (2 * N) ** -0.5)
    inp['ssm_c_im'] = nrm((N_A_LAYERS, G, P, N), (2 * N) ** -0.5)
    inp['ssm_d'] = nrm((N_A_LAYERS, D), 1.0)
    inp['ssm_w_glu'] = nrm((N_A_LAYERS, D, 2 * D), D ** -0.5)
    inp['norm_kv'] = 1.0 + nrm((D,), 0.02)
    inp['w_ada_kv'] = nrm((D, 2 * D), ada_s)
    inp['b_ada_kv'] = nrm((2 * D,), 0.02)
    inp['w_kv'] = nrm((D, H * 2 * HEAD_DK + H * HEAD_DV), D ** -0.5)
    inp['k_norm'] = 1.0 + nrm((2, HEAD_DK), 0.02)
    inp['w_q'] = nrm((N_B_LAYERS, D, H * 2 * HEAD_DK), D ** -0.5)
    inp['q_norm'] = 1.0 + nrm((N_B_LAYERS, 2, HEAD_DK), 0.02)
    inp['diff_lambda'] = nrm((N_B_LAYERS, 4, HEAD_DK), 0.1)
    inp['subln'] = 1.0 + nrm((N_B_LAYERS, HEAD_DV), 0.02)
    inp['w_o'] = nrm((N_B_LAYERS, H * HEAD_DV, D), (H * HEAD_DV) ** -0.5)
    return inp

def reference(x_prompt, x_sample, state_ssm_re, state_ssm_im, cache_k, cache_v, page_table,
              c_prompt, c_sample, norm_mix, w_ada_mix, b_ada_mix, norm_ffn, w_ada_ffn, b_ada_ffn,
              ffn_w13, ffn_w2, ssm_lam_re, ssm_lam_im, ssm_log_step, ssm_b_re, ssm_b_im,
              ssm_c_re, ssm_c_im, ssm_d, ssm_w_glu, norm_kv, w_ada_kv, b_ada_kv, w_kv, k_norm,
              w_q, q_norm, diff_lambda, subln, w_o):
    p = {'norm_mix': norm_mix, 'w_ada_mix': w_ada_mix, 'b_ada_mix': b_ada_mix,
         'norm_ffn': norm_ffn, 'w_ada_ffn': w_ada_ffn, 'b_ada_ffn': b_ada_ffn,
         'ffn_w13': ffn_w13, 'ffn_w2': ffn_w2,
         'ssm_lam_re': ssm_lam_re, 'ssm_lam_im': ssm_lam_im, 'ssm_log_step': ssm_log_step,
         'ssm_b_re': ssm_b_re, 'ssm_b_im': ssm_b_im, 'ssm_c_re': ssm_c_re, 'ssm_c_im': ssm_c_im,
         'ssm_d': ssm_d, 'ssm_w_glu': ssm_w_glu,
         'norm_kv': norm_kv, 'w_ada_kv': w_ada_kv, 'b_ada_kv': b_ada_kv, 'w_kv': w_kv, 'k_norm': k_norm,
         'w_q': w_q, 'q_norm': q_norm, 'diff_lambda': diff_lambda, 'subln': subln, 'w_o': w_o}

    bsz = x_prompt.shape[0]
    h0 = jnp.zeros((N_A_LAYERS, bsz, SSM_GROUPS, SSM_STATE), F32)
    y_prompt, ssm_re_prompt, ssm_im_prompt, k_prompt, v_prompt = run_group(
        x_prompt, c_prompt, h0, h0, None, p)

    db, n_pages = page_table.shape
    past_len = n_pages * cache_k.shape[1]
    k_past = cache_k[page_table].reshape(db, past_len, N_HEADS, 2, HEAD_DK)
    v_past = cache_v[page_table].reshape(db, past_len, N_HEADS, HEAD_DV)
    y_sample, ssm_re_sample, ssm_im_sample, k_sample, v_sample = run_group(
        x_sample, c_sample, state_ssm_re.astype(F32), state_ssm_im.astype(F32), (k_past, v_past), p)

    return (y_prompt, y_sample, ssm_re_prompt, ssm_im_prompt, ssm_re_sample, ssm_im_sample,
            k_prompt, v_prompt, k_sample, v_sample)


_drawn_inputs = setup_inputs


def setup_inputs(seed=0):
    import zlib

    import numpy as np

    out = dict(_drawn_inputs(seed))
    spreads = {}
    factors = {'norm_mix': 3.337,
     'norm_ffn': 7.168,
     'ssm_lam_re': 16.202,
     'norm_kv': 8.225,
     'k_norm': 7.9,
     'q_norm': 29.354,
     'diff_lambda': 64.0,
     'subln': 64.0}
    for name, (base, spread) in spreads.items():
        noise = np.random.default_rng([zlib.crc32(name.encode()), seed]).standard_normal(out[name].shape)
        drawn = base * np.exp(spread * noise) if base else spread * noise
        out[name] = jnp.asarray(drawn.astype(out[name].dtype))
    for name, factor in factors.items():
        out[name] = (out[name] * factor).astype(out[name].dtype)
    return out
```

```python
from contextlib import ExitStack
import math

import concourse.bass as bass
from concourse import mybir

ALU = mybir.AluOpType
ACT = mybir.ActivationFunctionType
F32 = mybir.dt.float32
F32R = mybir.dt.float32r
I32 = mybir.dt.int32
AX_X = mybir.AxisListType.X
ds = bass.ds

P = 128
BANK = 512
EPS = 1e-6
MASKED = -1.0e30
ROUND = 12582912.0
TWO_PI_PARTS = (6.28125, 0.001934051513671875, 1.2556659146e-06)
PI_BELOW = 3.1415925


class Steps:

    def __init__(self, eng, sem):
        self.eng, self.sem, self.start, self.k = eng, sem, 0, 0

    def __call__(self, ins):
        ins.then_inc(self.sem, 1)
        self.k += 1
        self.eng.wait_ge(self.sem, self.start + self.k)

    def loop(self, first, turns, per):
        steps = self

        class Turns:
            def __enter__(self):
                self.base = steps.start + steps.k
                self.fori = steps.eng.Fori(first, first + turns)
                i = self.fori.__enter__()
                steps.start, steps.k = self.base - first * per + i * per, 0
                return i

            def __exit__(self, *e):
                r = self.fori.__exit__(*e)
                assert e[0] is not None or steps.k == per, (steps.k, per)
                steps.start, steps.k = self.base + turns * per, 0
                return r

        return Turns()


def yoco_step(nc, a, out):
    SEQ, D = a["x_prompt"].shape[1:]
    DB, DS = a["x_sample"].shape[:2]
    G, N, PP = a["ssm_b_re"].shape[1:]
    H, DK = a["cache_k"].shape[2], a["cache_k"].shape[4]
    DV = a["cache_v"].shape[3]
    PAGES, NPOOL = a["page_table"].shape[1], a["cache_k"].shape[0]
    DFF = a["ffn_w2"].shape[1]
    T = SEQ + DB * DS
    HALF = T // 2
    KD = D // P
    FT = DFF // P
    CH = DS
    NCH = T // CH
    PCH = SEQ // CH
    J = G // 2
    TAU = CH + 1
    C9 = 1 + DB
    SCALE = DK ** -0.5
    LAM_INIT = 0.8 - 0.6 * math.exp(-0.3 * 1)
    QB = SEQ // P
    HQ = 2 * CH
    assert D == 1024 and 2 * DK == P and DV == P and CH * PP == P and 2 * N == P and H == KD
    assert a["cache_k"].shape[1] == P and PAGES == 16 and SEQ == BANK

    PLAN = [("small", 1), ("x", 5), ("ada0", 1), ("norm0", 1), ("ssm_k", 4), ("ada1", 1), ("ssm_v", 4),
            ("ada2", 1), ("ssm_w", 4), ("ada3", 1), ("ada4", 1), ("ssm_y", 4), ("ssm_h", 1),
            ("glu", 8), ("norm1", 1), ("up0", 22), ("down0", 8), ("norm2", 1), ("kv", 16), ("q", 8),
            ("khead", 8), ("qhead", 8), ("ktok", 5), ("vtok", 5), ("attn", None),
            ("ohead", 8), ("wo", 8), ("norm3", 1), ("up1", 22), ("down1", 8), ("y", 5)]
    USES, seen = {}, [0, 0]
    for name, n in PLAN:
        USES[name] = tuple(seen)
        seen[0] += H * (QB + 1) if n is None else (n + 1) // 2
        seen[1] += H * QB if n is None else n // 2

    COUNT = {"ada0": 24, "ada1": 24, "ada2": 16, "ada3": 24, "ada4": 24, "glu": 16, "up0": 2 * FT,
             "down0": 4 * KD, "kv": 16, "q": 8, "wo": 8, "up1": 2 * FT, "down1": 4 * KD}
    SLABS, n_slabs = {}, 0
    for name, n in COUNT.items():
        SLABS[name] = n_slabs
        n_slabs += n
        assert n % 4 == 0

    DENSE0 = SLABS["glu"]

    PAIR = [(0, 0, 8), (1, 0, 8)]
    ONE = [(0, 0, 8)]
    LONG = [(0, 0, 6), (0, 6, 6), (0, 12, 6), (0, 18, 4)]
    DENSE = {"glu": (8, PAIR, 2), "up0": (22, PAIR, 2), "down0": (8, LONG, 2), "kv": (16, ONE, 4),
             "q": (8, ONE, 4), "wo": (8, ONE, 4), "up1": (22, PAIR, 2), "down1": (8, LONG, 2)}
    INNER, n_inner = {}, 0
    for name, (units, slabs, _) in DENSE.items():
        INNER[name] = n_inner
        n_inner += units * (len(slabs) - 1)

    base = -(-nc.sbuf_base // 64) * 64
    place = [base]

    def keep(name, shape, dt=F32):
        size = 4 * math.prod(shape[1:])
        t = nc.alloc_sbuf_tensor_at(name, shape, dt, offset=place[0])
        place[0] += -(-size // 32) * 32
        return t

    x = keep("x", [P, KD, T])
    raw = keep("raw", [P, 4, 8, P])
    vec = keep("vec", [P, 3 * P])
    cond = keep("cond", [P, KD, C9])
    mod = keep("mod", [P, 5, 24, C9])
    gain = keep("gain", [P, 5, KD, C9])
    t1 = keep("t1", [P, 2, T])
    t2 = keep("t2", [P, 2, T])
    rstd = keep("rstd", [P, T])
    sqs = rstd
    sqt = keep("sqt", [P, HALF])
    ident = keep("ident", [P, P])
    ones = keep("ones", [P, P])
    blockd = keep("blockd", [P, P])
    eps = keep("eps", [P, 1])
    neglam = keep("neglam", [P, 1])
    gaino = keep("gaino", [P, 1])
    causal = keep("causal", [8, CH])
    pages = keep("pages", [1, DB * PAGES], I32)
    mark = keep("mark", [P, 12])
    over = place[0]

    def share(name, shape, at, dt=F32):
        return nc.alloc_sbuf_tensor_at(name, shape, dt, offset=over + at)

    KB = 1024
    SMALL = 21
    wh = share("wh", [P, (2 * NCH + 1) * 2 * J], 0)
    drive = wh[:, 0:NCH * 2 * J].rearrange("p (c r j) -> p c r j", c=NCH, r=2)
    hs = wh[:, NCH * 2 * J:].rearrange("p (c r j) -> p c r j", c=NCH + 1, r=2)
    vmat = wh[:, 0:2 * CH * J * PP].rearrange("p (r j s q) -> p r j s q", r=2, j=J, s=CH)
    o = 4 * (2 * NCH + 1) * 2 * J
    vk = share("vk", [P, G * P], o)
    vT = vk[:, :].rearrange("p (j r m) -> p j r m", j=J, r=2)
    kmat = vk[:, :].rearrange("p (g m) -> p g m", g=G)
    krow = share("krow", [PP, 2, 16, P], o)
    o += 4 * G * P
    cpow = share("cpow", [P, J, 2, TAU, PP], o)
    o += 4 * J * 2 * TAU * PP
    uch = share("uch", [P, G, NCH], o)
    craw = share("craw", [P, 2, 4, P], o)
    hraw = share("hraw", [P, 2, 2, P], o + 4 * KB)
    xtok = share("xtok", [P, 2, D], o + 6 * KB)
    v1 = share("v1", [P, P], o + 14 * KB)
    v2 = share("v2", [P, P], o + 14 * KB + 512)
    v3 = share("v3", [P, P], o + 15 * KB)
    lst = share("lst", [96, 2], o + 15 * KB + 512)
    lrow = share("lrow", [P, 4, DK], o + 16 * KB)
    ltmp = share("ltmp", [P, 2, DK], o + 17 * KB)
    lsum = share("lsum", [P, 4], o + 17 * KB + 512)
    o += 4 * G * NCH
    bmat = share("bmat", [P, 2, J, PP], o)
    bbar = share("bbar", [P, 2, J, PP], o + 4 * KB)
    cT = share("cT", [P, 2, J, PP], o + 8 * KB)
    ysb = share("ysb", [P, 2, 16 * NCH], o)
    hout = share("hout", [P, 6, P], o + 9 * KB)
    o += 12 * KB
    pw = share("pw", [P, TAU, 2, J], o)
    pws = share("pws", [P, 2, J], o + 4 * TAU * 2 * J)
    h0 = share("h0", [P, 2, DB * J], o + 3 * KB)
    hfin = share("hfin", [P, 2, DB, J], o + 5 * KB)
    tiny = share("tiny", [P, 14, J], o + 7 * KB)
    tA = share("tA", [P, J * PP], o + 9 * KB)
    tB = share("tB", [P, J * PP], o + 11 * KB)
    pA = share("pA", [P, J * PP], o + 13 * KB)
    pB = share("pB", [P, J * PP], o + 15 * KB)
    o += 17 * KB
    assert over + o <= nc.sbuf_usable_end, over + o
    yin = share("yin", [P, 2, CH, NCH], 120 * KB)
    uin = share("uin", [P, 2, CH, NCH], 125 * KB)
    ws = share("ws", [P, 2, 2, 8, P], 0, F32R)
    hr = share("hr", [P, KD, 2, T], 16 * KB, F32R)
    gr = share("gr", [P, FT, 2, T], 52 * KB, F32R)
    assert over + 52 * KB + 8 * FT * T <= nc.sbuf_usable_end, over + 52 * KB + 8 * FT * T
    kvT = share("kvT", [P, 2 * H, T], 52 * KB)
    kT, vTf = kvT[:, 0:H], kvT[:, H:2 * H]
    qT = share("qT", [P, H, T], 88 * KB)
    oT = vTf
    qbd = share("qbd", [P, H, DB, 2, CH], 106 * KB)
    tok = share("tok", [P, 2, D], 110 * KB)
    vtok = share("vtok", [P, QB, H, DV], 118 * KB)
    e01 = share("e01", [P, 2, SEQ], 134 * KB)
    wtT = share("wtT", [P, QB, SEQ], 138 * KB)
    l01 = share("l01", [P, 8], 146 * KB)
    qh = share("qh", [P, SEQ], 0)
    kh = share("kh", [P, SEQ], 2 * KB)
    vh = share("vh", [P, QB, DV], 4 * KB)
    tri = share("tri", [P, P], 6 * KB)
    kpg = share("kpg", [P, 4, H, P], 0)
    vpg = share("vpg", [P, 4, H, DV], 16 * KB)
    kTs = share("kTs", [P, 2, 2, BANK], 32 * KB)
    sc = share("sc", [P, 2, PAGES + 1, P], 110 * KB)
    mx = share("mx", [P, 4, P], 128 * KB)
    kn = share("kn", [P, H, CH], 130 * KB)
    vn = share("vn", [CH, D], 131 * KB)
    on = share("on", [P, H, 2, CH], 139 * KB)

    ps = nc.alloc_psum_tensor("ps", [P, 8, BANK], F32)

    u_scr = nc.dram_tensor("u_scr", [D, CH, NCH], F32, kind="Internal").ap()
    y_scr = nc.dram_tensor("y_scr", [D, CH, NCH], F32, kind="Internal").ap()
    k_scr = nc.dram_tensor("k_scr", [PP, G, P], F32, kind="Internal").ap()

    with ExitStack() as ctx:
        def sem(name):
            return ctx.enter_context(nc.semaphore(name))

        full = [sem(f"full{s}") for s in range(2)]
        free = [sem(f"free{s}") for s in range(2)]
        raw_full = [sem(f"raw_full{s}") for s in range(4)]
        raw_done = [sem(f"raw_done{s}") for s in range(4)]
        in_small, in_x, in_b = sem("in_small"), [sem("in_x0"), sem("in_x1")], sem("in_b")
        dve_step, act_step, pool_step = sem("dve_step"), sem("act_step"), sem("pool_step")
        consts, v3_built = sem("consts"), sem("v3_built")
        x_ready, sq_ready, root_ready = sem("x_ready"), sem("sq_ready"), sem("root_ready")
        cond_ready, dt_ready, sincos_in, sincos_out = sem("cond_ready"), sem("dt_ready"), sem("sincos_in"), sem("sincos_out")
        mod_ready, bbar_ready, cpow_ready, v_ready = sem("mod_ready"), sem("bbar_ready"), sem("cpow_ready"), sem("v_ready")
        t1_ready, t2_sample, t2_ready, h_high, h_ready = sem("t1_ready"), sem("t2_sample"), sem("t2_ready"), sem("h_high"), sem("h_ready")
        t2_prompt = sem("t2_prompt")
        u_got, kmat_zero, kmat_got = sem("u_got"), sem("kmat_zero"), sem("kmat_got")
        u_put, k_put = [sem("u_put0"), sem("u_put1")], [sem("k_put0"), sem("k_put1")]
        y_put, y_got, hs_ready, hfin_ready = [sem("y_put0"), sem("y_put1")], [sem("y_got0"), sem("y_got1")], sem("hs_ready"), sem("hfin_ready")
        hout_ready, yu_ready = sem("hout_ready"), sem("yu_ready")
        slab_high, slab_read = sem("slab_high"), sem("slab_read")
        e_ready, g_high, g_ready, kv_ready = sem("e_ready"), sem("g_high"), sem("g_ready"), sem("kv_ready")
        sq_head, root_head, head_ready = sem("sq_head"), sem("root_head"), sem("head_ready")
        tok_ready, tok_put, vtok_ready = sem("tok_ready"), [sem("tok_put0"), sem("tok_put1")], sem("vtok_ready")
        head_in, s_max, e_done, w_done, wt_done, pv_out = sem("head_in"), sem("s_max"), sem("e_done"), sem("w_done"), sem("wt_done"), sem("pv_out")
        k_full, v_full = [sem(f"k_full{s}") for s in range(4)], [sem(f"v_full{s}") for s in range(4)]
        k_turned, kt_ready, scored, s_copied, v_used = sem("k_turned"), sem("kt_ready"), sem("scored"), sem("s_copied"), sem("v_used")
        kn_ready, vn_full, new_scored, m_ready, m_turned, d_ready, m_spread, s_low, e_full, l_ready, l_spread, l_read, vn_used, o_ready = (
            sem("kn_ready"), sem("vn_full"), sem("new_scored"), sem("m_ready"), sem("m_turned"), sem("d_ready"), sem("m_spread"),
            sem("s_low"), sem("e_full"), sem("l_ready"), sem("l_spread"), sem("l_read"), sem("vn_used"), sem("o_ready"))
        qbd_ready, sinit, put, vput, in_pages = sem("qbd_ready"), sem("sinit"), sem("put"), sem("vput"), sem("in_pages")
        head_h = sem("head_h")

        def uses(phase, s, i=0):
            return USES[phase][s] + i

        def wait_unit(eng, phase, s, i=0):
            eng.wait_ge(full[s], uses(phase, s, i) + 1)

        def wait_set(phase, s, i=0):
            n = uses(phase, s, i)
            if not (isinstance(n, int) and n == 0):
                nc.tensor.wait_ge(free[s], n)

        def halves(t):
            return t.rearrange("p (a b) -> p a b", a=2)

        dtok = [a["x_prompt"][0, i * P:(i + 1) * P, :] for i in range(QB)] + [
            a["x_sample"].rearrange("b t d -> (b t) d")]
        NTOK = [P] * QB + [DB * DS]

        def slab_source(name):
            kp = "(k p) n -> p k n"
            w = {"ada0": a["w_ada_mix"][0], "ada1": a["w_ada_ffn"][0], "ada2": a["w_ada_kv"],
                 "ada3": a["w_ada_mix"][1], "ada4": a["w_ada_ffn"][1], "glu": a["ssm_w_glu"][0],
                 "up0": a["ffn_w13"][0], "down0": a["ffn_w2"][0], "kv": a["w_kv"], "q": a["w_q"][0],
                 "wo": a["w_o"][0], "up1": a["ffn_w13"][1], "down1": a["ffn_w2"][1]}[name]
            return w.rearrange(kp, p=P)

        block = ctx.enter_context(nc.Block())

        @block.sync
        def _(sp):
            def small(dst, src):
                sp.dma_start(dst, src).then_inc(in_small, 16)

            rows = "l (k p) -> (l k) p"
            small(v1[0:8, :], a["c_prompt"].rearrange(rows, p=P))
            small(v1[8:72, :], a["c_sample"].rearrange(rows, p=P))
            small(v1[72:88, :], a["norm_mix"].rearrange(rows, p=P))
            small(v1[88:104, :], a["norm_ffn"].rearrange(rows, p=P))
            small(v1[104:112, :], a["norm_kv"].rearrange("(k p) -> k p", p=P))
            small(v1[112:120, :], a["ssm_d"].rearrange(rows, p=P))
            small(v1[120:121, :], a["k_norm"].rearrange("(o m) d -> o (m d)", o=1))
            small(v1[121:122, :], a["q_norm"].rearrange("o m d -> o (m d)"))
            small(v1[122:123, :], a["subln"])
            small(v2[0:48, :], a["b_ada_mix"].rearrange(rows, p=P))
            small(v2[48:96, :], a["b_ada_ffn"].rearrange(rows, p=P))
            small(v2[96:112, :], a["b_ada_kv"].rearrange("(k p) -> k p", p=P))
            small(v3[0:32, :], a["ssm_lam_re"][0].rearrange("(j g) n -> j (g n)", g=2))
            small(v3[32:64, :], a["ssm_lam_im"][0].rearrange("(j g) n -> j (g n)", g=2))
            small(lst[64:96, :], a["ssm_log_step"][0].rearrange("(j g) -> j g", g=2))
            for r, name in enumerate(("state_ssm_re", "state_ssm_im")):
                for k in range(2):
                    small(hraw[:, r, k, :], a[name][0, 4 * k:4 * k + 4].rearrange("b (j g) n -> (b j) (g n)", g=2))
            small(lrow[:, :, :].rearrange("p k d -> p (k d)"), a["diff_lambda"].rearrange("o k d -> o (k d)").to_broadcast([P, 4 * DK]))
            small(pages[:, :], a["page_table"].rearrange("(o b) p -> o (b p)", o=1))
            sp.dma_start(xtok[:, 0, :], dtok[0]).then_inc(in_x[0], 16)
            sp.dma_start(xtok[:, 1, :], dtok[1]).then_inc(in_x[1], 16)

            def slabs(name, cols, k0=lambda j: 0, nk=lambda j: 8, per=4):
                src, first = slab_source(name), SLABS[name]

                def turn(i):
                    for j in range(per):
                        slot = j % 4
                        if first or not isinstance(i, int):
                            sp.wait_ge(raw_done[slot], (first + j) // 4 + i * (per // 4))
                        a0, n = k0(j), nk(j)
                        sp.dma_start(raw[:, slot, 0:n, :], src[:, a0:a0 + n, ds(cols(i, j), P)]
                                     ).then_inc(raw_full[slot], 16)

                if first == 0:
                    turn(0)
                with sp.Fori(0 if first else 1, COUNT[name] // per) as i:
                    turn(i)

            def one(i, j):
                return i * (4 * P) + j * P

            def pair(half):
                return lambda i, j: i * (2 * P) + (j // 2) * P + (j % 2) * half

            def long(i, j):
                return i * (2 * P) + (j // 4) * P

            def page_loads(b, o, u, keys, values):
                slot = u % 4
                for go, seq, cache, dst, ready in ((keys, b, "cache_k", kpg, k_full), (values, b - 1, "cache_v", vpg, v_full)):
                    if not go:
                        continue
                    at = seq * PAGES + o * 8 + u
                    page = sp.value_load(pages[0:1, ds(at, 1)], min_val=0, max_val=NPOOL - 1)
                    if cache == "cache_v":
                        sp.wait_ge(v_used, at + 1)
                    elif not isinstance(at, int) or at > 3:
                        sp.wait_ge(k_turned, at - 3)
                    form = "o k h m d -> k (o h m d)" if cache == "cache_k" else "o k h d -> k (o h d)"
                    sp.dma_start(dst[:, slot].rearrange("p h m -> p (h m)"), a[cache][ds(page, 1)].rearrange(form)
                                 ).then_inc(ready[slot], 16)

            slabs("ada0", one)
            for name in ("ada1", "ada2", "ada3", "ada4"):
                slabs(name, one)
            slabs("glu", pair(D))
            for layer in range(2):
                slabs(f"up{layer}", pair(DFF))
                slabs(f"down{layer}", long, k0=lambda j: 6 * (j % 4), nk=lambda j: (6, 6, 6, 4)[j % 4], per=8)
                if layer:
                    break
                slabs("kv", one)
                slabs("q", one)
                sp.wait_ge(in_small, 16 * SMALL)
                for s in range(2):
                    sp.wait_ge(free[s], USES["ohead"][s])
                sp.wait_ge(qbd_ready, 2)
                for u in range(PAGES):
                    page_loads(0, u // 8, u % 8, True, False)
                with sp.Fori(1, DB) as b:
                    with sp.Fori(0, PAGES // 8) as o:
                        for u in range(8):
                            page_loads(b, o, u, True, True)
                for u in range(PAGES):
                    page_loads(DB, u // 8, u % 8, False, True)
                slabs("wo", one)
            sp.wait_ge(put, 16 * 6)
            for s in range(2):
                sp.wait_ge(tok_put[s], 16 * 3 * (3 - s))

        @block.tensor
        def _(pe):
            mm = nc.tensor.matmul

            def turn(dst, src, rows=P):
                return nc.tensor.transpose(dst, src, ident[0:rows, 0:rows])

            pe.wait_ge(consts, 3)
            pe.wait_ge(in_small, 16 * SMALL)
            pe.wait_ge(in_b, 16 * 18)
            pe.wait_ge(v3_built, 1)
            turn(ps[:, 0, 0:123], v1[0:123, :], 123)
            turn(ps[:, 0, P:P + 112], v2[0:112, :], 112)
            turn(ps[:, 0, 2 * P:2 * P + 96], v3[0:96, :], 96)
            for r in range(2):
                for k in range(2):
                    turn(ps[:, 1, (2 * r + k) * P:(2 * r + k + 1) * P], hraw[:, r, k, :])
                for k in range(4):
                    last = turn(ps[:, 2 + r, k * P:(k + 1) * P], craw[:, r, k, :])
            last.then_inc(full[0], 1)

            for i in range(QB + 1):
                s = i % 2
                wait_set("x", s, i // 2)
                pe.wait_ge(in_x[s], 16 * (i // 2 + 1))
                for k in range(KD):
                    last = turn(ps[:, 4 * s + k // 4, (k % 4) * P:(k % 4) * P + NTOK[i]],
                                xtok[0:NTOK[i], s, k * P:(k + 1) * P], NTOK[i])
                last.then_inc(full[s], 1)

            def ada(n):
                name = f"ada{n}"
                wait_set(name, 0)
                pe.wait_ge(cond_ready, 1)
                with pe.Fori(0, COUNT[name] // 4) as i:
                    for j in range(4):
                        pe.wait_ge(raw_full[j], 16 * (SLABS[name] // 4 + 1) + 16 * i)
                        for k in range(KD):
                            last = mm(ps[:, 0, ds(i * (4 * C9) + j * C9, C9)], raw[:, j, k, :], cond[:, k, :],
                                      start=(k == 0), stop=(k == KD - 1))
                        last.then_inc(raw_done[j], 1)
                mm(ps[:, 1, 0:C9], ones[:, :], cond[:, 0, :], start=True, stop=True).then_inc(full[0], 1)

            def norm(n):
                name = f"norm{n}"
                wait_set(name, 0)
                pe.wait_ge(sq_ready, n + 1)
                for h in range(2):
                    last = mm(ps[:, h, 0:HALF], ones[:, :], halves(sqs[:, :])[:, h, :], start=True, stop=True)
                last.then_inc(full[0], 1)

            def dense(name, ready=None):
                units, slabs, per = DENSE[name]
                n0, S = SLABS[name], len(slabs)
                g0 = n0 - SLABS["glu"]
                src = gr if name.startswith("down") else hr
                kfirst = {"glu": 0, "up0": 8, "kv": 16, "q": 24, "wo": 32, "up1": 40}.get(name)
                with pe.Fori(0, units // per) as i:
                    for u in range(per):
                        s = u % 2
                        wait_set(name, s, i * (per // 2) + u // 2)
                        for j, (tile, k0, nk) in enumerate(slabs):
                            n = u * S + j
                            slot, wslot = n % 4, n % 2
                            pe.wait_ge(raw_done[slot], (n0 + n) // 4 + 1 + i * (per * S // 4))
                            for k in range(nk):
                                if u == 0 and name.startswith("down"):
                                    pe.wait_ge(g_ready, FT * int(name[-1]) + k0 + k + 1)
                                elif u == 0 and j == 0:
                                    pe.wait_ge(h_ready, kfirst + k + 1)
                                for w, v in ((0, 0), (0, 1), (1, 0)):
                                    for h in range(2):
                                        first = k0 + k == 0 and (w, v) == (0, 0)
                                        end = j == S - 1 or slabs[j + 1][0] != tile
                                        last = mm(ps[:, 4 * s + 2 * tile + h, 0:HALF], ws[:, wslot, w, k, :],
                                                  src[:, k0 + k, v, h * HALF:(h + 1) * HALF], start=first,
                                                  stop=(end and k == nk - 1 and (w, v) == (1, 0)))
                            last.then_inc(full[s] if j == S - 1 else slab_read, 1)

            ada(0)
            norm(0)

            pe.wait_ge(bbar_ready, 1)
            pe.wait_ge(cpow_ready, 1)
            for u in range(4):
                s = u % 2
                wait_set("ssm_k", s, u // 2)
                for i in range(16):
                    g2, jj = i // 8, i % 8
                    j = u * 8 + jj
                    q = slice(g2 * N, (g2 + 1) * N)
                    for r in range(2):
                        last = mm(ps[0:PP, 4 * s + 2 * g2 + jj // 4, (jj % 4) * P:(jj % 4 + 1) * P], bbar[q, r, j, :],
                                  cpow[q, j, r, 0:CH, :].rearrange("p t q -> p (t q)"), start=(r == 0), stop=(r == 1))
                last.then_inc(full[s], 1)
            ada(1)
            pe.wait_ge(v_ready, 1)
            for u in range(4):
                s = u % 2
                wait_set("ssm_v", s, u // 2)
                for jj in range(8):
                    for r in range(2):
                        i = jj * 2 + r
                        last = turn(ps[:, 4 * s + i // 4, (i % 4) * P:(i % 4 + 1) * P],
                                    vmat[:, r, u * 8 + jj].rearrange("p s q -> p (s q)"))
                last.then_inc(full[s], 1)
            ada(2)
            for s in range(2):
                pe.wait_ge(free[s], USES["ada2"][s])
            pe.wait_ge(u_got, 16 * CH)
            for u in range(4):
                s = u % 2
                wait_set("ssm_w", s, u // 2)
                for jj in range(8):
                    j = u * 8 + jj
                    for r in range(2):
                        for g2 in range(2):
                            at = (jj % 2) * 2 * NCH + r * NCH
                            last = mm(ps[g2 * N:(g2 + 1) * N, 4 * s + jj // 2, at:at + NCH],
                                      vT[:, j, r, g2 * N:(g2 + 1) * N], uch[:, 2 * j + g2, :], start=True, stop=True)
                last.then_inc(full[s], 1)
            ada(3)
            ada(4)
            pe.wait_ge(kmat_got, 16 * CH)
            pe.wait_ge(hs_ready, 1)
            for u in range(4):
                s = u % 2
                wait_set("ssm_y", s, u // 2)
                for i in range(16):
                    g2, jj = i // 8, i % 8
                    j = u * 8 + jj
                    q = slice(g2 * N, (g2 + 1) * N)
                    dst = ps[:, 4 * s + 2 * g2 + jj // 4, (jj % 4) * NCH:(jj % 4 + 1) * NCH]
                    mm(dst, kmat[:, 2 * j + g2, :], uch[:, 2 * j + g2, :], start=True, stop=False)
                    for r in range(2):
                        last = mm(dst, cpow[q, j, r, 1:TAU, :].rearrange("p t q -> p (t q)"), hs[q, 0:NCH, r, j],
                                  start=False, stop=(r == 1))
                last.then_inc(full[s], 1)
            wait_set("ssm_h", 0)
            pe.wait_ge(hfin_ready, 1)
            for r in range(2):
                turn(ps[0:J, r, 0:P], hs[:, NCH, r, :], P)
                for k in range(2):
                    last = turn(ps[:, r, (k + 1) * P:(k + 2) * P], hfin[:, r, 4 * k:4 * k + 4, :].rearrange("p b j -> p (b j)"))
            last.then_inc(full[0], 1)

            dense("glu")
            norm(1)
            dense("up0")
            dense("down0")
            norm(2)
            dense("kv")
            dense("q")

            def heads(name, m, n0):
                with pe.Fori(0, H // 2) as i:
                    for s in range(2):
                        wait_set(name, s, i)
                        pe.wait_ge(sq_head, n0 + s + 1 + 2 * i)
                        for h in range(2):
                            last = mm(ps[:, 4 * s + h, 0:HALF], m[:, :], t1[:, s, h * HALF:(h + 1) * HALF],
                                      start=True, stop=True)
                        last.then_inc(full[s], 1)

            heads("khead", blockd, 0)
            heads("qhead", blockd, 8)
            for n, (name, src) in enumerate((("ktok", kT), ("vtok", vTf))):
                if n == 0:
                    pe.wait_ge(head_ready, 8)
                for i in range(QB + 1):
                    s = i % 2
                    wait_set(name, s, i // 2)
                    for h in range(H):
                        last = turn(ps[0:NTOK[i], 4 * s + h // 4, (h % 4) * P:(h % 4 + 1) * P],
                                    src[:, h, i * P:i * P + NTOK[i]])
                    last.then_inc(full[s], 1)

            with pe.Fori(0, H) as h:
                pe.wait_ge(head_in, h + 1)
                for i in range(QB):
                    w = (i + 1) * P
                    wait_set("attn", 0, h * (QB + 1) + i)
                    for m in range(2):
                        q = slice(m * DK, (m + 1) * DK)
                        last = mm(ps[:, m, 0:w], qh[q, i * P:w], kh[q, 0:w], start=True, stop=True)
                    last.then_inc(full[0], 1)
                    wait_set("attn", 1, h * QB + i)
                    pe.wait_ge(w_done, h * QB + i + 1)
                    for k in range(i + 1):
                        last = turn(ps[:, 4, k * P:(k + 1) * P], e01[:, 0, k * P:(k + 1) * P])
                    last.then_inc(full[1], 1)
                wait_set("attn", 0, h * (QB + 1) + QB)
                wait_set("attn", 1, h * QB + QB)
                for k in range(QB):
                    last = mm(ps[:, 0, k * P:SEQ], vh[:, k, :], wtT[:, k, k * P:SEQ], start=(k == 0), stop=(k == QB - 1))
                last.then_inc(full[0], 1)

            for s in range(2):
                pe.wait_ge(free[s], USES["ohead"][s])
            pe.wait_ge(qbd_ready, 2)

            def page(b, o, u, keys, values):
                at = b * PAGES + o * 8 + u
                slot, half = u % 4, u % 2
                if keys:
                    pe.wait_ge(k_full[slot], 16 * (b * 4 + o * 2 + u // 4 + 1))
                    if not isinstance(at, int) or at > 1:
                        pe.wait_ge(kt_ready, at - 1)
                    for h in range(H):
                        last = turn(ps[:, 2 * half + h // 4, (h % 4) * P:(h % 4 + 1) * P], kpg[:, slot, h, :])
                    last.then_inc(k_turned, 1)
                if values:
                    pe.wait_ge(v_full[slot], 16 * ((b - 1) * 4 + o * 2 + u // 4 + 1))
                    for h in range(H):
                        last = mm(ps[:, 6, h * HQ:(h + 1) * HQ], vpg[:, slot, h, :],
                                  sc[:, ds((b - 1) % 2, 1), ds(o * 8 + u, 1), h * HQ:(h + 1) * HQ].rearrange("p a b c -> p (a b c)"),
                                  start=False, stop=False, skip_group_check=True)
                    last.then_inc(v_used, 1)
                if keys:
                    quad = b * 4 + o * 2 + u // 4
                    if u % 4 == 0 and (not isinstance(quad, int) or quad > 1):
                        pe.wait_ge(s_copied, quad - 1)
                    pe.wait_ge(kt_ready, at + 1)
                    for h in range(H):
                        last = mm(ps[:, 4 + u // 4, (u % 4) * P + h * HQ:(u % 4) * P + (h + 1) * HQ],
                                  kTs[:, half, h // 4, (h % 4) * P:(h % 4 + 1) * P],
                                  qbd[:, h, ds(b, 1)].rearrange("p a m t -> p (a m t)"), start=True, stop=True)
                    last.then_inc(scored, 1)

            def new_scores(b):
                if not isinstance(b, int) or b > 0:
                    pe.wait_ge(l_read, b)
                pe.wait_ge(kn_ready, b + 1)
                for h in range(H):
                    last = mm(ps[0:CH, 7, h * HQ:(h + 1) * HQ], kn[:, h, :], qbd[:, h, ds(b, 1)].rearrange("p a m t -> p (a m t)"),
                              start=True, stop=True)
                last.then_inc(new_scored, 1)

            def softmax(b):
                pe.wait_ge(m_ready, b)
                turn(ps[:, 7, 0:P], mx[:, 0, :]).then_inc(m_turned, 1)
                pe.wait_ge(d_ready, b)
                mm(ps[:, 7, P:2 * P], ones[:, :], mx[:, 1, :], start=True, stop=True).then_inc(m_spread, 1)
                pe.wait_ge(l_ready, b)
                mm(ps[:, 7, 2 * P:3 * P], ones[:, :], mx[:, 2, :], start=True, stop=True).then_inc(l_spread, 1)
                pe.wait_ge(vn_full, 16 * b)
                if not isinstance(b, int) or b > 1:
                    pe.wait_ge(o_ready, b - 1)
                for h in range(H):
                    last = mm(ps[:, 6, h * HQ:(h + 1) * HQ], vn[:, h * DV:(h + 1) * DV],
                              sc[0:CH, ds((b - 1) % 2, 1), PAGES, h * HQ:(h + 1) * HQ].rearrange("p a c -> p (a c)"),
                              start=(h == 0), stop=False, skip_group_check=True)
                last.then_inc(vn_used, 1)

            for u in range(PAGES):
                page(0, u // 8, u % 8, True, False)
            new_scores(0)
            with pe.Fori(1, DB) as b:
                softmax(b)
                with pe.Fori(0, PAGES // 8) as o:
                    for u in range(8):
                        page(b, o, u, True, True)
                new_scores(b)
            softmax(DB)
            for u in range(PAGES):
                page(DB, u // 8, u % 8, False, True)

            pe.wait_ge(o_ready, DB)
            heads("ohead", ones, 16)
            dense("wo")
            norm(3)
            dense("up1")
            dense("down1")
            pe.wait_ge(x_ready, 4 * KD)
            for i in range(QB + 1):
                s = i % 2
                wait_set("y", s, i // 2)
                for k in range(KD):
                    last = turn(ps[0:NTOK[i], 4 * s + k // 4, (k % 4) * P:(k % 4 + 1) * P],
                                x[:, k, i * P:i * P + NTOK[i]])
                last.then_inc(full[s], 1)

        BIAS = [128, 176, 224, 152, 200]
        NORM = [72, 88, 104, 80, 96]
        APPLY = {"s5": (0, 0, None), "up0": (1, 1, 8), "kv": (2, 2, 16), "q": (2, 3, 24), "up1": (3, 4, 40)}
        ORDER = list(APPLY)
        GATE = {"glu": 0, "down0": 1, "wo": 3, "down1": 4}
        XUP = {"glu": 0, "down0": 8, "wo": 16, "down1": 24}

        def cols(n, part, k, lo, hi):
            return mod[:, n, ds(part * KD + k, 1), lo:hi].rearrange("p a c -> p (a c)")

        def by_token(v):
            return v.unsqueeze(2).to_broadcast([P, DB, DS])

        def sample(t):
            return t[:, SEQ:T].rearrange("p (b t) -> p b t", b=DB)

        def tile(t, k):
            return t[:, ds(k, 1), :].rearrange("p a t -> p (a t)")

        def part(t, k, v):
            return t[:, ds(k, 1), v, :].rearrange("p a t -> p (a t)")

        def chunks_prompt(t):
            return t.rearrange("p (s c) -> p c s", s=CH)[:, DB:NCH, :]

        def chunks_sample(t):
            return t.rearrange("p (s c) -> p c s", s=CH)[:, 0:DB, :]

        def by_halves(t, k):
            return t[:, ds(k, 1), :].rearrange("p k (a b) -> p (k a) b", a=2)

        @block.scalar
        def _(act):
            A = nc.scalar.activation
            step = Steps(act, act_step)

            for r, name in enumerate(("ssm_c_re", "ssm_c_im")):
                for g in range(2):
                    for k in range(4):
                        act.dma_start(craw[:, r, k, g * N:(g + 1) * N],
                                      a[name][0, 16 * k:16 * k + 16].rearrange("(j g) p n -> g j p n", g=2)[g]
                                      ).then_inc(in_b, 16)
            for r, name in enumerate(("ssm_b_re", "ssm_b_im")):
                act.dma_start(bmat[:, r], a[name][0].rearrange("(j g) n p -> (g n) j p", g=2)).then_inc(in_b, 16)
            for i in range(2, QB + 1):
                wait_unit(act, "x", i % 2, i // 2 - 1)
                act.dma_start(xtok[0:NTOK[i], i % 2, :], dtok[i]).then_inc(in_x[i % 2], 16)
            wait_unit(act, "small", 0)
            act.wait_ge(dt_ready, 1)
            A(cond[:, :, :].rearrange("p k c -> p c k"), vec[:, 0:C9 * KD].rearrange("p (c k) -> p c k", c=C9), ACT.Silu
              ).then_inc(cond_ready, 1)
            A(tiny[:, 0], vec[:, 320:352], ACT.Exp).then_inc(sincos_out, 1)
            act.wait_ge(dt_ready, 2)
            A(neglam[:, :], lsum[:, 0:1], ACT.Exp)
            A(lsum[:, 2:3], lsum[:, 1:2], ACT.Exp).then_inc(sincos_out, 1)
            act.wait_ge(sincos_in, 1)
            A(tiny[:, 6], tiny[:, 1], ACT.Exp)
            A(tiny[:, 7], tiny[:, 4], ACT.Sin)
            A(tiny[:, 8], tiny[:, 5], ACT.Sin).then_inc(sincos_out, 1)

            def ada_out(n):
                c = COUNT[f"ada{n}"] * C9
                wait_unit(act, f"ada{n}", 0)
                A(mod[:, n].rearrange("p m c -> p (m c)")[:, 0:c], ps[:, 0, 0:c], ACT.Copy).then_inc(free[0], 1)

            def root(n):
                wait_unit(act, f"norm{n}", 0)
                A(halves(rstd[:, :]), ps[:, 0:2, 0:HALF], ACT.Sqrt, bias=eps[:, 0:1], scale=1.0 / D).then_inc(free[0], 1)

            def apply(name):
                _, m, h0_ = APPLY[name]
                b0 = KD * ORDER.index(name)
                act.wait_ge(mod_ready, m + 1)
                with act.Fori(0, KD // 2) as i:
                    for s in range(2):
                        k = i * 2 + s
                        act.wait_ge(t1_ready, b0 + s + 1 + i * 2)
                        A(t2[:, s, 0:SEQ], t1[:, s, 0:SEQ], ACT.Identity, bias=cols(m, 0, k, 0, 1),
                          scale=gain[:, m, ds(k, 1), 0:1].rearrange("p a c -> p (a c)")).then_inc(t2_prompt, 1)
                        act.wait_ge(t2_prompt, b0 + s + 1 + i * 2)
                        act.wait_ge(t2_sample, b0 + s + 1 + i * 2)
                        A(part(hr, k, 0), t2[:, s, :], ACT.Copy).then_inc(h_high, 1)

            ada_out(0)
            root(0)
            act.wait_ge(mod_ready, 1)
            for k in range(KD):
                s = k % 2
                act.wait_ge(t1_ready, k + 1)
                if k >= 2:
                    act.wait_ge(u_put[s], 16 * (k // 2))
                A(chunks_prompt(t2[:, s, :]), t1[:, s, 0:SEQ].rearrange("p (c s) -> p c s", s=CH), ACT.Identity,
                  bias=mod[:, 0, k, 0:1], scale=gain[:, 0, k, 0:1]).then_inc(t2_prompt, 1)
                act.wait_ge(t2_prompt, k + 1)
                act.wait_ge(t2_sample, k + 1)
                act.dma_start(u_scr[k * P:(k + 1) * P].rearrange("f s c -> f (s c)"), t2[:, s, :]).then_inc(u_put[s], 16)
            for s in range(2):
                act.wait_ge(u_put[s], 16 * (KD // 2))
            for s in range(CH):
                act.dma_start(uch[s * PP:(s + 1) * PP, :, :], u_scr.rearrange("(g p) s c -> s p g c", p=PP)[s]
                              ).then_inc(u_got, 16)
            for u in range(4):
                s = u % 2
                wait_unit(act, "ssm_k", s, u // 2)
                if u >= 2:
                    act.wait_ge(k_put[s], 16)
                for g in range(2):
                    done = A(krow[:, s, g:16:2, :],
                             ps[0:PP, 4 * s + 2 * g:4 * s + 2 * g + 2, :].rearrange("p b (j m) -> p (b j) m", m=P), ACT.Copy)
                done.then_inc(free[s], 1)
                act.wait_ge(free[s], uses("ssm_k", s, u // 2) + 1)
                act.dma_start(k_scr[:, 16 * u:16 * u + 16, :], krow[:, s, :, :]).then_inc(k_put[s], 16)
            ada_out(1)
            for s in range(2):
                act.wait_ge(k_put[s], 16 * 2)
            for u in range(4):
                s = u % 2
                wait_unit(act, "ssm_v", s, u // 2)
                A(vT[:, 8 * u:8 * u + 8].rearrange("p j r m -> p (j r m)"),
                  ps[:, 4 * s:4 * s + 4, :].rearrange("p b c -> p (b c)"), ACT.Copy).then_inc(free[s], 1)
            ada_out(2)
            for u in range(4):
                s = u % 2
                wait_unit(act, "ssm_w", s, u // 2)
                for r in range(2):
                    done = A(drive[:, :, r, 8 * u:8 * u + 8].rearrange("p c (b j) -> p b j c", j=2),
                             ps[:, 4 * s:4 * s + 4, 0:4 * NCH].rearrange("p b (j r c) -> p r b j c", j=2, r=2)[:, r], ACT.Copy)
                done.then_inc(free[s], 1)
            act.wait_ge(kmat_zero, 1)
            for s in range(CH):
                act.dma_start(kmat[s * PP:(s + 1) * PP, :, s * PP:P], k_scr[:, :, 0:P - s * PP]).then_inc(kmat_got, 16)
            ada_out(3)
            ada_out(4)
            for u in range(4):
                s = u % 2
                act.wait_ge(free[s], uses("ssm_y", s, u // 2) + 1)
                for t in range(CH):
                    act.dma_start(y_scr.rearrange("(g p) t c -> t p g c", p=PP)[t, :, 16 * u:16 * u + 16, :],
                                  ysb[t * PP:(t + 1) * PP, s, :].rearrange("p (g c) -> p g c", c=NCH)).then_inc(y_put[s], 16)
            wait_unit(act, "ssm_h", 0)
            for r in range(2):
                A(hout[0:J, 3 * r, :], ps[0:J, r, 0:P], ACT.Copy)
                done = A(hout[:, 3 * r + 1:3 * r + 3, :].rearrange("p k m -> p (k m)"), ps[:, r, P:3 * P], ACT.Copy)
            done.then_inc(free[0], 1)
            act.wait_ge(free[0], uses("ssm_h", 0) + 1)
            for r in range(2):
                act.dma_start(out[2 + r][0, 0].rearrange("(j g) n -> j (g n)", g=2), hout[0:J, 3 * r, :]).then_inc(put, 16)
                for k in range(2):
                    act.dma_start(out[4 + r][0, 4 * k:4 * k + 4].rearrange("b (j g) n -> (b j) (g n)", g=2),
                                  hout[:, 3 * r + 1 + k, :]).then_inc(put, 16)
            for s in range(2):
                act.wait_ge(y_put[s], 16 * 2 * CH)

            def split(m, late=0, nk=8):
                slot, w = m % 4, m % 2
                act.wait_ge(raw_full[slot], 16 * ((DENSE0 + m) // 4 + 1) + late * 4)
                A(ws[:, w, 0, 0:nk, :].rearrange("p k n -> p (k n)"), raw[:, slot, 0:nk, :].rearrange("p k n -> p (k n)"),
                  ACT.Copy).then_inc(slab_high, 1)

            def yu_load(k):
                s = k % 2
                act.dma_start(yin[:, s].rearrange("p s c -> p (s c)"), y_scr[k * P:(k + 1) * P].rearrange("f s c -> f (s c)")
                              ).then_inc(y_got[s], 16)
                act.dma_start(uin[:, s].rearrange("p s c -> p (s c)"), u_scr[k * P:(k + 1) * P].rearrange("f s c -> f (s c)")
                              ).then_inc(y_got[s], 16)

            yu_load(0)
            yu_load(1)
            split(0)
            split(1)
            for k in range(KD):
                s = k % 2
                act.wait_ge(yu_ready, k + 1)
                if k >= 2:
                    act.wait_ge(h_ready, k - 1)
                if k + 2 < KD:
                    yu_load(k + 2)
                A(t2[:, s, 0:SEQ].rearrange("p (c s) -> p c s", s=CH), chunks_prompt(t1[:, s, :]), ACT.Gelu_apprx_tanh)
                step(A(t2[:, s, SEQ:T].rearrange("p (c s) -> p c s", s=CH), chunks_sample(t1[:, s, :]), ACT.Gelu_apprx_tanh))
                A(hr[:, k, 0, :], t2[:, s, :], ACT.Copy).then_inc(h_high, 1)

            def dense(name, tail=True):
                units, slabs, per = DENSE[name]
                S, n0 = len(slabs), SLABS[name] - DENSE0

                def turn(i, last):
                    for u in range(per):
                        s = u % 2
                        for j in range(S):
                            n = u * S + j
                            if j == S - 1:
                                wait_unit(act, name, s, i * (per // 2) + u // 2)
                            else:
                                act.wait_ge(slab_read, INNER[name] + u * (S - 1) + j + 1 + i * (per * (S - 1)))
                            if not (last and n + 2 >= per * S):
                                split(n0 + n + 2, i * (per * S), slabs[(j + 2) % S][2] if S == 4 and j < 2 else 8)
                        at = i * (per // 2) + u // 2
                        if name == "glu":
                            A(halves(t1[:, s, :]), ps[:, 4 * s + 2:4 * s + 4, 0:HALF], ACT.Sigmoid).then_inc(e_ready, 1)
                        elif name.startswith("up"):
                            f = i * 2 + u
                            A(halves(t1[:, s, :]), ps[:, 4 * s:4 * s + 2, 0:HALF], ACT.Silu).then_inc(e_ready, 1)
                            act.wait_ge(free[s], uses(name, s, at) + 1)
                            A(part(gr, f, 0), t2[:, s, :], ACT.Copy).then_inc(g_high, 1)
                        elif name in ("kv", "q"):
                            A(by_halves(kvT if name == "kv" else qT, i * per + u), ps[:, 4 * s:4 * s + 2, 0:HALF], ACT.Copy).then_inc(free[s], 1)

                if tail:
                    with act.Fori(0, units // per) as i:
                        turn(i, False)
                else:
                    with act.Fori(0, units // per - 1) as i:
                        turn(i, False)
                    turn(units // per - 1, True)

            dense("glu")
            root(1)
            apply("up0")
            dense("up0")
            dense("down0")
            root(2)
            apply("kv")
            dense("kv")
            apply("q")
            dense("q", tail=False)

            def heads(name, src, n0):
                with act.Fori(0, H // 2) as i:
                    for s in range(2):
                        A(t1[:, s, :], tile(src, i * 2 + s), ACT.Square).then_inc(sq_head, 1)
                    for s in range(2):
                        wait_unit(act, name, s, i)
                        act.wait_ge(head_ready, n0 + i * 2)
                        A(halves(t2[:, s, :]), ps[:, 4 * s:4 * s + 2, 0:HALF], ACT.Sqrt, bias=eps[:, 0:1],
                          scale=1.0 / (DV if name == "ohead" else DK)).then_inc(free[s], 1)

            for s in range(2):
                act.wait_ge(free[s], USES["khead"][s])
            heads("khead", kT, 0)
            heads("qhead", qT, 8)
            for n, name in enumerate(("ktok", "vtok")):
                for i in range(QB + 1):
                    s = i % 2
                    wait_unit(act, name, s, i // 2)
                    if name == "vtok" and i < QB:
                        dst = vtok[:, i].rearrange("p h d -> p (h d)")
                    else:
                        dst = tok[0:NTOK[i], s, :]
                        if n or i >= 2:
                            act.wait_ge(tok_put[s], 16 * (i // 2 if not n else 3 + 2))
                    A(dst, ps[0:NTOK[i], 4 * s:4 * s + 2, :].rearrange("p b c -> p (b c)"), ACT.Copy).then_inc(free[s], 1)
                    act.wait_ge(free[s], uses(name, s, i // 2) + 1)
                    o_ = out[6 + n] if i < QB else out[8 + n]
                    rows_ = (o_[0, i * P:(i + 1) * P] if i < QB else o_)
                    form = {(0, 0): "t h m d -> t (h m d)", (0, 1): "t h d -> t (h d)", (1, 0): "b t h m d -> (b t) (h m d)",
                            (1, 1): "b t h d -> (b t) (h d)"}[(int(i == QB), n)]
                    act.dma_start(rows_.rearrange(form), dst).then_inc(tok_put[s], 16)

            with act.Fori(0, H) as h:
                for i in range(QB):
                    w = (i + 1) * P
                    act.wait_ge(s_max, h * QB + i + 1)
                    for m in range(2):
                        done = A(e01[:, m, 0:w], ps[:, m, 0:w], ACT.Exp, bias=l01[:, 2 + m:3 + m], scale=SCALE,
                                 accum_out=l01[:, 4 + m:5 + m])
                    done.then_inc(free[0], 1)
                wait_unit(act, "attn", 0, h * (QB + 1) + QB)
                A(oT[:, ds(h, 1), 0:SEQ].rearrange("p a t -> p (a t)"), ps[:, 0, :], ACT.Copy).then_inc(free[0], 1)

            def page(b, o, u):
                at, half = b * PAGES + o * 8 + u, u % 2
                act.wait_ge(k_turned, at + 1)
                if not isinstance(at, int) or at > 1:
                    act.wait_ge(scored, at - 1)
                A(kTs[:, half], ps[:, 2 * half:2 * half + 2, :], ACT.Copy).then_inc(kt_ready, 1)

            def weights(b):
                act.wait_ge(s_low, b)
                buf = sc[:, ds((b - 1) % 2, 1)].rearrange("p a k c -> p (a k) c")
                A(buf[:, 0:PAGES].rearrange("p k c -> p (k c)"), buf[:, 0:PAGES].rearrange("p k c -> p (k c)"), ACT.Exp, scale=SCALE)
                A(buf[0:CH, PAGES], buf[0:CH, PAGES], ACT.Exp, scale=SCALE).then_inc(e_full, 1)

            for u in range(PAGES):
                page(0, u // 8, u % 8)
            with act.Fori(1, DB) as b:
                weights(b)
                with act.Fori(0, PAGES // 8) as o:
                    for u in range(8):
                        page(b, o, u)
            weights(DB)

            act.wait_ge(o_ready, DB)
            heads("ohead", oT, 16)
            split(SLABS["wo"] - DENSE0)
            split(SLABS["wo"] - DENSE0 + 1)
            act.wait_ge(head_ready, 3 * H)
            with act.Fori(0, H) as i:
                A(part(hr, i, 0), tile(oT, i), ACT.Copy).then_inc(h_high, 1)
            dense("wo")
            root(3)
            apply("up1")
            dense("up1")
            dense("down1", tail=False)
            for i in range(QB + 1):
                s = i % 2
                wait_unit(act, "y", s, i // 2)
                if i >= 2:
                    act.wait_ge(tok_put[s], 16 * ((6, 4)[s] + i // 2))
                A(tok[0:NTOK[i], s, :], ps[0:NTOK[i], 4 * s:4 * s + 2, :].rearrange("p b c -> p (b c)"), ACT.Copy
                  ).then_inc(free[s], 1)
                act.wait_ge(free[s], uses("y", s, i // 2) + 1)
                act.dma_start(out[0][0, i * P:(i + 1) * P] if i < QB else out[1].rearrange("b t d -> (b t) d"),
                              tok[0:NTOK[i], s, :]).then_inc(tok_put[s], 16)

        @block.gpsimd
        def _(pool):
            TT = nc.gpsimd.tensor_tensor
            step = Steps(pool, pool_step)

            nc.gpsimd.memset(ones[:, :], 1.0).then_inc(consts, 1)
            step(nc.gpsimd.memset(ident[:, :], 0.0))
            nc.gpsimd.affine_select(out=ident[:, :], in_=ident[:, :], compare_op=ALU.not_equal, fill=1.0, base=0,
                                    pattern=[[-1, P]], channel_multiplier=1).then_inc(consts, 1)
            nc.gpsimd.memset(eps[:, :], EPS)
            step(nc.gpsimd.memset(blockd[:, :], 0.0))
            for m in range(2):
                nc.gpsimd.memset(blockd[m * DK:(m + 1) * DK, m * DK:(m + 1) * DK], 1.0)
            step(nc.gpsimd.memset(causal[:, :], 0.0))
            nc.gpsimd.affine_select(out=causal[:, :], in_=causal[:, :], compare_op=ALU.is_ge, fill=MASKED, base=0,
                                    pattern=[[1, CH]], channel_multiplier=-1).then_inc(consts, 1)

            def squares(n):
                if n == 0:
                    for s in range(2):
                        pool.wait_ge(free[s], USES["ada0"][s])
                else:
                    pool.wait_ge(x_ready, KD * (n - 1) + 1)
                for h in range(2):
                    q = slice(h * HALF, (h + 1) * HALF)
                    done = TT(sqs[:, q], x[:, 0, q], x[:, 0, q], ALU.mult)
                step(done)
                with step.loop(1, KD - 1, 4) as k:
                    if n:
                        pool.wait_ge(x_ready, KD * (n - 1) + 1 + k)
                    for h in range(2):
                        q = slice(h * HALF, (h + 1) * HALF)
                        step(TT(sqt[:, :], tile(x, k)[:, q], tile(x, k)[:, q], ALU.mult))
                        step(TT(sqs[:, q], sqs[:, q], sqt[:, :], ALU.add))
                nc.gpsimd.memset(mark[:, n:n + 1], 0.0).then_inc(sq_ready, 1)

            def cmul_pool(o_re, o_im, a_re, a_im, b_re, b_im, u, v):
                TT(u, a_re, b_re, ALU.mult)
                step(TT(v, a_im, b_im, ALU.mult))
                step(TT(o_re, u, v, ALU.subtract))
                TT(u, a_re, b_im, ALU.mult)
                step(TT(v, a_im, b_re, ALU.mult))
                step(TT(o_im, u, v, ALU.add))

            squares(0)
            pool.wait_ge(bbar_ready, 1)
            u_, v_ = (t[:, :].rearrange("p (j q) -> p j q", q=PP) for t in (pA, pB))
            for s in range(CH):
                p_ = [pw[:, CH - 1 - s, r].unsqueeze(2).to_broadcast([P, J, PP]) for r in range(2)]
                cmul_pool(vmat[:, 0, :, s, :], vmat[:, 1, :, s, :], p_[0], p_[1], bbar[:, 0], bbar[:, 1], u_, v_)
            nc.gpsimd.memset(mark[:, 4:5], 0.0).then_inc(v_ready, 1)

            def modulation(n):
                pool.wait_ge(free[0], USES[f"ada{n}"][0] + 1)
                c = COUNT[f"ada{n}"]
                step(TT(mod[:, n, 0:c], mod[:, n, 0:c], vec[:, BIAS[n]:BIAS[n] + c].unsqueeze(2).to_broadcast([P, c, C9]), ALU.add))
                g = vec[:, NORM[n]:NORM[n] + KD].unsqueeze(2).to_broadcast([P, KD, C9])
                step(TT(gain[:, n], mod[:, n, KD:2 * KD], g, ALU.mult))
                TT(gain[:, n], gain[:, n], g, ALU.add).then_inc(mod_ready, 1)
                pool.wait_ge(mod_ready, n + 1)

            def sample_part(s, m, k, b0, at, dst):
                pool.wait_ge(t1_ready, at)
                g = by_token(gain[:, m, ds(k, 1), 1:C9].rearrange("p a c -> p (a c)"))
                sh = by_token(cols(m, 0, k, 1, C9))
                step(TT(sample(t1[:, s, :]), sample(t1[:, s, :]), g, ALU.mult))
                TT(dst, sample(t1[:, s, :]), sh, ALU.add).then_inc(t2_sample, 1)

            def apply(name):
                _, m, _h = APPLY[name]
                b0 = KD * ORDER.index(name)
                with step.loop(0, KD // 2, 2) as i:
                    for s in range(2):
                        sample_part(s, m, i * 2 + s, b0, b0 + s + 1 + i * 2, sample(t2[:, s, :]))

            modulation(0)
            for k in range(KD):
                if k >= 2:
                    pool.wait_ge(u_put[k % 2], 16 * (k // 2))
                sample_part(k % 2, 0, k, 0, k + 1, chunks_sample(t2[:, k % 2, :]))
            modulation(1)
            modulation(2)
            for s in range(2):
                wait_unit(pool, "ssm_w", s, 1)
            nc.gpsimd.memset(vk[:, :], 0.0).then_inc(kmat_zero, 1)
            modulation(3)
            modulation(4)
            squares(1)
            apply("up0")
            squares(2)
            apply("kv")
            pool.wait_ge(h_ready, 3 * KD)
            nc.gpsimd.memset(qbd[:, :].rearrange("p h b m t -> p (h b m t)"), 0.0).then_inc(qbd_ready, 1)
            apply("q")
            pool.wait_ge(head_ready, 2 * H)
            step(nc.gpsimd.memset(tri[:, :], 0.0))
            step(nc.gpsimd.affine_select(out=tri[:, :], in_=tri[:, :], compare_op=ALU.is_ge, fill=MASKED, base=0,
                                         pattern=[[-1, P]], channel_multiplier=1))
            for s in range(2):
                pool.wait_ge(free[s], USES["attn"][s])
            with pool.Fori(0, H) as h:
                pool.wait_ge(free[0], USES["attn"][0] + h * (QB + 1))
                nc.gpsimd.tensor_copy(qh[:, :], tile(qT, h)[:, 0:SEQ])
                nc.gpsimd.tensor_copy(kh[:, :], tile(kT, h)[:, 0:SEQ])
                nc.gpsimd.tensor_copy(vh[:, :, :], vtok[:, :, ds(h, 1), :].rearrange("p k a d -> p k (a d)")).then_inc(head_in, 1)
            for s in range(2):
                pool.wait_ge(free[s], USES["ohead"][s])
                pool.wait_ge(tok_put[s], 16 * (6, 4)[s])
            nc.gpsimd.memset(mark[:, 9:10], 0.0).then_inc(v_used, 4)
            nc.gpsimd.memset(sc[:, :, PAGES, :], MASKED).then_inc(sinit, 1)

            def new_rows(b):
                if not isinstance(b, int) or b > 0:
                    pool.wait_ge(new_scored, b)
                    pool.wait_ge(vn_used, b)
                nc.gpsimd.tensor_copy(kn[:, :, :], kT[:, :, ds(SEQ + b * CH, CH)]).then_inc(kn_ready, 1)
                pool.dma_start(vn[:, :], out[9][ds(b, 1)].rearrange("b t h d -> t (b h d)")).then_inc(vn_full, 16)

            new_rows(0)
            with pool.Fori(1, DB) as b:
                new_rows(b)
            squares(3)
            apply("up1")

        @block.vector
        def _(dve):
            TT, TS, STT = nc.vector.tensor_tensor, nc.vector.tensor_scalar, nc.vector.scalar_tensor_tensor
            CP, RED, REC = nc.vector.tensor_copy, nc.vector.tensor_reduce, nc.vector.reciprocal
            step = Steps(dve, dve_step)

            dve.wait_ge(in_small, 16 * SMALL)
            CP(v3[64:96, :].rearrange("p (g n) -> p g n", g=2), lst[64:96, :].unsqueeze(2).to_broadcast([32, 2, N])
               ).then_inc(v3_built, 1)
            for k in range(2):
                step(TT(ltmp[:, k, :], lrow[:, 2 * k, :], lrow[:, 2 * k + 1, :], ALU.mult))
            RED(lsum[:, 0:2], ltmp[:, :, :], AX_X, ALU.add)
            wait_unit(dve, "small", 0)
            CP(vec[:, 0:123], ps[:, 0, 0:123])
            CP(vec[:, P:P + 112], ps[:, 0, P:P + 112])
            CP(vec[:, 2 * P:2 * P + 96], ps[:, 0, 2 * P:2 * P + 96]).then_inc(dt_ready, 1)
            CP(h0[:, :, :].rearrange("p r b -> p (r b)"), ps[:, 1, :]).then_inc(dt_ready, 1)
            CP(cT[:, :, :, :].rearrange("p r j q -> p r (j q)"), ps[:, 2:4, :]).then_inc(free[0], 1)
            for i in range(QB + 1):
                s = i % 2
                wait_unit(dve, "x", s, i // 2)
                CP(x[:, :, i * P:i * P + NTOK[i]].rearrange("p (b k) t -> p b k t", b=2),
                   ps[:, 4 * s:4 * s + 2, :].rearrange("p b (k t) -> p b k t", t=P)[:, :, :, 0:NTOK[i]]).then_inc(free[s], 1)

            lr, li = vec[:, 256:288], vec[:, 288:320]
            T_ = lambda n: tiny[:, n, :]
            dve.wait_ge(sincos_out, 1)
            TT(T_(1), lr, T_(0), ALU.mult)
            step(TT(T_(2), li, T_(0), ALU.mult))
            step(TS(T_(3), T_(2), 1 / (2 * math.pi), ROUND, ALU.mult, ALU.add))
            step(TS(T_(3), T_(3), -ROUND, None, ALU.add))
            step(STT(T_(4), T_(3), -TWO_PI_PARTS[0], T_(2), ALU.mult, ALU.add))
            step(STT(T_(4), T_(3), -TWO_PI_PARTS[1], T_(4), ALU.mult, ALU.add))
            step(STT(T_(4), T_(3), -TWO_PI_PARTS[2], T_(4), ALU.mult, ALU.add))
            step(TS(T_(4), T_(4), PI_BELOW, -PI_BELOW, ALU.min, ALU.max))
            step(STT(T_(5), T_(4), -1.0, T_(4), ALU.mult, ALU.max))
            TS(T_(5), T_(5), -1.0, math.pi / 2, ALU.mult, ALU.add).then_inc(sincos_in, 1)
            dve.wait_ge(sincos_out, 2)
            step(TT(neglam[:, :], lsum[:, 2:3], neglam[:, :], ALU.subtract))
            step(TS(neglam[:, :], neglam[:, :], -LAM_INIT, None, ALU.add))
            TS(gaino[:, :], vec[:, 122:123], 1.0 - LAM_INIT, None, ALU.mult)
            dve.wait_ge(sincos_out, 3)
            nc.vector.memset(pw[:, 0, 0, :], 1.0)
            nc.vector.memset(pw[:, 0, 1, :], 0.0)
            TT(pw[:, 1, 0, :], T_(6), T_(8), ALU.mult)
            step(TT(pw[:, 1, 1, :], T_(6), T_(7), ALU.mult))

            def cmul(o_re, o_im, a_re, a_im, b_re, b_im, u, v):
                TT(u, a_re, b_re, ALU.mult)
                step(TT(v, a_im, b_im, ALU.mult))
                step(TT(o_re, u, v, ALU.subtract))
                TT(u, a_re, b_im, ALU.mult)
                step(TT(v, a_im, b_re, ALU.mult))
                step(TT(o_im, u, v, ALU.add))

            for k in (1, 2, 4):
                u, v = (t[:, 0:k * J].rearrange("p (k j) -> p k j", j=J) for t in (tA, tB))
                a_ = [pw[:, k, r].unsqueeze(1).to_broadcast([P, k, J]) for r in range(2)]
                cmul(pw[:, k + 1:2 * k + 1, 0], pw[:, k + 1:2 * k + 1, 1], a_[0], a_[1], pw[:, 1:k + 1, 0], pw[:, 1:k + 1, 1], u, v)
            TS(pws[:, 1], pw[:, CH, 1], -1.0, None, ALU.mult)
            step(CP(pws[:, 0], pw[:, CH, 1]))
            ni = pw[:, 1, 1, :]
            TS(T_(9), pw[:, 1, 0, :], -1.0, None, ALU.add)
            TT(T_(10), lr, lr, ALU.mult)
            step(TT(T_(11), li, li, ALU.mult))
            step(TT(T_(10), T_(10), T_(11), ALU.add))
            step(REC(T_(10), T_(10)))
            TT(T_(11), T_(9), lr, ALU.mult)
            step(TT(T_(12), ni, li, ALU.mult))
            step(TT(T_(11), T_(11), T_(12), ALU.add))
            step(TT(T_(11), T_(11), T_(10), ALU.mult))
            TT(T_(12), ni, lr, ALU.mult)
            step(TT(T_(13), T_(9), li, ALU.mult))
            step(TT(T_(12), T_(12), T_(13), ALU.subtract))
            step(TT(T_(12), T_(12), T_(10), ALU.mult))
            dve.wait_ge(in_b, 16 * 18)
            u, v = (t[:, :].rearrange("p (j q) -> p j q", q=PP) for t in (tA, tB))
            f = [T_(11 + r).unsqueeze(2).to_broadcast([P, J, PP]) for r in range(2)]
            cmul(bbar[:, 0], bbar[:, 1], f[0], f[1], bmat[:, 0], bmat[:, 1], u, v)
            nc.vector.memset(mark[:, 5:6], 0.0).then_inc(bbar_ready, 1)
            with step.loop(0, TAU, 4) as t:
                p_ = [pw[:, ds(t, 1), r].rearrange("p a j -> p (a j)").unsqueeze(2).to_broadcast([P, J, PP]) for r in range(2)]
                o_ = [cpow[:, :, r, ds(t, 1), :].rearrange("p j a q -> p j (a q)") for r in range(2)]
                TT(u, p_[0], cT[:, 0], ALU.mult)
                step(TT(v, p_[1], cT[:, 1], ALU.mult))
                step(TT(o_[0], u, v, ALU.subtract))
                TT(u, p_[0], cT[:, 1], ALU.mult)
                step(TT(v, p_[1], cT[:, 0], ALU.mult))
                step(STT(o_[1], u, -1.0, v, ALU.mult, ALU.subtract))
            nc.vector.memset(mark[:, 6:7], 0.0).then_inc(cpow_ready, 1)

            def root(n):
                dve.wait_ge(free[0], USES[f"norm{n}"][0] + 1)
                step(REC(rstd[:, :], rstd[:, :]))

            root(0)
            for k in range(KD):
                if k >= 2:
                    dve.wait_ge(t2_prompt, k - 1)
                    dve.wait_ge(t2_sample, k - 1)
                TT(t1[:, k % 2, :], x[:, k, :], rstd[:, :], ALU.mult).then_inc(t1_ready, 1)
            for s in range(2):
                dve.wait_ge(free[s], USES["ada2"][s])
            for r in range(2):
                CP(hs[:, 0:DB, r, :], h0[:, r, :].rearrange("p (b j) -> p b j", b=DB))
            step(nc.vector.memset(hs[:, DB], 0.0))
            for s in range(2):
                dve.wait_ge(free[s], USES["ada3"][s])
            u, v = (t[:, 0:2 * J].rearrange("p (r j) -> p r j", r=2) for t in (tA, tB))
            a8 = pw[:, CH, 0, :].unsqueeze(1).to_broadcast([P, 2, J])
            UN = 4
            with step.loop(0, PCH // UN, 3 * UN) as i:
                for k in range(UN):
                    c = DB + k + i * UN
                    h_ = hs[:, ds(c, 1)].rearrange("p a r j -> p (a r) j")
                    TT(u, h_, a8, ALU.mult)
                    step(TT(v[:, ::-1, :], h_, pws[:, :, :], ALU.mult))
                    step(TT(u, u, v, ALU.add))
                    step(TT(hs[:, ds(c + 1, 1)].rearrange("p a r j -> p (a r) j"), u,
                            drive[:, ds(c, 1)].rearrange("p a r j -> p (a r) j"), ALU.add))
            nc.vector.memset(mark[:, 7:8], 0.0).then_inc(hs_ready, 1)
            u, v = (t[:, :].rearrange("p (b r j) -> p b r j", b=DB, r=2) for t in (tA, tB))
            step(TT(u, hs[:, 0:DB], pw[:, CH, 0, :].unsqueeze(1).unsqueeze(1).to_broadcast([P, DB, 2, J]), ALU.mult))
            step(TT(v[:, :, ::-1, :], hs[:, 0:DB], pws[:, :, :].unsqueeze(1).to_broadcast([P, DB, 2, J]), ALU.mult))
            step(TT(u, u, v, ALU.add))
            TT(hfin[:, :].rearrange("p r b j -> p b r j"), u, drive[:, 0:DB], ALU.add).then_inc(hfin_ready, 1)
            for n in range(4):
                s = n % 2
                wait_unit(dve, "ssm_y", s, n // 2)
                if n >= 2:
                    dve.wait_ge(y_put[s], 16 * CH)
                for g in range(2):
                    done = CP(ysb[:, s, :].rearrange("p (j g c) -> p g j c", g=2, c=NCH)[:, g].rearrange("p (b j) c -> p b j c", b=2),
                              ps[:, 4 * s + 2 * g:4 * s + 2 * g + 2, 0:4 * NCH].rearrange("p b (j c) -> p b j c", c=NCH))
                done.then_inc(free[s], 1)

            def split(m, late=0, nk=8):
                slot, w = m % 4, m % 2
                dve.wait_ge(slab_high, m + 1 + late)
                f = lambda t: t.rearrange("p k n -> p (k n)")
                TT(f(ws[:, w, 1, 0:nk, :]), f(raw[:, slot, 0:nk, :]), f(ws[:, w, 0, 0:nk, :]).bitcast(F32), ALU.subtract
                   ).then_inc(raw_done[slot], 1)

            def low(k, s, n):
                dve.wait_ge(h_high, n)
                TT(part(hr, k, 1), t2[:, s, :], part(hr, k, 0).bitcast(F32), ALU.subtract).then_inc(h_ready, 1)

            split(0)
            split(1)
            for k in range(KD + 1):
                if k < KD:
                    s = k % 2
                    dve.wait_ge(y_got[s], 32 * (k // 2 + 1))
                    f = lambda t: t[:, s].rearrange("p s c -> p (s c)")
                    if k >= 2:
                        dve.wait_ge(h_high, k - 1)
                    STT(t1[:, s, :], f(uin), vec[:, 112 + k:113 + k], f(yin), ALU.mult, ALU.add).then_inc(yu_ready, 1)
                if k:
                    low(k - 1, (k - 1) % 2, k)

            def apply(name):
                _, m, hb = APPLY[name]
                with dve.Fori(0, KD // 2) as i:
                    for s in range(2):
                        TT(t1[:, s, :], tile(x, i * 2 + s), rstd[:, :], ALU.mult).then_inc(t1_ready, 1)
                    for s in range(2):
                        low(i * 2 + s, s, hb + s + 1 + i * 2)

            def dense(name, tail=True):
                units, slabs, per = DENSE[name]
                S, n0 = len(slabs), SLABS[name] - DENSE0
                steps_ = per * {"glu": 1}.get(name, 0)

                def turn(i, last):
                    for u in range(per):
                        s = u % 2
                        at = i * (per // 2) + u // 2
                        k = i * per + u
                        for j in range(S):
                            n = u * S + j
                            if not (last and n + 2 >= per * S):
                                split(n0 + n + 2, i * (per * S), slabs[(j + 2) % S][2] if S == 4 and j < 2 else 8)
                        if name in ("kv", "q"):
                            continue
                        wait_unit(dve, name, s, at)
                        if name.startswith("up"):
                            at_e = (KD if name == "up0" else KD + FT) + k + 1
                            dve.wait_ge(e_ready, at_e)
                            TT(halves(t2[:, s, :]), ps[:, 4 * s + 2:4 * s + 4, 0:HALF], halves(t1[:, s, :]), ALU.mult
                               ).then_inc(free[s], 1)
                            dve.wait_ge(free[s], uses(name, s, at) + 1)
                            dve.wait_ge(g_high, (0 if name == "up0" else FT) + k + 1)
                            TT(part(gr, k, 1), t2[:, s, :], part(gr, k, 0).bitcast(F32), ALU.subtract).then_inc(g_ready, 1)
                            continue
                        gate = GATE[name]
                        g, gs = cols(gate, 2, k, 0, 1), by_token(cols(gate, 2, k, 1, C9))
                        xk = tile(x, k)
                        if name == "glu":
                            dve.wait_ge(e_ready, k + 1)
                            TT(halves(t2[:, s, :]), ps[:, 4 * s:4 * s + 2, 0:HALF], halves(t1[:, s, :]), ALU.mult
                               ).then_inc(free[s], 1)
                            dve.wait_ge(free[s], uses(name, s, at) + 1)
                            STT(xk[:, 0:SEQ], t2[:, s, 0:SEQ], g, xk[:, 0:SEQ], ALU.mult, ALU.add)
                            step(TT(sample(t2[:, s, :]), sample(t2[:, s, :]), gs, ALU.mult))
                        else:
                            STT(xk[:, 0:HALF], ps[:, 4 * s, 0:HALF], g, xk[:, 0:HALF], ALU.mult, ALU.add)
                            STT(xk[:, HALF:SEQ], ps[:, 4 * s + 1, 0:SEQ - HALF], g, xk[:, HALF:SEQ], ALU.mult, ALU.add)
                            TT(sample(t2[:, s, :]), ps[:, 4 * s + 1, SEQ - HALF:HALF].rearrange("p (b t) -> p b t", b=DB), gs,
                               ALU.mult).then_inc(free[s], 1)
                            dve.wait_ge(free[s], uses(name, s, at) + 1)
                        TT(xk[:, SEQ:T], xk[:, SEQ:T], t2[:, s, SEQ:T], ALU.add).then_inc(x_ready, 1)

                full_turns = units // per - (0 if tail else 1)
                with step.loop(0, full_turns, steps_) as i:
                    turn(i, False)
                if not tail:
                    turn(units // per - 1, True)

            dense("glu")
            root(1)
            apply("up0")
            dense("up0")
            dense("down0")
            root(2)
            apply("kv")
            dense("kv")
            apply("q")
            dense("q", tail=False)

            def heads(name, src, g, n0):
                with step.loop(0, H // 2, 2) as i:
                    for s in range(2):
                        dve.wait_ge(free[s], uses(name, s, i) + 1)
                        step(REC(t2[:, s, :], t2[:, s, :]))
                        t = tile(src, i * 2 + s)
                        STT(t, t, g, t2[:, s, :], ALU.mult, ALU.mult).then_inc(head_ready, 1)

            heads("khead", kT, vec[:, 120:121], 0)
            heads("qhead", qT, vec[:, 121:122], 8)
            dve.wait_ge(qbd_ready, 1)
            dve.wait_ge(head_ready, 2 * H)
            for m in range(2):
                q = slice(m * DK, (m + 1) * DK)
                done = CP(qbd[q, :, :, m, :], qT[q, :, SEQ:T].rearrange("p h (b t) -> p h b t", b=DB))
            done.then_inc(qbd_ready, 1)

            with step.loop(0, H, QB * 5) as h:
                for i in range(QB):
                    w = (i + 1) * P
                    wait_unit(dve, "attn", 0, h * (QB + 1) + i)
                    if i == 0:
                        dve.wait_ge(head_in, h + 1)
                    step(TT(ps[:, 0:2, i * P:w], ps[:, 0:2, i * P:w], tri[:, :].unsqueeze(1).to_broadcast([P, 2, P]), ALU.add))
                    step(RED(l01[:, 0:2], ps[:, 0:2, 0:w], AX_X, ALU.max))
                    TS(l01[:, 2:4], l01[:, 0:2], -SCALE, None, ALU.mult).then_inc(s_max, 1)
                    dve.wait_ge(free[0], uses("attn", 0, h * (QB + 1) + i) + 1)
                    step(REC(l01[:, 6:8], l01[:, 4:6]))
                    step(TT(l01[:, 7:8], l01[:, 7:8], neglam[:, :], ALU.mult))
                    step(TS(e01[:, 1, 0:w], e01[:, 1, 0:w], l01[:, 7:8], None, ALU.mult))
                    STT(e01[:, 0, 0:w], e01[:, 0, 0:w], l01[:, 6:7], e01[:, 1, 0:w], ALU.mult, ALU.add).then_inc(w_done, 1)
                    wait_unit(dve, "attn", 1, h * QB + i)
                    CP(wtT[:, 0:i + 1, i * P:w], ps[:, 4, 0:w].rearrange("p (k q) -> p k q", q=P)).then_inc(free[1], 1)

            dve.wait_ge(sinit, 1)

            def scores(b):
                buf = sc[:, ds(b % 2, 1)].rearrange("p a k c -> p (a k) c")
                for q in range(4):
                    dve.wait_ge(scored, b * PAGES + 4 * q + 4)
                    CP(buf[:, 4 * q:4 * q + 4].rearrange("p k c -> p (k c)"), ps[:, 4 + q % 2, :]).then_inc(s_copied, 1)

            def maxima(b):
                buf = sc[:, ds(b % 2, 1)].rearrange("p a k c -> p (a k) c")
                dve.wait_ge(new_scored, b + 1)
                step(TT(buf[0:CH, PAGES].rearrange("p (c t) -> p c t", t=CH), ps[0:CH, 7, 0:P].rearrange("p (c t) -> p c t", t=CH),
                        causal[:, :].unsqueeze(1).to_broadcast([CH, P // CH, CH]), ALU.add))
                nc.vector.memset(mark[:, 8:9], 0.0)
                RED(mx[:, 0, :], buf.rearrange("p k c -> p c k"), AX_X, ALU.max).then_inc(m_ready, 1)

            def softmax(b):
                buf = sc[:, ds((b - 1) % 2, 1)].rearrange("p a k c -> p (a k) c")
                dve.wait_ge(m_turned, b)
                step(RED(mx[:, 3, 0:1], ps[:, 7, 0:P], AX_X, ALU.max))
                TS(mx[:, 1, :], ident[:, :], mx[:, 3, 0:1], None, ALU.mult).then_inc(d_ready, 1)
                dve.wait_ge(m_spread, b)
                TT(buf[:, 0:PAGES], buf[:, 0:PAGES], ps[:, 7, P:2 * P].unsqueeze(1).to_broadcast([P, PAGES, P]), ALU.subtract)
                TT(buf[0:CH, PAGES], buf[0:CH, PAGES], ps[0:CH, 7, P:2 * P], ALU.subtract).then_inc(s_low, 1)
                dve.wait_ge(e_full, b)
                nc.vector.memset(mark[:, 10:11], 0.0)
                step(RED(mx[:, 2, :], buf[:, 0:PAGES].rearrange("p k c -> p c k"), AX_X, ALU.add))
                TT(mx[0:CH, 2, :], mx[0:CH, 2, :], buf[0:CH, PAGES], ALU.add).then_inc(l_ready, 1)
                dve.wait_ge(l_spread, b)
                REC(mx[:, 3, :], ps[:, 7, 2 * P:3 * P]).then_inc(l_read, 1)

            def outputs(b):
                dve.wait_ge(l_read, b)
                dve.wait_ge(v_used, b * PAGES + 4)
                o_ = on[:, :, :, :]
                step(TT(o_.rearrange("p h m t -> p (h m t)"), ps[:, 6, 0:P], mx[:, 3, :], ALU.mult))
                STT(oT[:, :, ds((b - 1) * CH + SEQ, CH)], o_[:, :, 1, :], neglam[:, 0:1], o_[:, :, 0, :], ALU.mult, ALU.add
                    ).then_inc(o_ready, 1)

            scores(0)
            maxima(0)
            with step.loop(1, DB - 1, 4) as b:
                softmax(b)
                scores(b)
                outputs(b)
                maxima(b)
            softmax(DB)
            outputs(DB)
            heads("ohead", oT, gaino[:, 0:1], 16)
            split(SLABS["wo"] - DENSE0)
            split(SLABS["wo"] - DENSE0 + 1)
            with dve.Fori(0, H) as k:
                dve.wait_ge(h_high, 4 * KD + 1 + k)
                TT(part(hr, k, 1), tile(oT, k), part(hr, k, 0).bitcast(F32), ALU.subtract).then_inc(h_ready, 1)
            dense("wo")
            root(3)
            apply("up1")
            dense("up1")
            dense("down1", tail=False)


INPUTS = ["x_prompt", "x_sample", "state_ssm_re", "state_ssm_im", "cache_k", "cache_v", "page_table", "c_prompt",
          "c_sample", "norm_mix", "w_ada_mix", "b_ada_mix", "norm_ffn", "w_ada_ffn", "b_ada_ffn", "ffn_w13", "ffn_w2",
          "ssm_lam_re", "ssm_lam_im", "ssm_log_step", "ssm_b_re", "ssm_b_im", "ssm_c_re", "ssm_c_im", "ssm_d",
          "ssm_w_glu", "norm_kv", "w_ada_kv", "b_ada_kv", "w_kv", "k_norm", "w_q", "q_norm", "diff_lambda", "subln", "w_o"]


def kernel(**inputs):
    import numpy as np
    import concourse.bacc as bacc
    from concourse.bass_utils import run_bass_kernel_spmd

    nc = bacc.Bacc("TRN2", target_bir_lowering=False, num_devices=1)
    arrays, args = {}, {}
    for name in INPUTS:
        v = np.ascontiguousarray(inputs[name])
        arrays[f"in_{name}"] = v
        args[name] = nc.dram_tensor(f"in_{name}", v.shape, mybir.dt.from_np(v.dtype), kind="ExternalInput").ap()
    xp, xs = inputs["x_prompt"].shape, inputs["x_sample"].shape
    layers, _, groups, states = inputs["state_ssm_re"].shape
    heads, two, dk = inputs["cache_k"].shape[2:]
    dv = inputs["cache_v"].shape[3]
    shapes = [xp, xs] + [(layers, xp[0], groups, states)] * 2 + [(layers, xs[0], groups, states)] * 2 + [
        (*xp[:2], heads, two, dk), (*xp[:2], heads, dv), (*xs[:2], heads, two, dk), (*xs[:2], heads, dv)]
    outs = [nc.dram_tensor(f"out_{i}", s, F32, kind="ExternalOutput").ap() for i, s in enumerate(shapes)]
    yoco_step(nc, args, outs)
    r = run_bass_kernel_spmd(nc, [arrays], core_ids=[0])
    return tuple(r.results[0][f"out_{i}"] for i in range(len(shapes)))
```

```python
from contextlib import ExitStack
import math

import concourse.bass as bass
from concourse import mybir

ALU = mybir.AluOpType
ACT = mybir.ActivationFunctionType
F32 = mybir.dt.float32
F32R = mybir.dt.float32r
I32 = mybir.dt.int32
AX_X = mybir.AxisListType.X
ds = bass.ds

P = 128
BANK = 512
EPS = 1e-6
MASKED = -1.0e30
ROUND = 12582912.0
TWO_PI_PARTS = (6.28125, 0.001934051513671875, 1.2556659146e-06)
PI_BELOW = 3.1415925


class Steps:

    def __init__(self, eng, sem):
        self.eng, self.sem, self.start, self.k = eng, sem, 0, 0

    def __call__(self, ins):
        ins.then_inc(self.sem, 1)
        self.k += 1
        self.eng.wait_ge(self.sem, self.start + self.k)

    def loop(self, first, turns, per):
        steps = self

        class Turns:
            def __enter__(self):
                self.base = steps.start + steps.k
                self.fori = steps.eng.Fori(first, first + turns)
                i = self.fori.__enter__()
                steps.start, steps.k = self.base - first * per + i * per, 0
                return i

            def __exit__(self, *e):
                r = self.fori.__exit__(*e)
                assert e[0] is not None or steps.k == per, (steps.k, per)
                steps.start, steps.k = self.base + turns * per, 0
                return r

        return Turns()


def yoco_step(nc, a, out):
    SEQ, D = a["x_prompt"].shape[1:]
    DB, DS = a["x_sample"].shape[:2]
    G, N, PP = a["ssm_b_re"].shape[1:]
    H, DK = a["cache_k"].shape[2], a["cache_k"].shape[4]
    DV = a["cache_v"].shape[3]
    PAGES, NPOOL = a["page_table"].shape[1], a["cache_k"].shape[0]
    DFF = a["ffn_w2"].shape[1]
    T = SEQ + DB * DS
    HALF = T // 2
    KD = D // P
    FT = DFF // P
    CH = DS
    NCH = T // CH
    PCH = SEQ // CH
    J = G // 2
    TAU = CH + 1
    C9 = 1 + DB
    SCALE = DK ** -0.5
    LAM_INIT = 0.8 - 0.6 * math.exp(-0.3 * 1)
    QB = SEQ // P
    LAG = 2
    NBUF = LAG + 1
    HQ = 2 * CH
    assert D == 1024 and 2 * DK == P and DV == P and CH * PP == P and 2 * N == P and H == KD
    assert a["cache_k"].shape[1] == P and PAGES == 16 and SEQ == BANK and (DB - LAG) % NBUF == 0

    PLAN = [("small", 1), ("x", 5), ("norm0", 1), ("ada0.0", 6), ("ssm_k0", 2), ("ada1.0", 2),
            ("ssm_k1", 2), ("ada1.1", 4), ("ssm_v", 4), ("ssm_w", 4), ("ada2.0", 4), ("ada3.0", 6), ("ssm_y0", 2),
            ("ada4.0", 2), ("ssm_y1", 2), ("ada4.1", 2), ("ssm_h", 1), ("ada4.2", 2),
            ("glu", 8), ("norm1", 1), ("up0", 22), ("down0", 8), ("norm2", 1), ("kv", 16), ("q", 8),
            ("khead", 8), ("qhead", 8), ("ktok", 5), ("vtok", 5), ("attn", None),
            ("ohead", 8), ("wo", 8), ("norm3", 1), ("up1", 22), ("down1", 8), ("y", 5)]
    USES, seen = {}, [0, 0]
    for name, n in PLAN:
        USES[name] = tuple(seen)
        seen[0] += H * (QB + 1) if n is None else (n + 1) // 2
        seen[1] += H * QB if n is None else n // 2

    ADA_END = [[USES[f"ada{n}.{p}"][s] + k for s in range(2)] for n, (p, k) in enumerate([(0, 3), (1, 2), (0, 2), (0, 3), (2, 1)])]

    COUNT = {"ada0": 24, "ada1": 24, "ada2": 16, "ada3": 24, "ada4": 24, "glu": 16, "up0": 2 * FT,
             "down0": 4 * KD, "kv": 16, "q": 8, "wo": 8, "up1": 2 * FT, "down1": 4 * KD}
    SLABS, n_slabs = {}, 0
    for name, n in COUNT.items():
        SLABS[name] = n_slabs
        n_slabs += n
        assert n % 4 == 0

    DENSE0 = SLABS["glu"]

    PAIR = [(0, 0, 8), (1, 0, 8)]
    ONE = [(0, 0, 8)]
    LONG = [(0, 0, 6), (0, 6, 6), (0, 12, 6), (0, 18, 4)]
    DENSE = {"glu": (8, PAIR, 2), "up0": (22, PAIR, 2), "down0": (8, LONG, 2), "kv": (16, ONE, 4),
             "q": (8, ONE, 4), "wo": (8, ONE, 4), "up1": (22, PAIR, 2), "down1": (8, LONG, 2)}
    INNER, n_inner = {}, 0
    for name, (units, slabs, _) in DENSE.items():
        INNER[name] = n_inner
        n_inner += units * (len(slabs) - 1)

    base = -(-nc.sbuf_base // 64) * 64
    place = [base]

    def keep(name, shape, dt=F32):
        size = 4 * math.prod(shape[1:])
        t = nc.alloc_sbuf_tensor_at(name, shape, dt, offset=place[0])
        place[0] += -(-size // 32) * 32
        return t

    x = keep("x", [P, KD, T])
    raw = keep("raw", [P, 4, 8, P])
    vec = keep("vec", [P, 3 * P])
    cond = keep("cond", [P, KD, 32])
    add4 = keep("add4", [P, C9])
    mod = keep("mod", [P, 5, 24, C9])
    gain = keep("gain", [P, 5, KD, C9])
    t1 = keep("t1", [P, 2, T])
    t2 = keep("t2", [P, 2, T])
    rstd = keep("rstd", [P, T])
    sqs = rstd
    sqt = keep("sqt", [P, HALF])
    ident = keep("ident", [P, P])
    ones = keep("ones", [P, P])
    eps = keep("eps", [P, 1])
    neglam = keep("neglam", [P, 1])
    gaino = keep("gaino", [P, 1])
    pages = keep("pages", [1, DB * PAGES], I32)
    mark = keep("mark", [P, 12])
    over = place[0]

    def share(name, shape, at, dt=F32):
        return nc.alloc_sbuf_tensor_at(name, shape, dt, offset=over + at)

    KB = 1024
    SMALL = 21
    wh = share("wh", [P, (2 * NCH + 1) * 2 * J], 0)
    drive = wh[:, 0:NCH * 2 * J].rearrange("p (c r j) -> p c r j", c=NCH, r=2)
    hs = wh[:, NCH * 2 * J:].rearrange("p (c r j) -> p c r j", c=NCH + 1, r=2)
    vmat = wh[:, 0:2 * CH * J * PP].rearrange("p (r j s q) -> p r j s q", r=2, j=J, s=CH)
    o = 4 * (2 * NCH + 1) * 2 * J
    vk = share("vk", [P, G * P], o)
    vT = vk[:, :].rearrange("p (j r m) -> p j r m", j=J, r=2)
    kmat = vk[:, :].rearrange("p (g m) -> p g m", g=G)
    krow = share("krow", [PP, 2, 16, P], o)
    o += 4 * G * P
    cpow = share("cpow", [P, J, 2, TAU, PP], o)
    o += 4 * J * 2 * TAU * PP
    uch = share("uch", [P, G, NCH], o)
    craw = share("craw", [P, 2, 4, P], o)
    hraw = share("hraw", [P, 2, 2, P], o + 4 * KB)
    xtok = share("xtok", [P, 2, D], o + 6 * KB)
    v1 = share("v1", [P, P], o + 14 * KB)
    v2 = share("v2", [P, P], o + 14 * KB + 512)
    v3 = share("v3", [P, P], o + 15 * KB)
    lst = share("lst", [96, 2], o + 15 * KB + 512)
    lrow = share("lrow", [P, 4, DK], o + 16 * KB)
    ltmp = share("ltmp", [P, 2, DK], o + 17 * KB)
    lsum = share("lsum", [P, 4], o + 17 * KB + 512)
    o += 4 * G * NCH
    bmat = share("bmat", [P, 2, J, PP], o)
    bbar = share("bbar", [P, 2, J, PP], o + 4 * KB)
    cT = share("cT", [P, 2, J, PP], o + 8 * KB)
    ysb = share("ysb", [P, 2, 16 * NCH], o)
    hout = share("hout", [P, 6, P], o + 9 * KB)
    o += 12 * KB
    pw = share("pw", [P, TAU, 2, J], o)
    pws = share("pws", [P, 2, J], o + 4 * TAU * 2 * J)
    h0 = share("h0", [P, 2, DB * J], o + 3 * KB)
    hfin = share("hfin", [P, 2, DB, J], o + 5 * KB)
    tiny = share("tiny", [P, 14, J], o + 7 * KB)
    tA = share("tA", [P, J * PP], o + 9 * KB)
    tB = share("tB", [P, J * PP], o + 11 * KB)
    pA = share("pA", [P, J * PP], o + 13 * KB)
    pB = share("pB", [P, J * PP], o + 15 * KB)
    o += 17 * KB
    assert over + o <= nc.sbuf_usable_end, over + o
    yin = share("yin", [P, 2, CH, NCH], 120 * KB)
    uin = share("uin", [P, 2, CH, NCH], 125 * KB)
    ws = share("ws", [P, 2, 2, 8, P], 0, F32R)
    hr = share("hr", [P, KD, 2, T], 16 * KB, F32R)
    gr = share("gr", [P, FT, 2, T], 52 * KB, F32R)
    assert over + 52 * KB + 8 * FT * T <= nc.sbuf_usable_end, over + 52 * KB + 8 * FT * T
    kvT = share("kvT", [P, 2 * H, T], 52 * KB)
    kT, vTf = kvT[:, 0:H], kvT[:, H:2 * H]
    qT = share("qT", [P, H, T], 88 * KB)
    oT = vTf
    tok = share("tok", [P, 2, D], 110 * KB)
    vtok = share("vtok", [P, QB, H, DV], 118 * KB)
    e01 = share("e01", [P, 2, SEQ], 134 * KB)
    wtT = share("wtT", [P, QB, SEQ], 138 * KB)
    l01 = share("l01", [P, 8], 146 * KB)
    qh = share("qh", [P, SEQ], 0)
    kh = share("kh", [P, SEQ], 2 * KB)
    vh = share("vh", [P, QB, DV], 4 * KB)
    tri = share("tri", [P, P], 6 * KB)
    kpg = share("kpg", [P, 4, H, P], 0)
    vpg = share("vpg", [P, 4, H, DV], 16 * KB)
    kTs = share("kTs", [P, 2, 2, BANK], 32 * KB)
    sc = share("sc", [P, NBUF, PAGES * P + CH], 110 * KB)
    wT = share("wT", [P, 2, BANK], 135 * KB)
    wn = share("wn", [CH, P], 139 * KB)
    osb = share("osb", [P, 2 * DV], 140 * KB)
    kn = share("kn", [P, NBUF, H, CH], 141 * KB)
    qn = share("qn", [P, NBUF, H, 2 * HQ], 142 * KB)
    vn = share("vn", [CH, D], 145 * KB)
    mq = share("mq", [P, 2, 8], 149 * KB)
    pick = share("pick", [P, 4 * CH], 149 * KB + 512)
    sign = share("sign", [P, 2], 150 * KB)
    blockd = share("blockd", [P, P], 150 * KB + 32)
    causal = share("causal", [CH, P], 150 * KB + 544)
    assert 151 * KB + 32 <= nc.sbuf_usable_end - over

    ps = nc.alloc_psum_tensor("ps", [P, 8, BANK], F32)

    u_scr = nc.dram_tensor("u_scr", [D, CH, NCH], F32, kind="Internal").ap()
    y_scr = nc.dram_tensor("y_scr", [D, CH, NCH], F32, kind="Internal").ap()
    k_scr = nc.dram_tensor("k_scr", [PP, G, P], F32, kind="Internal").ap()

    with ExitStack() as ctx:
        def sem(name):
            return ctx.enter_context(nc.semaphore(name))

        full = [sem(f"full{s}") for s in range(2)]
        free = [sem(f"free{s}") for s in range(2)]
        raw_full = [sem(f"raw_full{s}") for s in range(4)]
        raw_done = [sem(f"raw_done{s}") for s in range(4)]
        in_small, in_x, in_b = sem("in_small"), [sem("in_x0"), sem("in_x1")], sem("in_b")
        dve_step, act_step, pool_step = sem("dve_step"), sem("act_step"), sem("pool_step")
        consts, v3_built = sem("consts"), sem("v3_built")
        x_ready, sq_ready, root_ready = sem("x_ready"), sem("sq_ready"), sem("root_ready")
        cond_ready, dt_ready, sincos_in, sincos_out = sem("cond_ready"), sem("dt_ready"), sem("sincos_in"), sem("sincos_out")
        mod_ready, bbar_ready, cpow_ready, v_ready = sem("mod_ready"), sem("bbar_ready"), sem("cpow_ready"), sem("v_ready")
        t1_ready, t2_sample, t2_ready, h_high, h_ready = sem("t1_ready"), sem("t2_sample"), sem("t2_ready"), sem("h_high"), sem("h_ready")
        t2_prompt = sem("t2_prompt")
        u_got, kmat_zero, kmat_got = sem("u_got"), sem("kmat_zero"), sem("kmat_got")
        u_put, k_put = [sem("u_put0"), sem("u_put1")], [sem("k_put0"), sem("k_put1")]
        y_put, y_got, hs_ready, hfin_ready = [sem("y_put0"), sem("y_put1")], [sem("y_got0"), sem("y_got1")], sem("hs_ready"), sem("hfin_ready")
        hout_ready, yu_ready = sem("hout_ready"), sem("yu_ready")
        slab_high, slab_read = sem("slab_high"), sem("slab_read")
        e_ready, g_high, g_ready, rows_ready = sem("e_ready"), sem("g_high"), sem("g_ready"), sem("rows_ready")
        sq_head, root_head, head_ready = sem("sq_head"), sem("root_head"), sem("head_ready")
        tok_ready, tok_put, vtok_ready = sem("tok_ready"), [sem("tok_put0"), sem("tok_put1")], sem("vtok_ready")
        head_in, s_max, e_done, w_done, wt_done, pv_out = sem("head_in"), sem("s_max"), sem("e_done"), sem("w_done"), sem("wt_done"), sem("pv_out")
        k_full, v_full = [sem(f"k_full{s}") for s in range(4)], [sem(f"v_full{s}") for s in range(4)]
        k_turned, kt_ready, scored, s_copied, v_used, w_ready, w_turned, wt_copied, o_copied, o_turned = sem("k_turned"), sem("kt_ready"), sem("scored"), sem("s_copied"), sem("v_used"), sem("w_ready"), sem("w_turned"), sem("wt_copied"), sem("o_copied"), sem("o_turned")
        kn_ready, vn_full, new_scored, m_ready, m_turned, d_ready, m_spread, s_low, e_full, l_ready, l_spread, l_read, vn_used, o_ready = (
            sem("kn_ready"), sem("vn_full"), sem("new_scored"), sem("m_ready"), sem("m_turned"), sem("d_ready"), sem("m_spread"),
            sem("s_low"), sem("e_full"), sem("l_ready"), sem("l_spread"), sem("l_read"), sem("vn_used"), sem("o_ready"))
        qbd_ready, sinit, put, vput, in_pages = sem("qbd_ready"), sem("sinit"), sem("put"), sem("vput"), sem("in_pages")
        blocks_ready, square_ready, square_used = sem("blocks_ready"), sem("square_ready"), sem("square_used")

        def uses(phase, s, i=0):
            return USES[phase][s] + i

        def wait_unit(eng, phase, s, i=0):
            eng.wait_ge(full[s], uses(phase, s, i) + 1)

        def wait_set(phase, s, i=0):
            n = uses(phase, s, i)
            if not (isinstance(n, int) and n == 0):
                nc.tensor.wait_ge(free[s], n)

        def halves(t):
            return t.rearrange("p (a b) -> p a b", a=2)

        dtok = [a["x_prompt"][0, i * P:(i + 1) * P, :] for i in range(QB)] + [
            a["x_sample"].rearrange("b t d -> (b t) d")]
        NTOK = [P] * QB + [DB * DS]

        def slab_source(name):
            kp = "(k p) n -> p k n"
            w = {"ada0": a["w_ada_mix"][0], "ada1": a["w_ada_ffn"][0], "ada2": a["w_ada_kv"],
                 "ada3": a["w_ada_mix"][1], "ada4": a["w_ada_ffn"][1], "glu": a["ssm_w_glu"][0],
                 "up0": a["ffn_w13"][0], "down0": a["ffn_w2"][0], "kv": a["w_kv"], "q": a["w_q"][0],
                 "wo": a["w_o"][0], "up1": a["ffn_w13"][1], "down1": a["ffn_w2"][1]}[name]
            return w.rearrange(kp, p=P)

        block = ctx.enter_context(nc.Block())

        @block.sync
        def _(sp):
            def small(dst, src):
                sp.dma_start(dst, src).then_inc(in_small, 16)

            rows = "l (k p) -> (l k) p"
            small(v1[0:8, :], a["c_prompt"].rearrange(rows, p=P))
            small(v1[8:72, :], a["c_sample"].rearrange(rows, p=P))
            small(v1[72:88, :], a["norm_mix"].rearrange(rows, p=P))
            small(v1[88:104, :], a["norm_ffn"].rearrange(rows, p=P))
            small(v1[104:112, :], a["norm_kv"].rearrange("(k p) -> k p", p=P))
            small(v1[112:120, :], a["ssm_d"].rearrange(rows, p=P))
            small(v1[120:121, :], a["k_norm"].rearrange("(o m) d -> o (m d)", o=1))
            small(v1[121:122, :], a["q_norm"].rearrange("o m d -> o (m d)"))
            small(v1[122:123, :], a["subln"])
            small(v2[0:48, :], a["b_ada_mix"].rearrange(rows, p=P))
            small(v2[48:96, :], a["b_ada_ffn"].rearrange(rows, p=P))
            small(v2[96:112, :], a["b_ada_kv"].rearrange("(k p) -> k p", p=P))
            small(v3[0:32, :], a["ssm_lam_re"][0].rearrange("(j g) n -> j (g n)", g=2))
            small(v3[32:64, :], a["ssm_lam_im"][0].rearrange("(j g) n -> j (g n)", g=2))
            small(lst[64:96, :], a["ssm_log_step"][0].rearrange("(j g) -> j g", g=2))
            for r, name in enumerate(("state_ssm_re", "state_ssm_im")):
                for k in range(2):
                    small(hraw[:, r, k, :], a[name][0, 4 * k:4 * k + 4].rearrange("b (j g) n -> (b j) (g n)", g=2))
            small(lrow[:, :, :].rearrange("p k d -> p (k d)"), a["diff_lambda"].rearrange("o k d -> o (k d)").to_broadcast([P, 4 * DK]))
            small(pages[:, :], a["page_table"].rearrange("(o b) p -> o (b p)", o=1))
            sp.dma_start(xtok[:, 0, :], dtok[0]).then_inc(in_x[0], 16)
            sp.dma_start(xtok[:, 1, :], dtok[1]).then_inc(in_x[1], 16)

            def slabs(name, cols, k0=lambda j: 0, nk=lambda j: 8, per=4):
                src, first = slab_source(name), SLABS[name]

                def turn(i):
                    for j in range(per):
                        slot = j % 4
                        if first or not isinstance(i, int):
                            sp.wait_ge(raw_done[slot], (first + j) // 4 + i * (per // 4))
                        a0, n = k0(j), nk(j)
                        sp.dma_start(raw[:, slot, 0:n, :], src[:, a0:a0 + n, ds(cols(i, j), P)]
                                     ).then_inc(raw_full[slot], 16)

                if first == 0:
                    turn(0)
                with sp.Fori(0 if first else 1, COUNT[name] // per) as i:
                    turn(i)

            def one(i, j):
                return i * (4 * P) + j * P

            def pair(half):
                return lambda i, j: i * (2 * P) + (j // 2) * P + (j % 2) * half

            def long(i, j):
                return i * (2 * P) + (j // 4) * P

            def page_loads(b, o, u, keys, values):
                slot = u % 4
                for go, seq, cache, dst, ready in ((keys, b, "cache_k", kpg, k_full), (values, b - LAG, "cache_v", vpg, v_full)):
                    if not go:
                        continue
                    at = seq * PAGES + o * 8 + u
                    page = sp.value_load(pages[0:1, ds(at, 1)], min_val=0, max_val=NPOOL - 1)
                    if cache == "cache_v":
                        sp.wait_ge(v_used, at + 1)
                    elif not isinstance(at, int) or at > 3:
                        sp.wait_ge(k_turned, at * 2 - 6)
                    form = "o k h m d -> k (o h m d)" if cache == "cache_k" else "o k h d -> k (o h d)"
                    sp.dma_start(dst[:, slot].rearrange("p h m -> p (h m)"), a[cache][ds(page, 1)].rearrange(form)
                                 ).then_inc(ready[slot], 16)

            slabs("ada0", one)
            for name in ("ada1", "ada2", "ada3", "ada4"):
                slabs(name, one)
            slabs("glu", pair(D))
            for layer in range(2):
                slabs(f"up{layer}", pair(DFF))
                slabs(f"down{layer}", long, k0=lambda j: 6 * (j % 4), nk=lambda j: (6, 6, 6, 4)[j % 4], per=8)
                if layer:
                    break
                slabs("kv", one)
                slabs("q", one)
                sp.wait_ge(in_small, 16 * SMALL)
                for s in range(2):
                    sp.wait_ge(free[s], USES["ohead"][s])
                for u in range(PAGES):
                    page_loads(0, u // 8, u % 8, True, False)

                def loads(b, keys=True, values=True):
                    with sp.Fori(0, PAGES // 8) as o:
                        for u in range(8):
                            page_loads(b, o, u, keys, values)

                for b in range(1, LAG):
                    loads(b, values=False)
                with sp.Fori(LAG, DB) as b:
                    loads(b)
                for b in range(DB, DB + LAG):
                    loads(b, keys=False)
                slabs("wo", one)
            sp.wait_ge(put, 16 * 6)
            for s in range(2):
                sp.wait_ge(tok_put[s], 16 * 3 * (3 - s))

        @block.tensor
        def _(pe):
            mm = nc.tensor.matmul

            def turn(dst, src, rows=P):
                return nc.tensor.transpose(dst, src, ident[0:rows, 0:rows])

            pe.wait_ge(consts, 3)
            pe.wait_ge(in_small, 16 * SMALL)
            pe.wait_ge(in_b, 16 * 18)
            pe.wait_ge(v3_built, 1)
            turn(ps[:, 0, 0:123], v1[0:123, :], 123)
            turn(ps[:, 0, P:P + 112], v2[0:112, :], 112)
            turn(ps[:, 0, 2 * P:2 * P + 96], v3[0:96, :], 96)
            for r in range(2):
                for k in range(2):
                    turn(ps[:, 1, (2 * r + k) * P:(2 * r + k + 1) * P], hraw[:, r, k, :])
                for k in range(4):
                    last = turn(ps[:, 2 + r, k * P:(k + 1) * P], craw[:, r, k, :])
            last.then_inc(full[0], 1)

            for i in range(QB + 1):
                s = i % 2
                wait_set("x", s, i // 2)
                pe.wait_ge(in_x[s], 16 * (i // 2 + 1))
                for k in range(KD):
                    last = turn(ps[:, 4 * s + k // 4, (k % 4) * P:(k % 4) * P + NTOK[i]],
                                xtok[0:NTOK[i], s, k * P:(k + 1) * P], NTOK[i])
                last.then_inc(full[s], 1)

            def ada(n, first, turns):
                name = f"ada{n}.{first}"
                pe.wait_ge(cond_ready, 2)
                with pe.Fori(0, turns) as i:
                    for s in range(2):
                        unit = i * 2 + (SLABS[f"ada{n}"] // 4 + 2 * first + s)
                        wait_set(name, s, i)
                        for j in range(4):
                            pe.wait_ge(raw_full[j], (unit + 1) * 16)
                            for k in range(KD):
                                g = k % 4
                                last = mm(ps[32 * g:32 * g + 32, 4 * s, j * P:(j + 1) * P], cond[:, k, :], raw[:, j, k, :],
                                          start=(k < 4), stop=(k >= 4))
                            last.then_inc(raw_done[j], 1)
                        pe.wait_ge(rows_ready, unit + 1)
                        for j in range(4):
                            last = mm(ps[:, 4 * s + 1, j * C9:(j + 1) * C9], t2[:, s, j * P:(j + 1) * P], add4[:, :],
                                      start=True, stop=True)
                        last.then_inc(full[s], 1)

            def norm(n):
                name = f"norm{n}"
                wait_set(name, 0)
                pe.wait_ge(sq_ready, n)
                for h in range(2):
                    last = mm(ps[:, h, 0:HALF], ones[:, :], halves(sqs[:, :])[:, h, :], start=True, stop=True)
                last.then_inc(full[0], 1)

            def dense(name, ready=None):
                units, slabs, per = DENSE[name]
                n0, S = SLABS[name], len(slabs)
                g0 = n0 - SLABS["glu"]
                src = gr if name.startswith("down") else hr
                kfirst = {"glu": 0, "up0": 8, "kv": 16, "q": 24, "wo": 32, "up1": 40}.get(name)
                with pe.Fori(0, units // per) as i:
                    for u in range(per):
                        s = u % 2
                        wait_set(name, s, i * (per // 2) + u // 2)
                        for j, (tile, k0, nk) in enumerate(slabs):
                            n = u * S + j
                            slot, wslot = n % 4, n % 2
                            pe.wait_ge(raw_done[slot], (n0 + n) // 4 + 1 + i * (per * S // 4))
                            for k in range(nk):
                                if u == 0 and name.startswith("down"):
                                    pe.wait_ge(g_ready, FT * int(name[-1]) + k0 + k + 1)
                                elif u == 0 and j == 0:
                                    pe.wait_ge(h_ready, kfirst + k + 1)
                                for w, v in ((0, 0), (0, 1), (1, 0)):
                                    for h in range(2):
                                        first = k0 + k == 0 and (w, v) == (0, 0)
                                        end = j == S - 1 or slabs[j + 1][0] != tile
                                        last = mm(ps[:, 4 * s + 2 * tile + h, 0:HALF], ws[:, wslot, w, k, :],
                                                  src[:, k0 + k, v, h * HALF:(h + 1) * HALF], start=first,
                                                  stop=(end and k == nk - 1 and (w, v) == (1, 0)))
                            last.then_inc(full[s] if j == S - 1 else slab_read, 1)

            wait_set("norm0", 0)
            for k in range(KD):
                pe.wait_ge(square_ready, k + 1)
                for h in range(2):
                    last = mm(ps[:, h, 0:HALF], ones[:, :], t1[:, k % 2, h * HALF:(h + 1) * HALF], start=(k == 0), stop=(k == KD - 1))
                last.then_inc(square_used if k < KD - 1 else full[0], 1)
            ada(0, 0, 3)

            pe.wait_ge(bbar_ready, 1)
            pe.wait_ge(cpow_ready, 1)
            for u in range(4):
                s = u % 2
                if u == 2:
                    ada(1, 0, 1)
                wait_set(f"ssm_k{u // 2}", s)
                for i in range(4):
                    g2, jj = i // 2, i % 2
                    q = slice(g2 * N, (g2 + 1) * N)
                    for r in range(2):
                        for t in range(4):
                            j = u * 8 + jj * 4 + t
                            last = mm(ps[32 * t:32 * t + PP, 4 * s + g2, jj * P:(jj + 1) * P], bbar[q, r, j, :],
                                      cpow[q, j, r, 0:CH, :].rearrange("p t q -> p (t q)"), start=(r == 0), stop=(r == 1))
                last.then_inc(full[s], 1)
            ada(1, 1, 2)
            pe.wait_ge(v_ready, 2)
            for u in range(4):
                s = u % 2
                wait_set("ssm_v", s, u // 2)
                for jj in range(8):
                    for r in range(2):
                        i = jj * 2 + r
                        last = turn(ps[:, 4 * s + i // 4, (i % 4) * P:(i % 4 + 1) * P],
                                    vmat[:, r, u * 8 + jj].rearrange("p s q -> p (s q)"))
                last.then_inc(full[s], 1)
            for s in range(2):
                pe.wait_ge(free[s], USES["ssm_w"][s])
            pe.wait_ge(u_got, 16 * CH)
            for u in range(4):
                s = u % 2
                wait_set("ssm_w", s, u // 2)
                for jj in range(8):
                    j = u * 8 + jj
                    for r in range(2):
                        for g2 in range(2):
                            at = (jj % 2) * 2 * NCH + r * NCH
                            last = mm(ps[g2 * N:(g2 + 1) * N, 4 * s + jj // 2, at:at + NCH],
                                      vT[:, j, r, g2 * N:(g2 + 1) * N], uch[:, 2 * j + g2, :], start=True, stop=True)
                last.then_inc(full[s], 1)
            ada(2, 0, 2)
            ada(3, 0, 3)
            pe.wait_ge(kmat_got, 16 * CH)
            pe.wait_ge(hs_ready, 1)
            for u in range(4):
                s = u % 2
                if u == 2:
                    ada(4, 0, 1)
                wait_set(f"ssm_y{u // 2}", s)
                for i in range(16):
                    g2, jj = i // 8, i % 8
                    j = u * 8 + jj
                    q = slice(g2 * N, (g2 + 1) * N)
                    dst = ps[:, 4 * s + 2 * g2 + jj // 4, (jj % 4) * NCH:(jj % 4 + 1) * NCH]
                    mm(dst, kmat[:, 2 * j + g2, :], uch[:, 2 * j + g2, :], start=True, stop=False)
                    for r in range(2):
                        last = mm(dst, cpow[q, j, r, 1:TAU, :].rearrange("p t q -> p (t q)"), hs[q, 0:NCH, r, j],
                                  start=False, stop=(r == 1))
                last.then_inc(full[s], 1)
            ada(4, 1, 1)
            wait_set("ssm_h", 0)
            pe.wait_ge(hfin_ready, 1)
            for r in range(2):
                turn(ps[0:J, r, 0:P], hs[:, NCH, r, :], P)
                for k in range(2):
                    last = turn(ps[:, r, (k + 1) * P:(k + 2) * P], hfin[:, r, 4 * k:4 * k + 4, :].rearrange("p b j -> p (b j)"))
            last.then_inc(full[0], 1)

            ada(4, 2, 1)
            dense("glu")
            norm(1)
            dense("up0")
            dense("down0")
            norm(2)
            dense("kv")
            dense("q")

            def heads(name, m, n0):
                with pe.Fori(0, H // 2) as i:
                    for s in range(2):
                        wait_set(name, s, i)
                        pe.wait_ge(sq_head, n0 + s + 1 + 2 * i)
                        for h in range(2):
                            last = mm(ps[:, 4 * s + h, 0:HALF], m[:, :], t1[:, s, h * HALF:(h + 1) * HALF],
                                      start=True, stop=True)
                        last.then_inc(full[s], 1)

            pe.wait_ge(blocks_ready, 1)
            heads("khead", blockd, 0)
            heads("qhead", blockd, 8)
            for n, (name, src) in enumerate((("ktok", kT), ("vtok", vTf))):
                if n == 0:
                    pe.wait_ge(head_ready, 8)
                for i in range(QB + 1):
                    s = i % 2
                    wait_set(name, s, i // 2)
                    for h in range(H):
                        last = turn(ps[0:NTOK[i], 4 * s + h // 4, (h % 4) * P:(h % 4 + 1) * P],
                                    src[:, h, i * P:i * P + NTOK[i]])
                    last.then_inc(full[s], 1)

            with pe.Fori(0, H) as h:
                pe.wait_ge(head_in, h + 1)
                for i in range(QB):
                    w = (i + 1) * P
                    wait_set("attn", 0, h * (QB + 1) + i)
                    for m in range(2):
                        q = slice(m * DK, (m + 1) * DK)
                        last = mm(ps[:, m, 0:w], qh[q, i * P:w], kh[q, 0:w], start=True, stop=True)
                    last.then_inc(full[0], 1)
                    wait_set("attn", 1, h * QB + i)
                    pe.wait_ge(w_done, h * QB + i + 1)
                    for k in range(i + 1):
                        last = turn(ps[:, 4, k * P:(k + 1) * P], e01[:, 0, k * P:(k + 1) * P])
                    last.then_inc(full[1], 1)
                wait_set("attn", 0, h * (QB + 1) + QB)
                wait_set("attn", 1, h * QB + QB)
                for k in range(QB):
                    last = mm(ps[:, 0, k * P:SEQ], vh[:, k, :], wtT[:, k, k * P:SEQ], start=(k == 0), stop=(k == QB - 1))
                last.then_inc(full[0], 1)

            for s in range(2):
                pe.wait_ge(free[s], USES["ohead"][s])

            def turn_page(b, par, u):
                slot = u % 4
                pe.wait_ge(k_full[slot], 16 * (b * (PAGES // 4) + u // 4 + 1))
                for half in range(2):
                    at = (b * PAGES + u) * 2 + half
                    bank = ((par * PAGES + u) * 2 + half) % 3
                    if not isinstance(at, int) or at > 2:
                        pe.wait_ge(kt_ready, at - 2)
                    for h in range(4):
                        last = turn(ps[:, bank, h * P:(h + 1) * P], kpg[:, slot, 4 * half + h, :])
                    last.then_inc(k_turned, 1)

            def scores(b, par, u):
                at = b * PAGES + u
                quad = b * (PAGES // 4) + u // 4
                if u % 4 == 0 and (not isinstance(quad, int) or quad > 1):
                    pe.wait_ge(s_copied, quad - 1)
                if u == 0:
                    pe.wait_ge(kn_ready, b + 1)
                pe.wait_ge(kt_ready, at * 2 + 2)
                for o in range(2):
                    for g in range(4):
                        h = 2 * g + o
                        last = mm(ps[32 * g:32 * g + 32, 4 + u // 4 % 2, (u % 4) * P:(u % 4 + 1) * P], qn[:, par % NBUF, h, :],
                                  kTs[:, u % 2, h // 4, (h % 4) * P:(h % 4 + 1) * P], start=(o == 0), stop=(o == 1))
                last.then_inc(scored, 1)

            def b_has(b, n):
                return not isinstance(b, int) or b >= n

            def new_scores(b, par):
                if b_has(b, LAG):
                    pe.wait_ge(o_ready, b - LAG + 1)
                if b_has(b, 1):
                    pe.wait_ge(m_ready, b)
                for g in range(4):
                    dst = ps[32 * g:32 * g + 32, 3, 0:CH]
                    for o in range(2):
                        mm(dst, qn[:, par % NBUF, 2 * g + o, :], kn[:, par % NBUF, 2 * g + o, :], start=(o == 0), stop=False)
                    last = mm(dst, causal[:, 32 * g:32 * g + 32], ident[0:CH, 0:CH], start=False, stop=True)
                last.then_inc(new_scored, 1)

            def turn_weights(b, par, q):
                if q == 0:
                    pe.wait_ge(w_ready, b - LAG + 1)
                pe.wait_ge(wt_copied, (b - LAG) * 5 + q + 1)
                src = sc[:, (par - LAG) % NBUF]
                if q == 4:
                    last = turn(ps[0:CH, 7, 0:P], src[:, PAGES * P:])
                else:
                    for u in range(4):
                        last = turn(ps[:, 7, u * P:(u + 1) * P], src[:, (4 * q + u) * P:(4 * q + u + 1) * P])
                last.then_inc(w_turned, 1)

            def values(b, u):
                slot = u % 4
                if u == 0:
                    pe.wait_ge(o_copied, b - LAG + 1)
                if u % 4 == 0:
                    pe.wait_ge(wt_copied, (b - LAG) * 5 + u // 4 + 2)
                pe.wait_ge(v_full[slot], 16 * ((b - LAG) * (PAGES // 4) + u // 4 + 1))
                for h in range(H):
                    g = h % 4
                    last = mm(ps[32 * g:32 * g + HQ, 6, (h // 4) * DV:(h // 4 + 1) * DV],
                              wT[:, u // 4 % 2, (u % 4) * P + h * HQ:(u % 4) * P + (h + 1) * HQ],
                              vpg[:, slot, h, :], start=(u == 0 and h < 4), stop=False, skip_group_check=True)
                last.then_inc(v_used, 1)

            def new_values(b):
                for h in range(H):
                    g = h % 4
                    last = mm(ps[32 * g:32 * g + HQ, 6, (h // 4) * DV:(h // 4 + 1) * DV], wn[:, h * HQ:(h + 1) * HQ],
                              vn[:, h * DV:(h + 1) * DV], start=False, stop=False, skip_group_check=True)
                last.then_inc(vn_used, 1)

            def outputs(b):
                pe.wait_ge(o_copied, b - LAG + 2)
                for k in range(2):
                    last = mm(ps[:, 3, (k + 1) * 4 * CH:(k + 2) * 4 * CH], osb[:, k * DV:(k + 1) * DV], pick[:, :],
                              start=True, stop=True)
                last.then_inc(o_turned, 1)

            def sequence(b, par, keys=True, vals=True):
                if vals:
                    turn_weights(b, par, 0)
                if keys:
                    turn_page(b, par, 0)
                for u in range(PAGES):
                    if keys and u < PAGES - 1:
                        turn_page(b, par, u + 1)
                    if vals:
                        values(b, u)
                    if keys:
                        scores(b, par, u)
                    if vals and u % 4 == 2:
                        turn_weights(b, par, u // 4 + 1)
                if vals:
                    pe.wait_ge(vn_full, 16 * (b - LAG + 1))
                    pe.wait_ge(wt_copied, (b - LAG + 1) * 5 + 1)
                if keys:
                    new_scores(b, par)
                if vals:
                    new_values(b)
                    outputs(b)

            sequence(0, 0, vals=False)
            sequence(1, 1, vals=False)
            with pe.Fori(0, (DB - LAG) // NBUF) as i:
                for v in range(NBUF):
                    sequence(i * NBUF + (LAG + v), LAG + v)
            sequence(DB, DB, keys=False)
            sequence(DB + 1, DB + 1, keys=False)
            pe.wait_ge(o_ready, DB + 1)
            heads("ohead", ones, 16)
            dense("wo")
            norm(3)
            dense("up1")
            dense("down1")
            pe.wait_ge(x_ready, 4 * KD)
            for i in range(QB + 1):
                s = i % 2
                wait_set("y", s, i // 2)
                for k in range(KD):
                    last = turn(ps[0:NTOK[i], 4 * s + k // 4, (k % 4) * P:(k % 4 + 1) * P],
                                x[:, k, i * P:i * P + NTOK[i]])
                last.then_inc(full[s], 1)

        BIAS = [128, 176, 224, 152, 200]
        NORM = [72, 88, 104, 80, 96]
        APPLY = {"s5": (0, 0, None), "up0": (1, 1, 8), "kv": (2, 2, 16), "q": (2, 3, 24), "up1": (3, 4, 40)}
        ORDER = list(APPLY)
        GATE = {"glu": 0, "down0": 1, "wo": 3, "down1": 4}
        XUP = {"glu": 0, "down0": 8, "wo": 16, "down1": 24}

        def cols(n, part, k, lo, hi):
            return mod[:, n, ds(part * KD + k, 1), lo:hi].rearrange("p a c -> p (a c)")

        def by_token(v):
            return v.unsqueeze(2).to_broadcast([P, DB, DS])

        def sample(t):
            return t[:, SEQ:T].rearrange("p (b t) -> p b t", b=DB)

        def tile(t, k):
            return t[:, ds(k, 1), :].rearrange("p a t -> p (a t)")

        def part(t, k, v):
            return t[:, ds(k, 1), v, :].rearrange("p a t -> p (a t)")

        def chunks_prompt(t):
            return t.rearrange("p (s c) -> p c s", s=CH)[:, DB:NCH, :]

        def chunks_sample(t):
            return t.rearrange("p (s c) -> p c s", s=CH)[:, 0:DB, :]

        def by_halves(t, k):
            return t[:, ds(k, 1), :].rearrange("p k (a b) -> p (k a) b", a=2)

        @block.scalar
        def _(act):
            A = nc.scalar.activation
            step = Steps(act, act_step)

            for r, name in enumerate(("ssm_c_re", "ssm_c_im")):
                for g in range(2):
                    for k in range(4):
                        act.dma_start(craw[:, r, k, g * N:(g + 1) * N],
                                      a[name][0, 16 * k:16 * k + 16].rearrange("(j g) p n -> g j p n", g=2)[g]
                                      ).then_inc(in_b, 16)
            for r, name in enumerate(("ssm_b_re", "ssm_b_im")):
                act.dma_start(bmat[:, r], a[name][0].rearrange("(j g) n p -> (g n) j p", g=2)).then_inc(in_b, 16)
            wait_unit(act, "small", 0)
            act.wait_ge(dt_ready, 1)
            act.wait_ge(cond_ready, 1)
            A(cond[:, :, 0:C9].rearrange("p k c -> p c k"), vec[:, 0:C9 * KD].rearrange("p (c k) -> p c k", c=C9), ACT.Silu
              ).then_inc(cond_ready, 1)
            A(tiny[:, 0], vec[:, 320:352], ACT.Exp).then_inc(sincos_out, 1)
            act.wait_ge(dt_ready, 2)
            A(neglam[:, :], lsum[:, 0:1], ACT.Exp)
            A(lsum[:, 2:3], lsum[:, 1:2], ACT.Exp).then_inc(sincos_out, 1)
            act.wait_ge(sincos_in, 1)
            A(tiny[:, 6], tiny[:, 1], ACT.Exp)
            A(tiny[:, 7], tiny[:, 4], ACT.Sin)
            A(tiny[:, 8], tiny[:, 5], ACT.Sin).then_inc(sincos_out, 1)

            def ada_out(n, first, turns):
                with act.Fori(0, turns) as i:
                    for s in range(2):
                        act.wait_ge(raw_done[3], i * 2 + (SLABS[f"ada{n}"] // 4 + 2 * first + s + 1))
                        A(t2[:, s, 0:BANK], ps[:, 4 * s, :], ACT.Copy).then_inc(rows_ready, 1)
                        wait_unit(act, f"ada{n}.{first}", s, i)
                        A(mod[:, n].rearrange("p m c -> p (m c)")[:, ds(i * (8 * C9) + (2 * first + s) * (4 * C9), 4 * C9)],
                          ps[:, 4 * s + 1, 0:4 * C9], ACT.Copy).then_inc(free[s], 1)

            def root(n):
                wait_unit(act, f"norm{n}", 0)
                A(halves(rstd[:, :]), ps[:, 0:2, 0:HALF], ACT.Sqrt, bias=eps[:, 0:1], scale=1.0 / D).then_inc(free[0], 1)

            def apply(name):
                _, m, h0_ = APPLY[name]
                b0 = KD * ORDER.index(name)
                act.wait_ge(mod_ready, m + 1)
                with act.Fori(0, KD // 2) as i:
                    for s in range(2):
                        k = i * 2 + s
                        act.wait_ge(t1_ready, b0 + s + 1 + i * 2)
                        A(t2[:, s, 0:SEQ], t1[:, s, 0:SEQ], ACT.Identity, bias=cols(m, 0, k, 0, 1),
                          scale=gain[:, m, ds(k, 1), 0:1].rearrange("p a c -> p (a c)")).then_inc(t2_prompt, 1)
                        act.wait_ge(t2_prompt, b0 + s + 1 + i * 2)
                        act.wait_ge(t2_sample, b0 + s + 1 + i * 2)
                        A(part(hr, k, 0), t2[:, s, :], ACT.Copy).then_inc(h_high, 1)

            for i in range(QB + 1):
                s = i % 2
                wait_unit(act, "x", s, i // 2)
                if i + 2 <= QB:
                    act.dma_start(xtok[0:NTOK[i + 2], s, :], dtok[i + 2]).then_inc(in_x[s], 16)
                A(x[:, :, i * P:i * P + NTOK[i]].rearrange("p (b k) t -> p b k t", b=2),
                  ps[:, 4 * s:4 * s + 2, :].rearrange("p b (k t) -> p b k t", t=P)[:, :, :, 0:NTOK[i]], ACT.Copy).then_inc(free[s], 1)
            for s in range(2):
                act.wait_ge(free[s], USES["norm0"][s])
            for k in range(KD):
                if k >= 2:
                    act.wait_ge(square_used, k - 1)
                A(t1[:, k % 2, :], x[:, k, :], ACT.Square).then_inc(square_ready, 1)
            root(0)
            ada_out(0, 0, 3)
            act.wait_ge(mod_ready, 1)
            for k in range(KD):
                s = k % 2
                act.wait_ge(t1_ready, k + 1)
                if k >= 2:
                    act.wait_ge(u_put[s], 16 * (k // 2))
                A(chunks_prompt(t2[:, s, :]), t1[:, s, 0:SEQ].rearrange("p (c s) -> p c s", s=CH), ACT.Identity,
                  bias=mod[:, 0, k, 0:1], scale=gain[:, 0, k, 0:1]).then_inc(t2_prompt, 1)
                act.wait_ge(t2_prompt, k + 1)
                act.wait_ge(t2_sample, k + 1)
                act.dma_start(u_scr[k * P:(k + 1) * P].rearrange("f s c -> f (s c)"), t2[:, s, :]).then_inc(u_put[s], 16)
            for s in range(2):
                act.wait_ge(u_put[s], 16 * (KD // 2))
            for s in range(CH):
                act.dma_start(uch[s * PP:(s + 1) * PP, :, :], u_scr.rearrange("(g p) s c -> s p g c", p=PP)[s]
                              ).then_inc(u_got, 16)
            for u in range(4):
                s = u % 2
                if u == 2:
                    ada_out(1, 0, 1)
                wait_unit(act, f"ssm_k{u // 2}", s)
                if u >= 2:
                    act.wait_ge(k_put[s], 16)
                for t in range(4):
                    done = A(krow[:, s].rearrange("p (j t g) m -> p t g j m", t=4, g=2)[:, t],
                             ps[32 * t:32 * t + PP, 4 * s:4 * s + 2, 0:2 * P].rearrange("p g (j m) -> p g j m", m=P), ACT.Copy)
                done.then_inc(free[s], 1)
                act.wait_ge(free[s], uses(f"ssm_k{u // 2}", s) + 1)
                act.dma_start(k_scr[:, 16 * u:16 * u + 16, :], krow[:, s, :, :]).then_inc(k_put[s], 16)
            ada_out(1, 1, 2)
            for s in range(2):
                act.wait_ge(k_put[s], 16 * 2)
            for u in range(4):
                s = u % 2
                wait_unit(act, "ssm_v", s, u // 2)
                A(vT[:, 8 * u:8 * u + 8].rearrange("p j r m -> p (j r m)"),
                  ps[:, 4 * s:4 * s + 4, :].rearrange("p b c -> p (b c)"), ACT.Copy).then_inc(free[s], 1)
            for u in range(4):
                s = u % 2
                wait_unit(act, "ssm_w", s, u // 2)
                for r in range(2):
                    done = A(drive[:, :, r, 8 * u:8 * u + 8].rearrange("p c (b j) -> p b j c", j=2),
                             ps[:, 4 * s:4 * s + 4, 0:4 * NCH].rearrange("p b (j r c) -> p r b j c", j=2, r=2)[:, r], ACT.Copy)
                done.then_inc(free[s], 1)
            act.wait_ge(kmat_zero, 1)
            for s in range(CH):
                act.dma_start(kmat[s * PP:(s + 1) * PP, :, s * PP:P], k_scr[:, :, 0:P - s * PP]).then_inc(kmat_got, 16)
            ada_out(2, 0, 2)
            ada_out(3, 0, 3)
            for u in range(4):
                s = u % 2
                act.wait_ge(free[s], uses(f"ssm_y{u // 2}", s) + 1)
                for t in range(CH):
                    act.dma_start(y_scr.rearrange("(g p) t c -> t p g c", p=PP)[t, :, 16 * u:16 * u + 16, :],
                                  ysb[t * PP:(t + 1) * PP, s, :].rearrange("p (g c) -> p g c", c=NCH)).then_inc(y_put[s], 16)
                if s:
                    ada_out(4, u // 2, 1)
            wait_unit(act, "ssm_h", 0)
            for r in range(2):
                A(hout[0:J, 3 * r, :], ps[0:J, r, 0:P], ACT.Copy)
                done = A(hout[:, 3 * r + 1:3 * r + 3, :].rearrange("p k m -> p (k m)"), ps[:, r, P:3 * P], ACT.Copy)
            done.then_inc(free[0], 1)
            act.wait_ge(free[0], uses("ssm_h", 0) + 1)
            for r in range(2):
                act.dma_start(out[2 + r][0, 0].rearrange("(j g) n -> j (g n)", g=2), hout[0:J, 3 * r, :]).then_inc(put, 16)
                for k in range(2):
                    act.dma_start(out[4 + r][0, 4 * k:4 * k + 4].rearrange("b (j g) n -> (b j) (g n)", g=2),
                                  hout[:, 3 * r + 1 + k, :]).then_inc(put, 16)
            ada_out(4, 2, 1)
            for s in range(2):
                act.wait_ge(y_put[s], 16 * 2 * CH)

            def split(m, late=0, nk=8):
                slot, w = m % 4, m % 2
                act.wait_ge(raw_full[slot], 16 * ((DENSE0 + m) // 4 + 1) + late * 4)
                A(ws[:, w, 0, 0:nk, :].rearrange("p k n -> p (k n)"), raw[:, slot, 0:nk, :].rearrange("p k n -> p (k n)"),
                  ACT.Copy).then_inc(slab_high, 1)

            def yu_load(k):
                s = k % 2
                act.dma_start(yin[:, s].rearrange("p s c -> p (s c)"), y_scr[k * P:(k + 1) * P].rearrange("f s c -> f (s c)")
                              ).then_inc(y_got[s], 16)
                act.dma_start(uin[:, s].rearrange("p s c -> p (s c)"), u_scr[k * P:(k + 1) * P].rearrange("f s c -> f (s c)")
                              ).then_inc(y_got[s], 16)

            yu_load(0)
            yu_load(1)
            split(0)
            split(1)
            for k in range(KD):
                s = k % 2
                act.wait_ge(yu_ready, k + 1)
                if k >= 2:
                    act.wait_ge(h_ready, k - 1)
                if k + 2 < KD:
                    yu_load(k + 2)
                A(t2[:, s, 0:SEQ].rearrange("p (c s) -> p c s", s=CH), chunks_prompt(t1[:, s, :]), ACT.Gelu_apprx_tanh)
                step(A(t2[:, s, SEQ:T].rearrange("p (c s) -> p c s", s=CH), chunks_sample(t1[:, s, :]), ACT.Gelu_apprx_tanh))
                A(hr[:, k, 0, :], t2[:, s, :], ACT.Copy).then_inc(h_high, 1)

            def dense(name, tail=True):
                units, slabs, per = DENSE[name]
                S, n0 = len(slabs), SLABS[name] - DENSE0

                def turn(i, last):
                    for u in range(per):
                        s = u % 2
                        for j in range(S):
                            n = u * S + j
                            if j == S - 1:
                                wait_unit(act, name, s, i * (per // 2) + u // 2)
                            else:
                                act.wait_ge(slab_read, INNER[name] + u * (S - 1) + j + 1 + i * (per * (S - 1)))
                            if not (last and n + 2 >= per * S):
                                split(n0 + n + 2, i * (per * S), slabs[(j + 2) % S][2] if S == 4 and j < 2 else 8)
                        at = i * (per // 2) + u // 2
                        if name == "glu":
                            A(halves(t1[:, s, :]), ps[:, 4 * s + 2:4 * s + 4, 0:HALF], ACT.Sigmoid).then_inc(e_ready, 1)
                        elif name.startswith("up"):
                            f = i * 2 + u
                            A(halves(t1[:, s, :]), ps[:, 4 * s:4 * s + 2, 0:HALF], ACT.Silu).then_inc(e_ready, 1)
                            act.wait_ge(free[s], uses(name, s, at) + 1)
                            A(part(gr, f, 0), t2[:, s, :], ACT.Copy).then_inc(g_high, 1)
                        elif name in ("kv", "q"):
                            A(by_halves(kvT if name == "kv" else qT, i * per + u), ps[:, 4 * s:4 * s + 2, 0:HALF], ACT.Copy).then_inc(free[s], 1)

                if tail:
                    with act.Fori(0, units // per) as i:
                        turn(i, False)
                else:
                    with act.Fori(0, units // per - 1) as i:
                        turn(i, False)
                    turn(units // per - 1, True)

            dense("glu")
            root(1)
            apply("up0")
            dense("up0")
            dense("down0")
            root(2)
            apply("kv")
            dense("kv")
            apply("q")
            dense("q", tail=False)

            def heads(name, src, n0):
                with act.Fori(0, H // 2) as i:
                    for s in range(2):
                        A(t1[:, s, :], tile(src, i * 2 + s), ACT.Square).then_inc(sq_head, 1)
                    for s in range(2):
                        wait_unit(act, name, s, i)
                        act.wait_ge(head_ready, n0 + i * 2)
                        A(halves(t2[:, s, :]), ps[:, 4 * s:4 * s + 2, 0:HALF], ACT.Sqrt, bias=eps[:, 0:1],
                          scale=1.0 / (DV if name == "ohead" else DK)).then_inc(free[s], 1)

            for s in range(2):
                act.wait_ge(free[s], USES["khead"][s])
            heads("khead", kT, 0)
            heads("qhead", qT, 8)
            for n, name in enumerate(("ktok", "vtok")):
                for i in range(QB + 1):
                    s = i % 2
                    wait_unit(act, name, s, i // 2)
                    if name == "vtok" and i < QB:
                        dst = vtok[:, i].rearrange("p h d -> p (h d)")
                    else:
                        dst = tok[0:NTOK[i], s, :]
                        if n or i >= 2:
                            act.wait_ge(tok_put[s], 16 * (i // 2 if not n else 3 + 2))
                    A(dst, ps[0:NTOK[i], 4 * s:4 * s + 2, :].rearrange("p b c -> p (b c)"), ACT.Copy).then_inc(free[s], 1)
                    act.wait_ge(free[s], uses(name, s, i // 2) + 1)
                    o_ = out[6 + n] if i < QB else out[8 + n]
                    rows_ = (o_[0, i * P:(i + 1) * P] if i < QB else o_)
                    form = {(0, 0): "t h m d -> t (h m d)", (0, 1): "t h d -> t (h d)", (1, 0): "b t h m d -> (b t) (h m d)",
                            (1, 1): "b t h d -> (b t) (h d)"}[(int(i == QB), n)]
                    act.dma_start(rows_.rearrange(form), dst).then_inc(tok_put[s], 16)

            with act.Fori(0, H) as h:
                for i in range(QB):
                    w = (i + 1) * P
                    act.wait_ge(s_max, h * QB + i + 1)
                    for m in range(2):
                        done = A(e01[:, m, 0:w], ps[:, m, 0:w], ACT.Exp, bias=l01[:, 2 + m:3 + m], scale=SCALE,
                                 accum_out=l01[:, 4 + m:5 + m])
                    done.then_inc(free[0], 1)
                wait_unit(act, "attn", 0, h * (QB + 1) + QB)
                A(oT[:, ds(h, 1), 0:SEQ].rearrange("p a t -> p (a t)"), ps[:, 0, :], ACT.Copy).then_inc(free[0], 1)

            def page(b, par, u):
                for half in range(2):
                    at = b * PAGES + u
                    act.wait_ge(k_turned, at * 2 + half + 1)
                    if half == 0 and (not isinstance(at, int) or at > 1):
                        act.wait_ge(scored, at - 1)
                    A(kTs[:, u % 2, half], ps[:, ((par * PAGES + u) * 2 + half) % 3, :], ACT.Copy).then_inc(kt_ready, 1)

            def weights(b, par):
                act.wait_ge(m_ready, b)
                q = sc[:, (par - 1) % NBUF]
                A(q, q, ACT.Exp, bias=mq[:, 1, 0:1], scale=SCALE, accum_out=mq[:, 1, 1:2]).then_inc(e_full, 1)

            def sequence(b, par, keys=True, soft=True):
                for u in range(PAGES):
                    if keys:
                        page(b, par, u)
                    if soft and u == 1:
                        weights(b, par)

            sequence(0, 0, soft=False)
            sequence(1, 1)
            with act.Fori(0, (DB - LAG) // NBUF) as i:
                for v in range(NBUF):
                    sequence(i * NBUF + (LAG + v), LAG + v)
            sequence(DB, DB, keys=False)

            act.wait_ge(o_ready, DB + 1)
            heads("ohead", oT, 16)
            split(SLABS["wo"] - DENSE0)
            split(SLABS["wo"] - DENSE0 + 1)
            act.wait_ge(head_ready, 3 * H)
            with act.Fori(0, H) as i:
                A(part(hr, i, 0), tile(oT, i), ACT.Copy).then_inc(h_high, 1)
            dense("wo")
            root(3)
            apply("up1")
            dense("up1")
            dense("down1", tail=False)
            for i in range(QB + 1):
                s = i % 2
                wait_unit(act, "y", s, i // 2)
                if i >= 2:
                    act.wait_ge(tok_put[s], 16 * ((6, 4)[s] + i // 2))
                A(tok[0:NTOK[i], s, :], ps[0:NTOK[i], 4 * s:4 * s + 2, :].rearrange("p b c -> p (b c)"), ACT.Copy
                  ).then_inc(free[s], 1)
                act.wait_ge(free[s], uses("y", s, i // 2) + 1)
                act.dma_start(out[0][0, i * P:(i + 1) * P] if i < QB else out[1].rearrange("b t d -> (b t) d"),
                              tok[0:NTOK[i], s, :]).then_inc(tok_put[s], 16)

        @block.gpsimd
        def _(pool):
            TT = nc.gpsimd.tensor_tensor
            step = Steps(pool, pool_step)

            nc.gpsimd.memset(ones[:, :], 1.0).then_inc(consts, 1)
            step(nc.gpsimd.memset(ident[:, :], 0.0))
            nc.gpsimd.affine_select(out=ident[:, :], in_=ident[:, :], compare_op=ALU.not_equal, fill=1.0, base=0,
                                    pattern=[[-1, P]], channel_multiplier=1).then_inc(consts, 1)
            nc.gpsimd.memset(eps[:, :], EPS).then_inc(consts, 1)
            pool.wait_ge(consts, 3)
            quarter = ident[:, :].rearrange("p (g c) -> p g c", c=32)[:, :, 0:C9]
            step(TT(add4[:, :], quarter[:, 0], quarter[:, 1], ALU.add))
            for g in (2, 3):
                step(TT(add4[:, :], add4[:, :], quarter[:, g], ALU.add))
            nc.gpsimd.memset(cond[:, :, :].rearrange("p k c -> p (k c)"), 0.0).then_inc(cond_ready, 1)

            def squares(n):
                pool.wait_ge(x_ready, KD * (n - 1) + 1)
                for h in range(2):
                    q = slice(h * HALF, (h + 1) * HALF)
                    done = TT(sqs[:, q], x[:, 0, q], x[:, 0, q], ALU.mult)
                step(done)
                with step.loop(1, KD - 1, 4) as k:
                    pool.wait_ge(x_ready, KD * (n - 1) + 1 + k)
                    for h in range(2):
                        q = slice(h * HALF, (h + 1) * HALF)
                        step(TT(sqt[:, :], tile(x, k)[:, q], tile(x, k)[:, q], ALU.mult))
                        step(TT(sqs[:, q], sqs[:, q], sqt[:, :], ALU.add))
                nc.gpsimd.memset(mark[:, n:n + 1], 0.0).then_inc(sq_ready, 1)

            def cmul_pool(o_re, o_im, a_re, a_im, b_re, b_im, u, v):
                TT(u, a_re, b_re, ALU.mult)
                step(TT(v, a_im, b_im, ALU.mult))
                step(TT(o_re, u, v, ALU.subtract))
                TT(u, a_re, b_im, ALU.mult)
                step(TT(v, a_im, b_re, ALU.mult))
                step(TT(o_im, u, v, ALU.add))

            pool.wait_ge(bbar_ready, 1)
            u_, v_ = (t[:, :].rearrange("p (j q) -> p j q", q=PP) for t in (pA, pB))
            for s in range(CH // 2):
                p_ = [pw[:, CH - 1 - s, r].unsqueeze(2).to_broadcast([P, J, PP]) for r in range(2)]
                cmul_pool(vmat[:, 0, :, s, :], vmat[:, 1, :, s, :], p_[0], p_[1], bbar[:, 0], bbar[:, 1], u_, v_)
            nc.gpsimd.memset(mark[:, 4:5], 0.0).then_inc(v_ready, 1)

            def modulation(n):
                c = COUNT[f"ada{n}"]
                for s in range(2):
                    pool.wait_ge(free[s], ADA_END[n][s])
                step(TT(mod[:, n, 0:c], mod[:, n, 0:c], vec[:, BIAS[n]:BIAS[n] + c].unsqueeze(2).to_broadcast([P, c, C9]), ALU.add))
                g = vec[:, NORM[n]:NORM[n] + KD].unsqueeze(2).to_broadcast([P, KD, C9])
                step(TT(gain[:, n], mod[:, n, KD:2 * KD], g, ALU.mult))
                TT(gain[:, n], gain[:, n], g, ALU.add).then_inc(mod_ready, 1)
                pool.wait_ge(mod_ready, n + 1)

            def sample_part(s, m, k, b0, at, dst):
                pool.wait_ge(t1_ready, at)
                g = by_token(gain[:, m, ds(k, 1), 1:C9].rearrange("p a c -> p (a c)"))
                sh = by_token(cols(m, 0, k, 1, C9))
                step(TT(sample(t1[:, s, :]), sample(t1[:, s, :]), g, ALU.mult))
                TT(dst, sample(t1[:, s, :]), sh, ALU.add).then_inc(t2_sample, 1)

            def apply(name):
                _, m, _h = APPLY[name]
                b0 = KD * ORDER.index(name)
                with step.loop(0, KD // 2, 2) as i:
                    for s in range(2):
                        sample_part(s, m, i * 2 + s, b0, b0 + s + 1 + i * 2, sample(t2[:, s, :]))

            modulation(0)
            for k in range(KD):
                if k >= 2:
                    pool.wait_ge(u_put[k % 2], 16 * (k // 2))
                sample_part(k % 2, 0, k, 0, k + 1, chunks_sample(t2[:, k % 2, :]))
            for s in range(2):
                wait_unit(pool, "ssm_w", s, 1)
            nc.gpsimd.memset(vk[:, :], 0.0).then_inc(kmat_zero, 1)
            modulation(1)
            modulation(2)
            modulation(3)
            modulation(4)
            squares(1)
            apply("up0")
            squares(2)
            apply("kv")
            step(nc.gpsimd.memset(blockd[:, :], 0.0))
            for m in range(2):
                nc.gpsimd.memset(blockd[m * DK:(m + 1) * DK, m * DK:(m + 1) * DK], 1.0)
            step(nc.gpsimd.memset(causal[:, :], 0.0))
            masks = causal[:, :].rearrange("k (r t) -> k r t", t=CH)
            nc.gpsimd.affine_select(out=masks, in_=masks, compare_op=ALU.is_ge, fill=MASKED, base=0,
                                    pattern=[[0, P // CH], [1, CH]], channel_multiplier=-1).then_inc(blocks_ready, 1)
            apply("q")
            pool.wait_ge(head_ready, 2 * H)
            step(nc.gpsimd.memset(tri[:, :], 0.0))
            step(nc.gpsimd.affine_select(out=tri[:, :], in_=tri[:, :], compare_op=ALU.is_ge, fill=MASKED, base=0,
                                         pattern=[[-1, P]], channel_multiplier=1))
            for s in range(2):
                pool.wait_ge(free[s], USES["attn"][s])
            with pool.Fori(0, H) as h:
                pool.wait_ge(free[0], USES["attn"][0] + h * (QB + 1))
                nc.gpsimd.tensor_copy(qh[:, :], tile(qT, h)[:, 0:SEQ])
                nc.gpsimd.tensor_copy(kh[:, :], tile(kT, h)[:, 0:SEQ])
                nc.gpsimd.tensor_copy(vh[:, :, :], vtok[:, :, ds(h, 1), :].rearrange("p k a d -> p k (a d)")).then_inc(head_in, 1)
            for s in range(2):
                pool.wait_ge(free[s], USES["ohead"][s])
                pool.wait_ge(tok_put[s], 16 * (6, 4)[s])
            nc.gpsimd.memset(mark[:, 9:10], 0.0).then_inc(v_used, 4)
            step(nc.gpsimd.memset(qn[:, :].rearrange("p b h c -> p (b h c)"), 0.0))
            quarter = ident[:, :].rearrange("p (g c) -> p g c", c=32)
            TT(pick[:, :].rearrange("p (g t) -> p g t", t=CH), quarter[:, :, 0:CH], quarter[:, :, CH:2 * CH], ALU.add)
            TT(sign[:, 1:2], ones[:, 0:1], neglam[:, :], ALU.subtract).then_inc(sinit, 1)

            def new_keys(b, buf):
                for m in range(2):
                    q = slice(m * DK, (m + 1) * DK)
                    for o in range(2):
                        at = o * HQ + m * CH
                        step(nc.gpsimd.tensor_copy(qn[q, buf, o::2, at:at + CH], qT[q, o::2, ds(b * CH + SEQ, CH)]))
                nc.gpsimd.tensor_copy(kn[:, buf], kT[:, :, ds(b * CH + SEQ, CH)]).then_inc(kn_ready, 1)

            def new_values(b):
                if not isinstance(b, int) or b > 0:
                    pool.wait_ge(vn_used, b)
                pool.dma_start(vn[:, :], out[9][ds(b, 1)].rearrange("b t h d -> t (b h d)")).then_inc(vn_full, 16)

            for b in range(NBUF):
                new_keys(b, b)
            new_values(0)
            for b in range(NBUF, DB):
                new_values(b - LAG)
                pool.wait_ge(new_scored, b - NBUF + 1)
                new_keys(b, b % NBUF)
            for b in range(DB - LAG, DB):
                new_values(b)
            squares(3)
            apply("up1")

        @block.vector
        def _(dve):
            TT, TS, STT = nc.vector.tensor_tensor, nc.vector.tensor_scalar, nc.vector.scalar_tensor_tensor
            CP, RED, REC = nc.vector.tensor_copy, nc.vector.tensor_reduce, nc.vector.reciprocal
            step = Steps(dve, dve_step)

            dve.wait_ge(in_small, 16 * SMALL)
            CP(v3[64:96, :].rearrange("p (g n) -> p g n", g=2), lst[64:96, :].unsqueeze(2).to_broadcast([32, 2, N])
               ).then_inc(v3_built, 1)
            for k in range(2):
                step(TT(ltmp[:, k, :], lrow[:, 2 * k, :], lrow[:, 2 * k + 1, :], ALU.mult))
            RED(lsum[:, 0:2], ltmp[:, :, :], AX_X, ALU.add)
            wait_unit(dve, "small", 0)
            CP(vec[:, 0:123], ps[:, 0, 0:123])
            CP(vec[:, P:P + 112], ps[:, 0, P:P + 112])
            CP(vec[:, 2 * P:2 * P + 96], ps[:, 0, 2 * P:2 * P + 96]).then_inc(dt_ready, 1)
            CP(h0[:, :, :].rearrange("p r b -> p (r b)"), ps[:, 1, :]).then_inc(dt_ready, 1)
            CP(cT[:, :, :, :].rearrange("p r j q -> p r (j q)"), ps[:, 2:4, :]).then_inc(free[0], 1)
            lr, li = vec[:, 256:288], vec[:, 288:320]
            T_ = lambda n: tiny[:, n, :]
            dve.wait_ge(sincos_out, 1)
            TT(T_(1), lr, T_(0), ALU.mult)
            step(TT(T_(2), li, T_(0), ALU.mult))
            step(TS(T_(3), T_(2), 1 / (2 * math.pi), ROUND, ALU.mult, ALU.add))
            step(TS(T_(3), T_(3), -ROUND, None, ALU.add))
            step(STT(T_(4), T_(3), -TWO_PI_PARTS[0], T_(2), ALU.mult, ALU.add))
            step(STT(T_(4), T_(3), -TWO_PI_PARTS[1], T_(4), ALU.mult, ALU.add))
            step(STT(T_(4), T_(3), -TWO_PI_PARTS[2], T_(4), ALU.mult, ALU.add))
            step(TS(T_(4), T_(4), PI_BELOW, -PI_BELOW, ALU.min, ALU.max))
            step(STT(T_(5), T_(4), -1.0, T_(4), ALU.mult, ALU.max))
            TS(T_(5), T_(5), -1.0, math.pi / 2, ALU.mult, ALU.add).then_inc(sincos_in, 1)
            dve.wait_ge(sincos_out, 2)
            step(TT(neglam[:, :], lsum[:, 2:3], neglam[:, :], ALU.subtract))
            step(TS(neglam[:, :], neglam[:, :], -LAM_INIT, None, ALU.add))
            TS(gaino[:, :], vec[:, 122:123], 1.0 - LAM_INIT, None, ALU.mult)
            dve.wait_ge(sincos_out, 3)
            nc.vector.memset(pw[:, 0, 0, :], 1.0)
            nc.vector.memset(pw[:, 0, 1, :], 0.0)
            TT(pw[:, 1, 0, :], T_(6), T_(8), ALU.mult)
            step(TT(pw[:, 1, 1, :], T_(6), T_(7), ALU.mult))

            def cmul(o_re, o_im, a_re, a_im, b_re, b_im, u, v):
                TT(u, a_re, b_re, ALU.mult)
                step(TT(v, a_im, b_im, ALU.mult))
                step(TT(o_re, u, v, ALU.subtract))
                TT(u, a_re, b_im, ALU.mult)
                step(TT(v, a_im, b_re, ALU.mult))
                step(TT(o_im, u, v, ALU.add))

            for k in (1, 2, 4):
                u, v = (t[:, 0:k * J].rearrange("p (k j) -> p k j", j=J) for t in (tA, tB))
                a_ = [pw[:, k, r].unsqueeze(1).to_broadcast([P, k, J]) for r in range(2)]
                cmul(pw[:, k + 1:2 * k + 1, 0], pw[:, k + 1:2 * k + 1, 1], a_[0], a_[1], pw[:, 1:k + 1, 0], pw[:, 1:k + 1, 1], u, v)
            TS(pws[:, 1], pw[:, CH, 1], -1.0, None, ALU.mult)
            step(CP(pws[:, 0], pw[:, CH, 1]))
            ni = pw[:, 1, 1, :]
            TS(T_(9), pw[:, 1, 0, :], -1.0, None, ALU.add)
            TT(T_(10), lr, lr, ALU.mult)
            step(TT(T_(11), li, li, ALU.mult))
            step(TT(T_(10), T_(10), T_(11), ALU.add))
            step(REC(T_(10), T_(10)))
            TT(T_(11), T_(9), lr, ALU.mult)
            step(TT(T_(12), ni, li, ALU.mult))
            step(TT(T_(11), T_(11), T_(12), ALU.add))
            step(TT(T_(11), T_(11), T_(10), ALU.mult))
            TT(T_(12), ni, lr, ALU.mult)
            step(TT(T_(13), T_(9), li, ALU.mult))
            step(TT(T_(12), T_(12), T_(13), ALU.subtract))
            step(TT(T_(12), T_(12), T_(10), ALU.mult))
            dve.wait_ge(in_b, 16 * 18)
            u, v = (t[:, :].rearrange("p (j q) -> p j q", q=PP) for t in (tA, tB))
            f = [T_(11 + r).unsqueeze(2).to_broadcast([P, J, PP]) for r in range(2)]
            cmul(bbar[:, 0], bbar[:, 1], f[0], f[1], bmat[:, 0], bmat[:, 1], u, v)
            nc.vector.memset(mark[:, 5:6], 0.0).then_inc(bbar_ready, 1)
            with step.loop(0, TAU, 4) as t:
                p_ = [pw[:, ds(t, 1), r].rearrange("p a j -> p (a j)").unsqueeze(2).to_broadcast([P, J, PP]) for r in range(2)]
                o_ = [cpow[:, :, r, ds(t, 1), :].rearrange("p j a q -> p j (a q)") for r in range(2)]
                TT(u, p_[0], cT[:, 0], ALU.mult)
                step(TT(v, p_[1], cT[:, 1], ALU.mult))
                step(TT(o_[0], u, v, ALU.subtract))
                TT(u, p_[0], cT[:, 1], ALU.mult)
                step(TT(v, p_[1], cT[:, 0], ALU.mult))
                step(STT(o_[1], u, -1.0, v, ALU.mult, ALU.subtract))
            nc.vector.memset(mark[:, 6:7], 0.0).then_inc(cpow_ready, 1)

            def root(n):
                dve.wait_ge(free[0], USES[f"norm{n}"][0] + 1)
                step(REC(rstd[:, :], rstd[:, :]))

            root(0)
            for k in range(KD):
                if k >= 2:
                    dve.wait_ge(t2_prompt, k - 1)
                    dve.wait_ge(t2_sample, k - 1)
                TT(t1[:, k % 2, :], x[:, k, :], rstd[:, :], ALU.mult).then_inc(t1_ready, 1)
            u, v = (t[:, :].rearrange("p (j q) -> p j q", q=PP) for t in (tA, tB))
            for s in range(CH // 2, CH):
                p_ = [pw[:, CH - 1 - s, r].unsqueeze(2).to_broadcast([P, J, PP]) for r in range(2)]
                cmul(vmat[:, 0, :, s, :], vmat[:, 1, :, s, :], p_[0], p_[1], bbar[:, 0], bbar[:, 1], u, v)
            nc.vector.memset(mark[:, 0:1], 0.0).then_inc(v_ready, 1)
            for s in range(2):
                dve.wait_ge(free[s], USES["ssm_w"][s])
            for r in range(2):
                CP(hs[:, 0:DB, r, :], h0[:, r, :].rearrange("p (b j) -> p b j", b=DB))
            step(nc.vector.memset(hs[:, DB], 0.0))
            for s in range(2):
                dve.wait_ge(free[s], USES["ada2.0"][s])
            u, v = (t[:, 0:2 * J].rearrange("p (r j) -> p r j", r=2) for t in (tA, tB))
            a8 = pw[:, CH, 0, :].unsqueeze(1).to_broadcast([P, 2, J])
            UN = 4
            with step.loop(0, PCH // UN, 3 * UN) as i:
                for k in range(UN):
                    c = DB + k + i * UN
                    h_ = hs[:, ds(c, 1)].rearrange("p a r j -> p (a r) j")
                    TT(u, h_, a8, ALU.mult)
                    step(TT(v[:, ::-1, :], h_, pws[:, :, :], ALU.mult))
                    step(TT(u, u, v, ALU.add))
                    step(TT(hs[:, ds(c + 1, 1)].rearrange("p a r j -> p (a r) j"), u,
                            drive[:, ds(c, 1)].rearrange("p a r j -> p (a r) j"), ALU.add))
            nc.vector.memset(mark[:, 7:8], 0.0).then_inc(hs_ready, 1)
            u, v = (t[:, :].rearrange("p (b r j) -> p b r j", b=DB, r=2) for t in (tA, tB))
            step(TT(u, hs[:, 0:DB], pw[:, CH, 0, :].unsqueeze(1).unsqueeze(1).to_broadcast([P, DB, 2, J]), ALU.mult))
            step(TT(v[:, :, ::-1, :], hs[:, 0:DB], pws[:, :, :].unsqueeze(1).to_broadcast([P, DB, 2, J]), ALU.mult))
            step(TT(u, u, v, ALU.add))
            TT(hfin[:, :].rearrange("p r b j -> p b r j"), u, drive[:, 0:DB], ALU.add).then_inc(hfin_ready, 1)
            for n in range(4):
                s = n % 2
                wait_unit(dve, f"ssm_y{n // 2}", s)
                if n >= 2:
                    dve.wait_ge(y_put[s], 16 * CH)
                for g in range(2):
                    done = CP(ysb[:, s, :].rearrange("p (j g c) -> p g j c", g=2, c=NCH)[:, g].rearrange("p (b j) c -> p b j c", b=2),
                              ps[:, 4 * s + 2 * g:4 * s + 2 * g + 2, 0:4 * NCH].rearrange("p b (j c) -> p b j c", c=NCH))
                done.then_inc(free[s], 1)

            def split(m, late=0, nk=8):
                slot, w = m % 4, m % 2
                dve.wait_ge(slab_high, m + 1 + late)
                f = lambda t: t.rearrange("p k n -> p (k n)")
                TT(f(ws[:, w, 1, 0:nk, :]), f(raw[:, slot, 0:nk, :]), f(ws[:, w, 0, 0:nk, :]).bitcast(F32), ALU.subtract
                   ).then_inc(raw_done[slot], 1)

            def low(k, s, n):
                dve.wait_ge(h_high, n)
                TT(part(hr, k, 1), t2[:, s, :], part(hr, k, 0).bitcast(F32), ALU.subtract).then_inc(h_ready, 1)

            split(0)
            split(1)
            for k in range(KD + 1):
                if k < KD:
                    s = k % 2
                    dve.wait_ge(y_got[s], 32 * (k // 2 + 1))
                    f = lambda t: t[:, s].rearrange("p s c -> p (s c)")
                    if k >= 2:
                        dve.wait_ge(h_high, k - 1)
                    STT(t1[:, s, :], f(uin), vec[:, 112 + k:113 + k], f(yin), ALU.mult, ALU.add).then_inc(yu_ready, 1)
                if k:
                    low(k - 1, (k - 1) % 2, k)

            def apply(name):
                _, m, hb = APPLY[name]
                with dve.Fori(0, KD // 2) as i:
                    for s in range(2):
                        TT(t1[:, s, :], tile(x, i * 2 + s), rstd[:, :], ALU.mult).then_inc(t1_ready, 1)
                    for s in range(2):
                        low(i * 2 + s, s, hb + s + 1 + i * 2)

            def dense(name, tail=True):
                units, slabs, per = DENSE[name]
                S, n0 = len(slabs), SLABS[name] - DENSE0
                steps_ = per * {"glu": 1}.get(name, 0)

                def turn(i, last):
                    for u in range(per):
                        s = u % 2
                        at = i * (per // 2) + u // 2
                        k = i * per + u
                        for j in range(S):
                            n = u * S + j
                            if not (last and n + 2 >= per * S):
                                split(n0 + n + 2, i * (per * S), slabs[(j + 2) % S][2] if S == 4 and j < 2 else 8)
                        if name in ("kv", "q"):
                            continue
                        wait_unit(dve, name, s, at)
                        if name.startswith("up"):
                            at_e = (KD if name == "up0" else KD + FT) + k + 1
                            dve.wait_ge(e_ready, at_e)
                            TT(halves(t2[:, s, :]), ps[:, 4 * s + 2:4 * s + 4, 0:HALF], halves(t1[:, s, :]), ALU.mult
                               ).then_inc(free[s], 1)
                            dve.wait_ge(free[s], uses(name, s, at) + 1)
                            dve.wait_ge(g_high, (0 if name == "up0" else FT) + k + 1)
                            TT(part(gr, k, 1), t2[:, s, :], part(gr, k, 0).bitcast(F32), ALU.subtract).then_inc(g_ready, 1)
                            continue
                        gate = GATE[name]
                        g, gs = cols(gate, 2, k, 0, 1), by_token(cols(gate, 2, k, 1, C9))
                        xk = tile(x, k)
                        if name == "glu":
                            dve.wait_ge(e_ready, k + 1)
                            TT(halves(t2[:, s, :]), ps[:, 4 * s:4 * s + 2, 0:HALF], halves(t1[:, s, :]), ALU.mult
                               ).then_inc(free[s], 1)
                            dve.wait_ge(free[s], uses(name, s, at) + 1)
                            STT(xk[:, 0:SEQ], t2[:, s, 0:SEQ], g, xk[:, 0:SEQ], ALU.mult, ALU.add)
                            step(TT(sample(t2[:, s, :]), sample(t2[:, s, :]), gs, ALU.mult))
                        else:
                            STT(xk[:, 0:HALF], ps[:, 4 * s, 0:HALF], g, xk[:, 0:HALF], ALU.mult, ALU.add)
                            STT(xk[:, HALF:SEQ], ps[:, 4 * s + 1, 0:SEQ - HALF], g, xk[:, HALF:SEQ], ALU.mult, ALU.add)
                            TT(sample(t2[:, s, :]), ps[:, 4 * s + 1, SEQ - HALF:HALF].rearrange("p (b t) -> p b t", b=DB), gs,
                               ALU.mult).then_inc(free[s], 1)
                            dve.wait_ge(free[s], uses(name, s, at) + 1)
                        TT(xk[:, SEQ:T], xk[:, SEQ:T], t2[:, s, SEQ:T], ALU.add).then_inc(x_ready, 1)

                full_turns = units // per - (0 if tail else 1)
                with step.loop(0, full_turns, steps_) as i:
                    turn(i, False)
                if not tail:
                    turn(units // per - 1, True)

            dense("glu")
            root(1)
            apply("up0")
            dense("up0")
            dense("down0")
            root(2)
            apply("kv")
            dense("kv")
            apply("q")
            dense("q", tail=False)

            def heads(name, src, g, n0):
                with step.loop(0, H // 2, 2) as i:
                    for s in range(2):
                        dve.wait_ge(free[s], uses(name, s, i) + 1)
                        step(REC(t2[:, s, :], t2[:, s, :]))
                        t = tile(src, i * 2 + s)
                        STT(t, t, g, t2[:, s, :], ALU.mult, ALU.mult).then_inc(head_ready, 1)

            heads("khead", kT, vec[:, 120:121], 0)
            heads("qhead", qT, vec[:, 121:122], 8)
            with step.loop(0, H, QB * 5) as h:
                for i in range(QB):
                    w = (i + 1) * P
                    wait_unit(dve, "attn", 0, h * (QB + 1) + i)
                    if i == 0:
                        dve.wait_ge(head_in, h + 1)
                    step(TT(ps[:, 0:2, i * P:w], ps[:, 0:2, i * P:w], tri[:, :].unsqueeze(1).to_broadcast([P, 2, P]), ALU.add))
                    step(RED(l01[:, 0:2], ps[:, 0:2, 0:w], AX_X, ALU.max))
                    TS(l01[:, 2:4], l01[:, 0:2], -SCALE, None, ALU.mult).then_inc(s_max, 1)
                    dve.wait_ge(free[0], uses("attn", 0, h * (QB + 1) + i) + 1)
                    step(REC(l01[:, 6:8], l01[:, 4:6]))
                    step(TT(l01[:, 7:8], l01[:, 7:8], neglam[:, :], ALU.mult))
                    step(TS(e01[:, 1, 0:w], e01[:, 1, 0:w], l01[:, 7:8], None, ALU.mult))
                    STT(e01[:, 0, 0:w], e01[:, 0, 0:w], l01[:, 6:7], e01[:, 1, 0:w], ALU.mult, ALU.add).then_inc(w_done, 1)
                    wait_unit(dve, "attn", 1, h * QB + i)
                    CP(wtT[:, 0:i + 1, i * P:w], ps[:, 4, 0:w].rearrange("p (k q) -> p k q", q=P)).then_inc(free[1], 1)

            dve.wait_ge(sinit, 1)
            first_map = ident[:, :].rearrange("p (r m t) -> p r m t", m=2, t=CH)[:, :, 0, :]
            step(RED(sign[:, 0:1], first_map, mybir.AxisListType.XY, ALU.add))
            step(TT(sign[:, 0:1], sign[:, 0:1], sign[:, 1:2], ALU.mult))
            step(TT(sign[:, 0:1], sign[:, 0:1], neglam[:, :], ALU.add))
            for s in range(2):
                dve.wait_ge(free[s], USES["ohead"][s])
            nc.vector.memset(ps[:, 6, 0:2 * DV], 0.0).then_inc(o_copied, 1)
            nc.vector.memset(mark[:, 10:11], 0.0).then_inc(wt_copied, 1)
            nc.vector.memset(mark[:, 11:12], 0.0).then_inc(o_ready, 1)

            def scores(b, par, q):
                dst = sc[:, par % NBUF, q * BANK:(q + 1) * BANK]
                dve.wait_ge(scored, b * PAGES + 4 * q + 4)
                CP(dst, ps[:, 4 + q % 2, :]).then_inc(s_copied, 1)
                dve.wait_ge(s_copied, b * 4 + q + 1)
                RED(mq[:, 0, q:q + 1], dst, AX_X, ALU.max)

            def new_scores(b, par):
                dst = sc[:, par % NBUF, PAGES * P:]
                dve.wait_ge(new_scored, b + 1)
                step(CP(dst, ps[:, 3, 0:CH]))
                step(RED(mq[:, 0, 4:5], dst, AX_X, ALU.max))
                step(RED(mq[:, 0, 5:6], mq[:, 0, 0:5], AX_X, ALU.max))

            def bias(b):
                if not isinstance(b, int) or b > 0:
                    dve.wait_ge(e_full, b)
                TS(mq[:, 1, 0:1], mq[:, 0, 5:6], -SCALE, None, ALU.mult).then_inc(m_ready, 1)

            def normalize(b, par):
                dve.wait_ge(e_full, b)
                step(REC(mq[:, 1, 2:3], mq[:, 1, 1:2]))
                step(TT(mq[:, 1, 3:4], mq[:, 1, 2:3], sign[:, 0:1], ALU.mult))
                q = sc[:, (par - 1) % NBUF]
                TS(q, q, mq[:, 1, 3:4], None, ALU.mult).then_inc(w_ready, 1)

            def weights(b, q):
                dve.wait_ge(w_turned, (b - LAG) * 5 + q + 1)
                if q == 4:
                    CP(wn[:, :], ps[0:CH, 7, 0:P]).then_inc(wt_copied, 1)
                    return
                dve.wait_ge(v_used, (b - LAG) * PAGES + 4 * q)
                CP(wT[:, q % 2, :], ps[:, 7, :]).then_inc(wt_copied, 1)

            def outputs(b):
                dve.wait_ge(vn_used, b - LAG + 1)
                CP(osb[:, :], ps[:, 6, 0:2 * DV]).then_inc(o_copied, 1)
                dve.wait_ge(o_turned, b - LAG + 1)
                CP(oT[:, :, ds((b - LAG) * CH + SEQ, CH)], ps[:, 3, 4 * CH:12 * CH].rearrange("p (h t) -> p h t", t=CH)
                   ).then_inc(o_ready, 1)

            def sequence(b, par, keys=True, vals=True, soft=True):
                if vals:
                    weights(b, 0)
                if soft:
                    normalize(b, par)
                for q in range(4):
                    if vals:
                        weights(b, q + 1)
                    if keys:
                        scores(b, par, q)
                if keys:
                    new_scores(b, par)
                    bias(b)
                if vals:
                    outputs(b)

            sequence(0, 0, vals=False, soft=False)
            sequence(1, 1, vals=False)
            with step.loop(0, (DB - LAG) // NBUF, 5 * NBUF) as i:
                for v in range(NBUF):
                    sequence(i * NBUF + (LAG + v), LAG + v)
            sequence(DB, DB, keys=False)
            sequence(DB + 1, DB + 1, keys=False, soft=False)
            heads("ohead", oT, gaino[:, 0:1], 16)
            split(SLABS["wo"] - DENSE0)
            split(SLABS["wo"] - DENSE0 + 1)
            with dve.Fori(0, H) as k:
                dve.wait_ge(h_high, 4 * KD + 1 + k)
                TT(part(hr, k, 1), tile(oT, k), part(hr, k, 0).bitcast(F32), ALU.subtract).then_inc(h_ready, 1)
            dense("wo")
            root(3)
            apply("up1")
            dense("up1")
            dense("down1", tail=False)


INPUTS = ["x_prompt", "x_sample", "state_ssm_re", "state_ssm_im", "cache_k", "cache_v", "page_table", "c_prompt",
          "c_sample", "norm_mix", "w_ada_mix", "b_ada_mix", "norm_ffn", "w_ada_ffn", "b_ada_ffn", "ffn_w13", "ffn_w2",
          "ssm_lam_re", "ssm_lam_im", "ssm_log_step", "ssm_b_re", "ssm_b_im", "ssm_c_re", "ssm_c_im", "ssm_d",
          "ssm_w_glu", "norm_kv", "w_ada_kv", "b_ada_kv", "w_kv", "k_norm", "w_q", "q_norm", "diff_lambda", "subln", "w_o"]


def kernel(**inputs):
    import numpy as np
    import concourse.bacc as bacc
    from concourse.bass_utils import run_bass_kernel_spmd

    nc = bacc.Bacc("TRN2", target_bir_lowering=False, num_devices=1)
    arrays, args = {}, {}
    for name in INPUTS:
        v = np.ascontiguousarray(inputs[name])
        arrays[f"in_{name}"] = v
        args[name] = nc.dram_tensor(f"in_{name}", v.shape, mybir.dt.from_np(v.dtype), kind="ExternalInput").ap()
    xp, xs = inputs["x_prompt"].shape, inputs["x_sample"].shape
    layers, _, groups, states = inputs["state_ssm_re"].shape
    heads, two, dk = inputs["cache_k"].shape[2:]
    dv = inputs["cache_v"].shape[3]
    shapes = [xp, xs] + [(layers, xp[0], groups, states)] * 2 + [(layers, xs[0], groups, states)] * 2 + [
        (*xp[:2], heads, two, dk), (*xp[:2], heads, dv), (*xs[:2], heads, two, dk), (*xs[:2], heads, dv)]
    outs = [nc.dram_tensor(f"out_{i}", s, F32, kind="ExternalOutput").ap() for i, s in enumerate(shapes)]
    yoco_step(nc, args, outs)
    r = run_bass_kernel_spmd(nc, [arrays], core_ids=[0])
    return tuple(r.results[0][f"out_{i}"] for i in range(len(shapes)))
```

```python
from contextlib import ExitStack
import math

import concourse.bass as bass
from concourse import mybir

ALU = mybir.AluOpType
ACT = mybir.ActivationFunctionType
F32 = mybir.dt.float32
F32R = mybir.dt.float32r
I32 = mybir.dt.int32
AX_X = mybir.AxisListType.X
ds = bass.ds

P = 128
BANK = 512
EPS = 1e-6
MASKED = -1.0e30
ROUND = 12582912.0
TWO_PI_PARTS = (6.28125, 0.001934051513671875, 1.2556659146e-06)
PI_BELOW = 3.1415925


class Steps:

    def __init__(self, eng, sem):
        self.eng, self.sem, self.start, self.k = eng, sem, 0, 0

    def __call__(self, ins):
        ins.then_inc(self.sem, 1)
        self.k += 1
        self.eng.wait_ge(self.sem, self.start + self.k)

    def mark(self, ins):
        ins.then_inc(self.sem, 1)
        self.k += 1
        return self.k

    def wait(self, k):
        self.eng.wait_ge(self.sem, self.start + k)

    def loop(self, first, turns, per):
        steps = self

        class Turns:
            def __enter__(self):
                self.base = steps.start + steps.k
                self.fori = steps.eng.Fori(first, first + turns)
                i = self.fori.__enter__()
                steps.start, steps.k = self.base - first * per + i * per, 0
                return i

            def __exit__(self, *e):
                r = self.fori.__exit__(*e)
                assert e[0] is not None or steps.k == per, (steps.k, per)
                steps.start, steps.k = self.base + turns * per, 0
                return r

        return Turns()


def yoco_step(nc, a, out):
    SEQ, D = a["x_prompt"].shape[1:]
    DB, DS = a["x_sample"].shape[:2]
    G, N, PP = a["ssm_b_re"].shape[1:]
    H, DK = a["cache_k"].shape[2], a["cache_k"].shape[4]
    DV = a["cache_v"].shape[3]
    PAGES, NPOOL = a["page_table"].shape[1], a["cache_k"].shape[0]
    DFF = a["ffn_w2"].shape[1]
    T = SEQ + DB * DS
    HALF = T // 2
    KD = D // P
    FT = DFF // P
    CH = DS
    NCH = T // CH
    PCH = SEQ // CH
    J = G // 2
    TAU = CH + 1
    C9 = 1 + DB
    SCALE = DK ** -0.5
    LAM_INIT = 0.8 - 0.6 * math.exp(-0.3 * 1)
    QB = SEQ // P
    LAG = 2
    NBUF = LAG + 1
    HQ = 2 * CH
    assert D == 1024 and 2 * DK == P and DV == P and CH * PP == P and 2 * N == P and H == KD
    assert a["cache_k"].shape[1] == P and PAGES == 16 and SEQ == BANK and (DB - LAG) % NBUF == 0

    PLAN = [("x", 5), ("small", 1), ("ada0.0", 6), ("norm0", 1), ("ssm_k0", 2), ("ada1.0", 2),
            ("ssm_k1", 2), ("ssm_v", 4), ("ssm_w", 4), ("ada1.1", 4), ("ada2.0", 4), ("ada3.0", 6), ("ssm_y0", 2),
            ("ada4.0", 2), ("ssm_y1", 2), ("ada4.1", 2), ("ssm_h", 1), ("ada4.2", 2),
            ("glu", 8), ("norm1", 1), ("up0", 22), ("down0", 8), ("norm2", 1), ("kv", 16), ("q", 8),
            ("qtok", 10), ("attn", 0),
            ("ohead", 8), ("wo", 8), ("norm3", 1), ("up1", 22), ("down1", 8), ("y", 5)]
    USES, seen = {}, [0, 0]
    for name, n in PLAN:
        USES[name] = tuple(seen)
        seen[0] += (n + 1) // 2
        seen[1] += n // 2

    ADA_END = [[USES[f"ada{n}.{p}"][s] + k for s in range(2)] for n, (p, k) in enumerate([(0, 3), (1, 2), (0, 2), (0, 3), (2, 1)])]

    COUNT = {"ada0": 24, "ada1": 24, "ada2": 16, "ada3": 24, "ada4": 24, "glu": 16, "up0": 2 * FT,
             "down0": 4 * KD, "kv": 16, "q": 8, "wo": 8, "up1": 2 * FT, "down1": 4 * KD}
    SLABS, n_slabs = {}, 0
    for name, n in COUNT.items():
        SLABS[name] = n_slabs
        n_slabs += n
        assert n % 4 == 0

    DENSE0 = SLABS["glu"]

    PAIR = [(0, 0, 8), (1, 0, 8)]
    ONE = [(0, 0, 8)]
    LONG = [(0, 0, 6), (0, 6, 6), (0, 12, 6), (0, 18, 4)]
    DENSE = {"glu": (8, PAIR, 2), "up0": (22, PAIR, 2), "down0": (8, LONG, 2), "kv": (16, ONE, 4),
             "q": (8, ONE, 4), "wo": (8, ONE, 4), "up1": (22, PAIR, 2), "down1": (8, LONG, 2)}
    INNER, n_inner = {}, 0
    for name, (units, slabs, _) in DENSE.items():
        INNER[name] = n_inner
        n_inner += units * (len(slabs) - 1)

    base = -(-nc.sbuf_base // 64) * 64
    place = [base]

    def keep(name, shape, dt=F32):
        size = 4 * math.prod(shape[1:])
        t = nc.alloc_sbuf_tensor_at(name, shape, dt, offset=place[0])
        place[0] += -(-size // 32) * 32
        return t

    x = keep("x", [P, KD, T])
    raw = keep("raw", [P, 4, 8, P])
    vec = keep("vec", [P, 3 * P])
    cond = keep("cond", [P, KD, 32])
    add4 = keep("add4", [P, C9])
    mod = keep("mod", [P, 5, 24, C9])
    gain = keep("gain", [P, 5, KD, C9])
    t1 = keep("t1", [P, 2, T])
    t2 = keep("t2", [P, 2, T])
    rstd = keep("rstd", [P, T])
    sqs = rstd
    sqt = keep("sqt", [P, HALF])
    ident = keep("ident", [P, P])
    ones = keep("ones", [P, P])
    eps = keep("eps", [P, 1])
    neglam = keep("neglam", [P, 1])
    gaino = keep("gaino", [P, 1])
    pages = keep("pages", [1, DB * PAGES], I32)
    mark = keep("mark", [P, 17])
    over = place[0]

    def share(name, shape, at, dt=F32):
        return nc.alloc_sbuf_tensor_at(name, shape, dt, offset=over + at)

    KB = 1024
    SMALL = 21
    wh = share("wh", [P, (2 * NCH + 1) * 2 * J], 0)
    drive = wh[:, 0:NCH * 2 * J].rearrange("p (c r j) -> p c r j", c=NCH, r=2)
    hs = wh[:, NCH * 2 * J:].rearrange("p (c r j) -> p c r j", c=NCH + 1, r=2)
    vmat = wh[:, 0:2 * CH * J * PP].rearrange("p (r j s q) -> p r j s q", r=2, j=J, s=CH)
    o = 4 * (2 * NCH + 1) * 2 * J
    vk = share("vk", [P, G * P], o)
    vT = vk[:, :].rearrange("p (j r m) -> p j r m", j=J, r=2)
    kmat = vk[:, :].rearrange("p (g m) -> p g m", g=G)
    krow = share("krow", [PP, 2, 16, P], o)
    o += 4 * G * P
    cpow = share("cpow", [P, J, 2, TAU, PP], o)
    o += 4 * J * 2 * TAU * PP
    uch = share("uch", [P, G, NCH], o)
    craw = share("craw", [P, 2, 4, P], o)
    hraw = share("hraw", [P, 2, 2, P], o + 4 * KB)
    xtok = share("xtok", [P, 2, D], o + 6 * KB)
    v1 = share("v1", [P, P], o + 14 * KB)
    v2 = share("v2", [P, P], o + 14 * KB + 512)
    v3 = share("v3", [P, P], o + 15 * KB)
    lst = share("lst", [96, 2], o + 15 * KB + 512)
    lrow = share("lrow", [P, 4, DK], o + 16 * KB)
    ltmp = share("ltmp", [P, 2, DK], o + 17 * KB)
    lsum = share("lsum", [P, 4], o + 17 * KB + 512)
    o += 4 * G * NCH
    bmat = share("bmat", [P, 2, J, PP], o)
    bbar = share("bbar", [P, 2, J, PP], o + 4 * KB)
    cT = share("cT", [P, 2, J, PP], o + 8 * KB)
    ysb = share("ysb", [P, 2, 16 * NCH], o)
    hout = share("hout", [P, 6, P], o + 9 * KB)
    o += 12 * KB
    pw = share("pw", [P, TAU, 2, J], o)
    pws = share("pws", [P, 2, J], o + 4 * TAU * 2 * J)
    h0 = share("h0", [P, 2, DB * J], o + 3 * KB)
    hfin = share("hfin", [P, 2, DB, J], o + 5 * KB)
    tiny = share("tiny", [P, 14, J], o + 7 * KB)
    tA = share("tA", [P, J * PP], o + 9 * KB)
    tB = share("tB", [P, J * PP], o + 11 * KB)
    pA = share("pA", [P, J * PP], o + 13 * KB)
    pB = share("pB", [P, J * PP], o + 15 * KB)
    o += 17 * KB
    assert over + o <= nc.sbuf_usable_end, over + o
    yin = share("yin", [P, 2, CH, NCH], 120 * KB)
    uin = share("uin", [P, 2, CH, NCH], 125 * KB)
    ws = share("ws", [P, 2, 2, 8, P], 0, F32R)
    hr = share("hr", [P, KD, 2, T], 16 * KB, F32R)
    gr = share("gr", [P, FT, 2, T], 52 * KB, F32R)
    assert over + 52 * KB + 8 * FT * T <= nc.sbuf_usable_end, over + 52 * KB + 8 * FT * T
    kvT = share("kvT", [P, 2 * H, T], 52 * KB)
    kT, vTf = kvT[:, 0:H], kvT[:, H:2 * H]
    qT = share("qT", [P, H, T], 88 * KB)
    oT = vTf
    tok = share("tok", [P, 2, D], 110 * KB)
    vtok = share("vtok", [P, QB, H, DV], 118 * KB)
    e01 = share("e01", [P, 2, 2, SEQ], 134 * KB)
    wtT = share("wtT", [P, QB, SEQ], 142 * KB)
    l01 = share("l01", [P, 2, 8], 151 * KB + 32)
    qh = share("qh", [P, 2, SEQ], 32 * KB)
    kh = share("kh", [P, 2, SEQ], 36 * KB)
    vh = share("vh", [P, 2, QB, DV], 40 * KB)
    tri = share("tri", [P, P], 44 * KB)
    kpg = share("kpg", [P, 4, H, P], 0)
    vpg = share("vpg", [P, 4, H, DV], 16 * KB)
    kTs = share("kTs", [P, 2, 2, BANK], 32 * KB)
    sc = share("sc", [P, NBUF, PAGES * P + CH], 110 * KB)
    wT = share("wT", [P, 2, BANK], 135 * KB)
    wn = share("wn", [CH, P], 139 * KB)
    osb = share("osb", [P, 2 * DV], 140 * KB)
    kn = share("kn", [P, NBUF, H, CH], 141 * KB)
    qn = share("qn", [P, NBUF, H, 2 * HQ], 142 * KB)
    vn = share("vn", [CH, D], 145 * KB)
    mq = share("mq", [P, 2, 8], 149 * KB)
    pick = share("pick", [P, 4 * CH], 149 * KB + 512)
    sign = share("sign", [P, 2], 150 * KB)
    blockd = share("blockd", [P, P], 150 * KB + 32)
    causal = share("causal", [CH, P], 150 * KB + 544)
    assert 151 * KB + 96 <= nc.sbuf_usable_end - over

    ps = nc.alloc_psum_tensor("ps", [P, 8, BANK], F32)

    u_scr = nc.dram_tensor("u_scr", [D, CH, NCH], F32, kind="Internal").ap()
    y_scr = nc.dram_tensor("y_scr", [D, CH, NCH], F32, kind="Internal").ap()
    k_scr = nc.dram_tensor("k_scr", [PP, G, P], F32, kind="Internal").ap()

    with ExitStack() as ctx:
        def sem(name):
            return ctx.enter_context(nc.semaphore(name))

        def sems(names):
            return [sem(name) for name in names.split()]

        def pair(name):
            return [sem(f"{name}{s}") for s in range(2)]

        full, free = pair("full"), pair("free")
        raw_full = [sem(f"raw_full{s}") for s in range(4)]
        raw_done = [sem(f"raw_done{s}") for s in range(4)]
        slab_high, slab_read = sems("slab_high slab_read")
        dve_step, act_step, pool_step = sems("dve_step act_step pool_step")
        in_small, in_b, in_x = sem("in_small"), sem("in_b"), pair("in_x")
        consts, v3_built, cond_ready, dt_ready, sincos_in, sincos_out = sems("consts v3_built cond_ready dt_ready sincos_in sincos_out")
        square_ready, square_used = sems("square_ready square_used")
        rows_ready, mod_ready = sems("rows_ready mod_ready")
        x_ready, sq_ready, t1_ready, t2_prompt, t2_sample, h_high, h_ready = sems(
            "x_ready sq_ready t1_ready t2_prompt t2_sample h_high h_ready")
        bbar_ready, cpow_ready, v_ready, kmat_zero, hs_ready, hfin_ready, yu_ready = sems(
            "bbar_ready cpow_ready v_ready kmat_zero hs_ready hfin_ready yu_ready")
        u_put, k_put, y_put, y_got = pair("u_put"), pair("k_put"), pair("y_put"), pair("y_got")
        u_got, kmat_got, put = sems("u_got kmat_got put")
        e_ready, g_high, g_ready = sems("e_ready g_high g_ready")
        sq_head, root_head, head_ready, blocks_ready = sems("sq_head root_head head_ready blocks_ready")
        tok_put = pair("tok_put")
        head_in, s_full, s_max, e_done, w_done, wp_turned, wp_copied, pv_full, head_out = sems(
            "head_in s_full s_max e_done w_done wp_turned wp_copied pv_full head_out")
        k_full, v_full = [sem(f"k_full{s}") for s in range(4)], [sem(f"v_full{s}") for s in range(4)]
        k_turned, kt_ready, scored, s_copied, v_used = sems("k_turned kt_ready scored s_copied v_used")
        sinit, kn_ready, new_scored, vn_full, vn_used = sems("sinit kn_ready new_scored vn_full vn_used")
        m_ready, e_full, w_ready, w_turned, wt_copied, o_copied, o_turned, o_ready = sems(
            "m_ready e_full w_ready w_turned wt_copied o_copied o_turned o_ready")

        def uses(phase, s, i=0):
            return USES[phase][s] + i

        def wait_unit(eng, phase, s, i=0):
            eng.wait_ge(full[s], uses(phase, s, i) + 1)

        def wait_set(phase, s, i=0):
            n = uses(phase, s, i)
            if not (isinstance(n, int) and n == 0):
                nc.tensor.wait_ge(free[s], n)

        def halves(t):
            return t.rearrange("p (a b) -> p a b", a=2)

        dtok = [a["x_prompt"][0, i * P:(i + 1) * P, :] for i in range(QB)] + [
            a["x_sample"].rearrange("b t d -> (b t) d")]
        NTOK = [P] * QB + [DB * DS]

        def slab_source(name):
            kp = "(k p) n -> p k n"
            w = {"ada0": a["w_ada_mix"][0], "ada1": a["w_ada_ffn"][0], "ada2": a["w_ada_kv"],
                 "ada3": a["w_ada_mix"][1], "ada4": a["w_ada_ffn"][1], "glu": a["ssm_w_glu"][0],
                 "up0": a["ffn_w13"][0], "down0": a["ffn_w2"][0], "kv": a["w_kv"], "q": a["w_q"][0],
                 "wo": a["w_o"][0], "up1": a["ffn_w13"][1], "down1": a["ffn_w2"][1]}[name]
            return w.rearrange(kp, p=P)

        block = ctx.enter_context(nc.Block())

        @block.sync
        def _(sp):
            for s in range(2):
                sp.dma_start(xtok[:, s, :], dtok[s]).then_inc(in_x[s], 16)

            def small(dst, src):
                sp.dma_start(dst, src).then_inc(in_small, 16)

            rows = "l (k p) -> (l k) p"
            small(v1[0:8, :], a["c_prompt"].rearrange(rows, p=P))
            small(v1[8:72, :], a["c_sample"].rearrange(rows, p=P))
            small(v1[72:88, :], a["norm_mix"].rearrange(rows, p=P))
            small(v1[88:104, :], a["norm_ffn"].rearrange(rows, p=P))
            small(v1[104:112, :], a["norm_kv"].rearrange("(k p) -> k p", p=P))
            small(v1[112:120, :], a["ssm_d"].rearrange(rows, p=P))
            small(v1[120:121, :], a["k_norm"].rearrange("(o m) d -> o (m d)", o=1))
            small(v1[121:122, :], a["q_norm"].rearrange("o m d -> o (m d)"))
            small(v1[122:123, :], a["subln"])
            small(v2[0:48, :], a["b_ada_mix"].rearrange(rows, p=P))
            small(v2[48:96, :], a["b_ada_ffn"].rearrange(rows, p=P))
            small(v2[96:112, :], a["b_ada_kv"].rearrange("(k p) -> k p", p=P))
            small(v3[0:32, :], a["ssm_lam_re"][0].rearrange("(j g) n -> j (g n)", g=2))
            small(v3[32:64, :], a["ssm_lam_im"][0].rearrange("(j g) n -> j (g n)", g=2))
            small(lst[64:96, :], a["ssm_log_step"][0].rearrange("(j g) -> j g", g=2))
            for r, name in enumerate(("state_ssm_re", "state_ssm_im")):
                for k in range(2):
                    small(hraw[:, r, k, :], a[name][0, 4 * k:4 * k + 4].rearrange("b (j g) n -> (b j) (g n)", g=2))
            small(lrow[:, :, :].rearrange("p k d -> p (k d)"), a["diff_lambda"].rearrange("o k d -> o (k d)").to_broadcast([P, 4 * DK]))
            small(pages[:, :], a["page_table"].rearrange("(o b) p -> o (b p)", o=1))

            def slabs(name, cols, k0=lambda j: 0, nk=lambda j: 8, per=4):
                src, first = slab_source(name), SLABS[name]

                def turn(i):
                    for j in range(per):
                        slot = j % 4
                        if first or not isinstance(i, int):
                            sp.wait_ge(raw_done[slot], (first + j) // 4 + i * (per // 4))
                        a0, n = k0(j), nk(j)
                        sp.dma_start(raw[:, slot, 0:n, :], src[:, a0:a0 + n, ds(cols(i, j), P)]
                                     ).then_inc(raw_full[slot], 16)

                if first == 0:
                    turn(0)
                with sp.Fori(0 if first else 1, COUNT[name] // per) as i:
                    turn(i)

            def one(i, j):
                return i * (4 * P) + j * P

            def halves_in_turns(half):
                return lambda i, j: i * (2 * P) + (j // 2) * P + (j % 2) * half

            def long(i, j):
                return i * (2 * P) + (j // 4) * P

            def page_loads(b, o, u, keys, values):
                slot = u % 4
                for go, seq, cache, dst, ready in ((keys, b, "cache_k", kpg, k_full), (values, b - LAG, "cache_v", vpg, v_full)):
                    if not go:
                        continue
                    at = seq * PAGES + o * 8 + u
                    page = sp.value_load(pages[0:1, ds(at, 1)], min_val=0, max_val=NPOOL - 1)
                    if cache == "cache_v":
                        sp.wait_ge(v_used, at + 1)
                    elif not isinstance(at, int) or at > 3:
                        sp.wait_ge(k_turned, at * 2 - 6)
                    form = "o k h m d -> k (o h m d)" if cache == "cache_k" else "o k h d -> k (o h d)"
                    sp.dma_start(dst[:, slot].rearrange("p h m -> p (h m)"), a[cache][ds(page, 1)].rearrange(form)
                                 ).then_inc(ready[slot], 16)

            slabs("ada0", one)
            for name in ("ada1", "ada2", "ada3", "ada4"):
                slabs(name, one)
            slabs("glu", halves_in_turns(D))
            for layer in range(2):
                slabs(f"up{layer}", halves_in_turns(DFF))
                slabs(f"down{layer}", long, k0=lambda j: 6 * (j % 4), nk=lambda j: (6, 6, 6, 4)[j % 4], per=8)
                if layer:
                    break
                slabs("kv", one)
                slabs("q", one)
                sp.wait_ge(in_small, 16 * SMALL)
                for s in range(2):
                    sp.wait_ge(free[s], USES["qtok"][s])
                for u in range(PAGES):
                    page_loads(0, u // 8, u % 8, True, False)

                def loads(b, keys=True, values=True):
                    with sp.Fori(0, PAGES // 8) as o:
                        for u in range(8):
                            page_loads(b, o, u, keys, values)

                for b in range(1, LAG):
                    loads(b, values=False)
                with sp.Fori(LAG, DB) as b:
                    loads(b)
                for b in range(DB, DB + LAG):
                    loads(b, keys=False)
                slabs("wo", one)
            sp.wait_ge(put, 16 * 6)
            for s in range(2):
                sp.wait_ge(tok_put[s], 16 * 3 * (3 - s))

        @block.tensor
        def _(pe):
            mm = nc.tensor.matmul

            def turn(dst, src, rows=P):
                return nc.tensor.transpose(dst, src, ident[0:rows, 0:rows])

            pe.wait_ge(consts, 3)
            for i in range(QB + 1):
                s = i % 2
                wait_set("x", s, i // 2)
                pe.wait_ge(in_x[s], 16 * (i // 2 + 1))
                for k in range(KD):
                    last = turn(ps[:, 4 * s + k // 4, (k % 4) * P:(k % 4) * P + NTOK[i]],
                                xtok[0:NTOK[i], s, k * P:(k + 1) * P], NTOK[i])
                last.then_inc(full[s], 1)

            def ada(n, first, turns):
                name = f"ada{n}.{first}"
                pe.wait_ge(cond_ready, 2)

                def add_up(unit, s, j):
                    if j == 0:
                        pe.wait_ge(rows_ready, unit + 1)
                    last = mm(ps[:, 4 * s + 1, j * C9:(j + 1) * C9], t2[:, s, j * P:(j + 1) * P], add4[:, :],
                              start=True, stop=True)
                    if j == 3:
                        last.then_inc(full[s], 1)

                def turn_(i, opening=False):
                    for s in range(2):
                        unit = i * 2 + (SLABS[f"ada{n}"] // 4 + 2 * first + s)
                        wait_set(name, s, i)
                        for j in range(4):
                            pe.wait_ge(raw_full[j], (unit + 1) * 16)
                            for k in range(KD):
                                g = k % 4
                                last = mm(ps[32 * g:32 * g + 32, 4 * s, j * P:(j + 1) * P], cond[:, k, :], raw[:, j, k, :],
                                          start=(k < 4), stop=(k >= 4))
                            last.then_inc(raw_done[j], 1)
                            if s or not opening:
                                add_up(unit - 1, 1 - s, j)

                turn_(0, opening=True)
                if turns > 1:
                    with pe.Fori(1, turns) as i:
                        turn_(i)
                for j in range(4):
                    add_up(SLABS[f"ada{n}"] // 4 + 2 * (first + turns) - 1, 1, j)

            def norm(n):
                name = f"norm{n}"
                wait_set(name, 0)
                pe.wait_ge(sq_ready, n)
                for h in range(2):
                    last = mm(ps[:, h, 0:HALF], ones[:, :], halves(sqs[:, :])[:, h, :], start=True, stop=True)
                last.then_inc(full[0], 1)

            def head_sum(m, bank, s, n):
                pe.wait_ge(sq_head, n)
                for h in range(2):
                    last = mm(ps[:, bank + h, 0:HALF], m[:, :], t1[:, s, h * HALF:(h + 1) * HALF], start=True, stop=True)
                return last

            def dense(name):
                units, slabs, per = DENSE[name]
                n0, S = SLABS[name], len(slabs)
                g0 = n0 - SLABS["glu"]
                src = gr if name.startswith("down") else hr
                kfirst = {"glu": 0, "up0": 8, "kv": 16, "q": 24, "wo": 32, "up1": 40}.get(name)
                with pe.Fori(0, units // per) as i:
                    for u in range(per):
                        s = u % 2
                        wait_set(name, s, i * (per // 2) + u // 2)
                        for j, (tile, k0, nk) in enumerate(slabs):
                            n = u * S + j
                            slot, wslot = n % 4, n % 2
                            pe.wait_ge(raw_done[slot], (n0 + n) // 4 + 1 + i * (per * S // 4))
                            for k in range(nk):
                                if name == "q" and k == nk - 1:
                                    head_sum(blockd, 4 * s + 2, s, i * per + u + 1)
                                if u == 0 and name.startswith("down"):
                                    pe.wait_ge(g_ready, FT * int(name[-1]) + k0 + k + 1)
                                elif u == 0 and j == 0:
                                    pe.wait_ge(h_ready, kfirst + k + 1)
                                for w, v in ((0, 0), (0, 1), (1, 0)):
                                    for h in range(2):
                                        first = k0 + k == 0 and (w, v) == (0, 0)
                                        end = j == S - 1 or slabs[j + 1][0] != tile
                                        last = mm(ps[:, 4 * s + 2 * tile + h, 0:HALF], ws[:, wslot, w, k, :],
                                                  src[:, k0 + k, v, h * HALF:(h + 1) * HALF], start=first,
                                                  stop=(end and k == nk - 1 and (w, v) == (1, 0)))
                            last.then_inc(full[s] if j == S - 1 else slab_read, 1)

            wait_set("small", 0)
            pe.wait_ge(in_small, 16 * SMALL)
            pe.wait_ge(in_b, 16 * 18)
            pe.wait_ge(v3_built, 1)
            turn(ps[:, 0, 0:123], v1[0:123, :], 123)
            turn(ps[:, 0, P:P + 112], v2[0:112, :], 112)
            turn(ps[:, 0, 2 * P:2 * P + 96], v3[0:96, :], 96)
            for r in range(2):
                for k in range(2):
                    turn(ps[:, 1, (2 * r + k) * P:(2 * r + k + 1) * P], hraw[:, r, k, :])
                for k in range(4):
                    last = turn(ps[:, 2 + r, k * P:(k + 1) * P], craw[:, r, k, :])
            last.then_inc(full[0], 1)

            ada(0, 0, 3)
            wait_set("norm0", 0)
            for k in range(KD):
                pe.wait_ge(square_ready, k + 1)
                for h in range(2):
                    last = mm(ps[:, h, 0:HALF], ones[:, :], t1[:, k % 2, h * HALF:(h + 1) * HALF], start=(k == 0), stop=(k == KD - 1))
                last.then_inc(square_used if k < KD - 1 else full[0], 1)

            pe.wait_ge(bbar_ready, 1)
            pe.wait_ge(cpow_ready, 1)
            for u in range(4):
                s = u % 2
                if u == 2:
                    ada(1, 0, 1)
                wait_set(f"ssm_k{u // 2}", s)
                for jj in range(2):
                    for r, t, g2 in ((r, t, g2) for r in range(2) for t in range(4) for g2 in range(2)):
                        q = slice(g2 * N, (g2 + 1) * N)
                        j = u * 8 + jj * 4 + t
                        last = mm(ps[32 * t:32 * t + PP, 4 * s + g2, jj * P:(jj + 1) * P], bbar[q, r, j, :],
                                  cpow[q, j, r, 0:CH, :].rearrange("p t q -> p (t q)"), start=(r == 0), stop=(r == 1))
                last.then_inc(full[s], 1)
            pe.wait_ge(v_ready, 2)
            for u in range(4):
                s = u % 2
                wait_set("ssm_v", s, u // 2)
                for jj in range(8):
                    for r in range(2):
                        i = jj * 2 + r
                        last = turn(ps[:, 4 * s + i // 4, (i % 4) * P:(i % 4 + 1) * P],
                                    vmat[:, r, u * 8 + jj].rearrange("p s q -> p (s q)"))
                last.then_inc(full[s], 1)
            for s in range(2):
                pe.wait_ge(free[s], USES["ssm_w"][s])
            pe.wait_ge(u_got, 16 * CH)
            for u in range(4):
                s = u % 2
                wait_set("ssm_w", s, u // 2)
                for jj in range(8):
                    j = u * 8 + jj
                    for r in range(2):
                        for g2 in range(2):
                            at = (jj % 2) * 2 * NCH + r * NCH
                            last = mm(ps[g2 * N:(g2 + 1) * N, 4 * s + jj // 2, at:at + NCH],
                                      vT[:, j, r, g2 * N:(g2 + 1) * N], uch[:, 2 * j + g2, :], start=True, stop=True)
                last.then_inc(full[s], 1)
            ada(1, 1, 2)
            ada(2, 0, 2)
            ada(3, 0, 3)
            pe.wait_ge(kmat_got, 16 * CH)
            for u in range(4):
                s = u % 2
                if u == 2:
                    ada(4, 0, 1)
                wait_set(f"ssm_y{u // 2}", s)
                groups = [(g2, jj, u * 8 + jj, half, ps[half * 64:(half + 1) * 64, 4 * s + 2 * g2 + jj // 4, (jj % 4) * NCH:(jj % 4 + 1) * NCH])
                          for jj in range(8) for g2 in range(2) for half in range(2)]
                for g2, jj, j, half, dst in groups:
                    mm(dst, kmat[:, 2 * j + g2, half * 64:(half + 1) * 64], uch[:, 2 * j + g2, :], start=(jj % 4 == 0), stop=False,
                       skip_group_check=True)
                if u == 0:
                    pe.wait_ge(hs_ready, 1)
                for r in range(2):
                    for g2, jj, j, half, dst in groups:
                        q, t0 = slice(g2 * N, (g2 + 1) * N), 1 + half * (CH // 2)
                        last = mm(dst, cpow[q, j, r, t0:t0 + CH // 2, :].rearrange("p t q -> p (t q)"), hs[q, 0:NCH, r, j],
                                  start=False, stop=(r == 1), skip_group_check=True)
                last.then_inc(full[s], 1)
            ada(4, 1, 1)
            wait_set("ssm_h", 0)
            pe.wait_ge(hfin_ready, 1)
            for r in range(2):
                turn(ps[0:J, r, 0:P], hs[:, NCH, r, :], P)
                for k in range(2):
                    last = turn(ps[:, r, (k + 1) * P:(k + 2) * P], hfin[:, r, 4 * k:4 * k + 4, :].rearrange("p b j -> p (b j)"))
            last.then_inc(full[0], 1)

            ada(4, 2, 1)
            dense("glu")
            norm(1)
            dense("up0")
            dense("down0")
            norm(2)
            dense("kv")
            pe.wait_ge(blocks_ready, 1)
            dense("q")

            def heads(name, m, n0):
                with pe.Fori(0, H // 2) as i:
                    for s in range(2):
                        wait_set(name, s, i)
                        head_sum(m, 4 * s, s, n0 + s + 1 + 2 * i).then_inc(full[s], 1)

            pe.wait_ge(head_ready, 2 + H)
            for n in range(2 * (QB + 1)):
                s, src, i = n % 2, (kT, vTf)[n // (QB + 1)], n % (QB + 1)
                wait_set("qtok", s, n // 2)
                if n < H:
                    head_sum(blockd, 4 * s, s, H + n + 1)
                for h in range(H):
                    last = turn(ps[0:NTOK[i], 4 * s + 2 + h // 4, (h % 4) * P:(h % 4 + 1) * P],
                                src[:, h, i * P:i * P + NTOK[i]])
                last.then_inc(full[s], 1)

            for s in range(2):
                pe.wait_ge(free[s], USES["attn"][s])

            def block_scores(h, hp, i):
                w = (i + 1) * P
                if i == 0:
                    pe.wait_ge(head_in, h + 1)
                pe.wait_ge(e_done, h * QB + (i + 1))
                for m in range(2):
                    q = slice(m * DK, (m + 1) * DK)
                    last = mm(ps[:, 2 * (i % 2) + m, 0:w], qh[q, hp, i * P:w], kh[q, hp, 0:w], start=True, stop=True)
                last.then_inc(s_full, 1)

            def block_weights(h, i):
                pe.wait_ge(w_done, h * QB + (i + 1))
                pe.wait_ge(wp_copied, h * QB + (i + 1))
                for k in range(i + 1):
                    last = turn(ps[:, 4 + i % 2, k * P:(k + 1) * P], e01[:, i % 2, 0, k * P:(k + 1) * P])
                last.then_inc(wp_turned, 1)

            def head_values(h, hp):
                pe.wait_ge(wp_copied, h * QB + (QB + 2))
                pe.wait_ge(head_out, h + 1)
                for k in range(QB):
                    last = mm(ps[:, 6, k * P:SEQ], vh[:, hp, k, :], wtT[:, k, k * P:SEQ], start=(k == 0), stop=(k == QB - 1))
                last.then_inc(pv_full, 1)

            def head_pair(k, first=False, final=False):
                for hp in range(2):
                    h = k * 2 + hp
                    for i in range(QB):
                        if i == 1 and not (first and hp == 0):
                            head_values(h - 1, 1 - hp)
                        if i < QB - 2:
                            block_scores(h, hp, i + 2)
                        elif not (final and hp):
                            block_scores(h + 1, 1 - hp, i + 2 - QB)
                        block_weights(h, i)

            for i in range(2):
                block_scores(0, 0, i)
            head_pair(0, first=True)
            with pe.Fori(1, H // 2 - 1) as k:
                head_pair(k)
            head_pair(H // 2 - 1, final=True)
            head_values(H - 1, 1)

            pe.wait_ge(head_out, H + 1)

            def turn_page(b, par, u):
                slot = u % 4
                pe.wait_ge(k_full[slot], 16 * (b * (PAGES // 4) + u // 4 + 1))
                for half in range(2):
                    at = (b * PAGES + u) * 2 + half
                    bank = ((par * PAGES + u) * 2 + half) % 3
                    if not isinstance(at, int) or at > 2:
                        pe.wait_ge(kt_ready, at - 2)
                    for h in range(4):
                        last = turn(ps[:, bank, h * P:(h + 1) * P], kpg[:, slot, 4 * half + h, :])
                    last.then_inc(k_turned, 1)

            def scores(b, par, u):
                at = b * PAGES + u
                quad = b * (PAGES // 4) + u // 4
                if u % 4 == 0 and (not isinstance(quad, int) or quad > 1):
                    pe.wait_ge(s_copied, quad - 1)
                if u == 0:
                    pe.wait_ge(kn_ready, b + 1)
                pe.wait_ge(kt_ready, at * 2 + 2)
                for o in range(2):
                    for g in range(4):
                        h = 2 * g + o
                        last = mm(ps[32 * g:32 * g + 32, 4 + u // 4 % 2, (u % 4) * P:(u % 4 + 1) * P], qn[:, par % NBUF, h, :],
                                  kTs[:, u % 2, h // 4, (h % 4) * P:(h % 4 + 1) * P], start=(o == 0), stop=(o == 1))
                last.then_inc(scored, 1)

            def b_has(b, n):
                return not isinstance(b, int) or b >= n

            def new_scores(b, par):
                if b_has(b, LAG):
                    pe.wait_ge(o_ready, b - LAG + 1)
                if b_has(b, 1):
                    pe.wait_ge(m_ready, b)
                for g in range(4):
                    dst = ps[32 * g:32 * g + 32, 3, 0:CH]
                    for o in range(2):
                        mm(dst, qn[:, par % NBUF, 2 * g + o, :], kn[:, par % NBUF, 2 * g + o, :], start=(o == 0), stop=False)
                    last = mm(dst, causal[:, 32 * g:32 * g + 32], ident[0:CH, 0:CH], start=False, stop=True)
                last.then_inc(new_scored, 1)

            def turn_weights(b, par, q):
                if q == 0:
                    pe.wait_ge(w_ready, b - LAG + 1)
                pe.wait_ge(wt_copied, (b - LAG) * 5 + q + 1)
                src = sc[:, (par - LAG) % NBUF]
                if q == 4:
                    last = turn(ps[0:CH, 7, 0:P], src[:, PAGES * P:])
                else:
                    for u in range(4):
                        last = turn(ps[:, 7, u * P:(u + 1) * P], src[:, (4 * q + u) * P:(4 * q + u + 1) * P])
                last.then_inc(w_turned, 1)

            def values(b, u):
                slot = u % 4
                if u == 0:
                    pe.wait_ge(o_copied, b - LAG + 1)
                if u % 4 == 0:
                    pe.wait_ge(wt_copied, (b - LAG) * 5 + u // 4 + 2)
                pe.wait_ge(v_full[slot], 16 * ((b - LAG) * (PAGES // 4) + u // 4 + 1))
                for h in range(H):
                    g = h % 4
                    last = mm(ps[32 * g:32 * g + HQ, 6, (h // 4) * DV:(h // 4 + 1) * DV],
                              wT[:, u // 4 % 2, (u % 4) * P + h * HQ:(u % 4) * P + (h + 1) * HQ],
                              vpg[:, slot, h, :], start=(u == 0 and h < 4), stop=False, skip_group_check=True)
                last.then_inc(v_used, 1)

            def new_values(b):
                for h in range(H):
                    g = h % 4
                    last = mm(ps[32 * g:32 * g + HQ, 6, (h // 4) * DV:(h // 4 + 1) * DV], wn[:, h * HQ:(h + 1) * HQ],
                              vn[:, h * DV:(h + 1) * DV], start=False, stop=False, skip_group_check=True)
                last.then_inc(vn_used, 1)

            def outputs(b):
                pe.wait_ge(o_copied, b - LAG + 2)
                for k in range(2):
                    last = mm(ps[:, 3, (k + 1) * 4 * CH:(k + 2) * 4 * CH], osb[:, k * DV:(k + 1) * DV], pick[:, :],
                              start=True, stop=True)
                last.then_inc(o_turned, 1)

            def sequence(b, par, keys=True, vals=True):
                if vals:
                    turn_weights(b, par, 0)
                if keys:
                    turn_page(b, par, 0)
                for u in range(PAGES):
                    if keys and u < PAGES - 1:
                        turn_page(b, par, u + 1)
                    if vals:
                        values(b, u)
                    if keys:
                        scores(b, par, u)
                    if vals and u % 4 == 2:
                        turn_weights(b, par, u // 4 + 1)
                if vals:
                    pe.wait_ge(vn_full, 16 * (b - LAG + 1))
                    pe.wait_ge(wt_copied, (b - LAG + 1) * 5 + 1)
                if keys:
                    new_scores(b, par)
                if vals:
                    new_values(b)
                    outputs(b)

            sequence(0, 0, vals=False)
            sequence(1, 1, vals=False)
            with pe.Fori(0, (DB - LAG) // NBUF) as i:
                for v in range(NBUF):
                    sequence(i * NBUF + (LAG + v), LAG + v)
            sequence(DB, DB, keys=False)
            sequence(DB + 1, DB + 1, keys=False)
            pe.wait_ge(o_ready, DB + 1)
            heads("ohead", ones, 16)
            dense("wo")
            norm(3)
            dense("up1")
            dense("down1")
            pe.wait_ge(x_ready, 4 * KD)
            for i in range(QB + 1):
                s = i % 2
                wait_set("y", s, i // 2)
                for k in range(KD):
                    last = turn(ps[0:NTOK[i], 4 * s + k // 4, (k % 4) * P:(k % 4 + 1) * P],
                                x[:, k, i * P:i * P + NTOK[i]])
                last.then_inc(full[s], 1)

        BIAS = [128, 176, 224, 152, 200]
        NORM = [72, 88, 104, 80, 96]
        APPLY = {"s5": (0, 0, None), "up0": (1, 1, 8), "kv": (2, 2, 16), "q": (2, 3, 24), "up1": (3, 4, 40)}
        ORDER = list(APPLY)
        GATE = {"glu": 0, "down0": 1, "wo": 3, "down1": 4}
        XUP = {"glu": 0, "down0": 8, "wo": 16, "down1": 24}

        def cols(n, part, k, lo, hi):
            return mod[:, n, ds(part * KD + k, 1), lo:hi].rearrange("p a c -> p (a c)")

        def by_token(v):
            return v.unsqueeze(2).to_broadcast([P, DB, DS])

        def sample(t):
            return t[:, SEQ:T].rearrange("p (b t) -> p b t", b=DB)

        def tile(t, k):
            return t[:, ds(k, 1), :].rearrange("p a t -> p (a t)")

        def part(t, k, v):
            return t[:, ds(k, 1), v, :].rearrange("p a t -> p (a t)")

        def chunks_prompt(t):
            return t.rearrange("p (s c) -> p c s", s=CH)[:, DB:NCH, :]

        def chunks_sample(t):
            return t.rearrange("p (s c) -> p c s", s=CH)[:, 0:DB, :]

        def by_halves(t, k):
            return t[:, ds(k, 1), :].rearrange("p k (a b) -> p (k a) b", a=2)

        @block.scalar
        def _(act):
            A = nc.scalar.activation
            step = Steps(act, act_step)

            def load_bc():
                for r, name in enumerate(("ssm_c_re", "ssm_c_im")):
                    for g in range(2):
                        for k in range(4):
                            act.dma_start(craw[:, r, k, g * N:(g + 1) * N],
                                          a[name][0, 16 * k:16 * k + 16].rearrange("(j g) p n -> g j p n", g=2)[g]
                                          ).then_inc(in_b, 16)
                for r, name in enumerate(("ssm_b_re", "ssm_b_im")):
                    act.dma_start(bmat[:, r], a[name][0].rearrange("(j g) n p -> (g n) j p", g=2)).then_inc(in_b, 16)

            def root(n):
                wait_unit(act, f"norm{n}", 0)
                A(halves(rstd[:, :]), ps[:, 0:2, 0:HALF], ACT.Sqrt, bias=eps[:, 0:1], scale=1.0 / D).then_inc(free[0], 1)

            for i in range(QB + 1):
                s = i % 2
                if i == 3:
                    load_bc()
                wait_unit(act, "x", s, i // 2)
                if i + 2 <= QB:
                    act.dma_start(xtok[0:NTOK[i + 2], s, :], dtok[i + 2]).then_inc(in_x[s], 16)
                A(x[:, :, i * P:i * P + NTOK[i]].rearrange("p (b k) t -> p b k t", b=2),
                  ps[:, 4 * s:4 * s + 2, :].rearrange("p b (k t) -> p b k t", t=P)[:, :, :, 0:NTOK[i]], ACT.Copy).then_inc(free[s], 1)
            wait_unit(act, "small", 0)
            act.wait_ge(dt_ready, 1)
            act.wait_ge(cond_ready, 1)
            A(cond[:, :, 0:C9].rearrange("p k c -> p c k"), vec[:, 0:C9 * KD].rearrange("p (c k) -> p c k", c=C9), ACT.Silu
              ).then_inc(cond_ready, 1)
            A(tiny[:, 0], vec[:, 320:352], ACT.Exp).then_inc(sincos_out, 1)
            act.wait_ge(dt_ready, 2)
            A(neglam[:, :], lsum[:, 0:1], ACT.Exp)
            A(lsum[:, 2:3], lsum[:, 1:2], ACT.Exp).then_inc(sincos_out, 1)
            act.wait_ge(sincos_in, 1)
            A(tiny[:, 6], tiny[:, 1], ACT.Exp)
            A(tiny[:, 7], tiny[:, 4], ACT.Sin)
            A(tiny[:, 8], tiny[:, 5], ACT.Sin).then_inc(sincos_out, 1)

            def ada_out(n, first, turns):
                with act.Fori(0, turns) as i:
                    for s in range(2):
                        act.wait_ge(raw_done[3], i * 2 + (SLABS[f"ada{n}"] // 4 + 2 * first + s + 1))
                        A(t2[:, s, 0:BANK], ps[:, 4 * s, :], ACT.Copy).then_inc(rows_ready, 1)
                        wait_unit(act, f"ada{n}.{first}", s, i)
                        A(mod[:, n].rearrange("p m c -> p (m c)")[:, ds(i * (8 * C9) + (2 * first + s) * (4 * C9), 4 * C9)],
                          ps[:, 4 * s + 1, 0:4 * C9], ACT.Copy).then_inc(free[s], 1)

            def apply(name):
                _, m, h0_ = APPLY[name]
                b0 = KD * ORDER.index(name)
                act.wait_ge(mod_ready, m + 1)
                with act.Fori(0, KD // 2) as i:
                    for s in range(2):
                        k = i * 2 + s
                        act.wait_ge(t1_ready, b0 + s + 1 + i * 2)
                        A(t2[:, s, 0:SEQ], t1[:, s, 0:SEQ], ACT.Identity, bias=cols(m, 0, k, 0, 1),
                          scale=gain[:, m, ds(k, 1), 0:1].rearrange("p a c -> p (a c)")).then_inc(t2_prompt, 1)
                        act.wait_ge(t2_prompt, b0 + s + 1 + i * 2)
                        act.wait_ge(t2_sample, b0 + s + 1 + i * 2)
                        A(part(hr, k, 0), t2[:, s, :], ACT.Copy).then_inc(h_high, 1)

            ada_out(0, 0, 3)
            for s in range(2):
                act.wait_ge(free[s], USES["norm0"][s])
            for k in range(KD):
                if k >= 2:
                    act.wait_ge(square_used, k - 1)
                A(t1[:, k % 2, :], x[:, k, :], ACT.Square).then_inc(square_ready, 1)
            root(0)
            act.wait_ge(mod_ready, 1)
            for k in range(KD):
                s = k % 2
                act.wait_ge(t1_ready, k + 1)
                if k >= 2:
                    act.wait_ge(u_put[s], 16 * (k // 2))
                A(chunks_prompt(t2[:, s, :]), t1[:, s, 0:SEQ].rearrange("p (c s) -> p c s", s=CH), ACT.Identity,
                  bias=mod[:, 0, k, 0:1], scale=gain[:, 0, k, 0:1]).then_inc(t2_prompt, 1)
                act.wait_ge(t2_prompt, k + 1)
                act.wait_ge(t2_sample, k + 1)
                act.dma_start(u_scr[k * P:(k + 1) * P].rearrange("f s c -> f (s c)"), t2[:, s, :]).then_inc(u_put[s], 16)
            for s in range(2):
                act.wait_ge(u_put[s], 16 * (KD // 2))
            for s in range(CH):
                act.dma_start(uch[s * PP:(s + 1) * PP, :, :], u_scr.rearrange("(g p) s c -> s p g c", p=PP)[s]
                              ).then_inc(u_got, 16)
            for u in range(4):
                s = u % 2
                if u == 2:
                    ada_out(1, 0, 1)
                wait_unit(act, f"ssm_k{u // 2}", s)
                if u >= 2:
                    act.wait_ge(k_put[s], 16)
                for t in range(4):
                    done = A(krow[:, s].rearrange("p (j t g) m -> p t g j m", t=4, g=2)[:, t],
                             ps[32 * t:32 * t + PP, 4 * s:4 * s + 2, 0:2 * P].rearrange("p g (j m) -> p g j m", m=P), ACT.Copy)
                done.then_inc(free[s], 1)
                act.wait_ge(free[s], uses(f"ssm_k{u // 2}", s) + 1)
                act.dma_start(k_scr[:, 16 * u:16 * u + 16, :], krow[:, s, :, :]).then_inc(k_put[s], 16)
            for s in range(2):
                act.wait_ge(k_put[s], 16 * 2)
            for u in range(4):
                s = u % 2
                wait_unit(act, "ssm_v", s, u // 2)
                A(vT[:, 8 * u:8 * u + 8].rearrange("p j r m -> p (j r m)"),
                  ps[:, 4 * s:4 * s + 4, :].rearrange("p b c -> p (b c)"), ACT.Copy).then_inc(free[s], 1)
            for u in range(4):
                s = u % 2
                wait_unit(act, "ssm_w", s, u // 2)
                for r in range(2):
                    done = A(drive[:, :, r, 8 * u:8 * u + 8].rearrange("p c (b j) -> p b j c", j=2),
                             ps[:, 4 * s:4 * s + 4, 0:4 * NCH].rearrange("p b (j r c) -> p r b j c", j=2, r=2)[:, r], ACT.Copy)
                done.then_inc(free[s], 1)
            act.wait_ge(kmat_zero, 1)
            for s in range(CH):
                act.dma_start(kmat[s * PP:(s + 1) * PP, :, s * PP:P], k_scr[:, :, 0:P - s * PP]).then_inc(kmat_got, 16)
            ada_out(1, 1, 2)
            ada_out(2, 0, 2)
            ada_out(3, 0, 3)
            for u in range(4):
                s = u % 2
                act.wait_ge(free[s], uses(f"ssm_y{u // 2}", s) + 1)
                for t in range(CH):
                    act.dma_start(y_scr.rearrange("(g p) t c -> t p g c", p=PP)[t, :, 16 * u:16 * u + 16, :],
                                  ysb[t * PP:(t + 1) * PP, s, :].rearrange("p (g c) -> p g c", c=NCH)).then_inc(y_put[s], 16)
                if s:
                    ada_out(4, u // 2, 1)
            wait_unit(act, "ssm_h", 0)
            for r in range(2):
                A(hout[0:J, 3 * r, :], ps[0:J, r, 0:P], ACT.Copy)
                done = A(hout[:, 3 * r + 1:3 * r + 3, :].rearrange("p k m -> p (k m)"), ps[:, r, P:3 * P], ACT.Copy)
            done.then_inc(free[0], 1)
            act.wait_ge(free[0], uses("ssm_h", 0) + 1)
            for r in range(2):
                act.dma_start(out[2 + r][0, 0].rearrange("(j g) n -> j (g n)", g=2), hout[0:J, 3 * r, :]).then_inc(put, 16)
                for k in range(2):
                    act.dma_start(out[4 + r][0, 4 * k:4 * k + 4].rearrange("b (j g) n -> (b j) (g n)", g=2),
                                  hout[:, 3 * r + 1 + k, :]).then_inc(put, 16)
            ada_out(4, 2, 1)
            for s in range(2):
                act.wait_ge(y_put[s], 16 * 2 * CH)

            def split(m, late=0, nk=8):
                slot, w = m % 4, m % 2
                act.wait_ge(raw_full[slot], 16 * ((DENSE0 + m) // 4 + 1) + late * 4)
                A(ws[:, w, 0, 0:nk, :].rearrange("p k n -> p (k n)"), raw[:, slot, 0:nk, :].rearrange("p k n -> p (k n)"),
                  ACT.Copy).then_inc(slab_high, 1)

            def yu_load(k):
                s = k % 2
                act.dma_start(yin[:, s].rearrange("p s c -> p (s c)"), y_scr[k * P:(k + 1) * P].rearrange("f s c -> f (s c)")
                              ).then_inc(y_got[s], 16)
                act.dma_start(uin[:, s].rearrange("p s c -> p (s c)"), u_scr[k * P:(k + 1) * P].rearrange("f s c -> f (s c)")
                              ).then_inc(y_got[s], 16)

            yu_load(0)
            yu_load(1)
            split(0)
            split(1)
            for k in range(KD):
                s = k % 2
                act.wait_ge(yu_ready, k + 1)
                if k >= 2:
                    act.wait_ge(h_ready, k - 1)
                if k + 2 < KD:
                    yu_load(k + 2)
                A(t2[:, s, 0:SEQ].rearrange("p (c s) -> p c s", s=CH), chunks_prompt(t1[:, s, :]), ACT.Gelu_apprx_tanh)
                step(A(t2[:, s, SEQ:T].rearrange("p (c s) -> p c s", s=CH), chunks_sample(t1[:, s, :]), ACT.Gelu_apprx_tanh))
                A(hr[:, k, 0, :], t2[:, s, :], ACT.Copy).then_inc(h_high, 1)

            def square(src, h, s):
                A(t1[:, s, :], tile(src, h), ACT.Square).then_inc(sq_head, 1)

            def head_root(n, bank, s, width):
                act.wait_ge(head_ready, n + 1)
                return A(halves(t2[:, s, :]), ps[:, bank:bank + 2, 0:HALF], ACT.Sqrt, bias=eps[:, 0:1], scale=1.0 / width)

            def dense(name, tail=True):
                units, slabs, per = DENSE[name]
                S, n0 = len(slabs), SLABS[name] - DENSE0

                def turn(i, last):
                    for u in range(per):
                        s = u % 2
                        for j in range(S):
                            n = u * S + j
                            if j == S - 1:
                                wait_unit(act, name, s, i * (per // 2) + u // 2)
                            else:
                                act.wait_ge(slab_read, INNER[name] + u * (S - 1) + j + 1 + i * (per * (S - 1)))
                            if not (last and n + 2 >= per * S):
                                split(n0 + n + 2, i * (per * S), slabs[(j + 2) % S][2] if S == 4 and j < 2 else 8)
                        at = i * (per // 2) + u // 2
                        if name == "glu":
                            A(halves(t1[:, s, :]), ps[:, 4 * s + 2:4 * s + 4, 0:HALF], ACT.Sigmoid).then_inc(e_ready, 1)
                        elif name.startswith("up"):
                            f = i * 2 + u
                            A(halves(t1[:, s, :]), ps[:, 4 * s:4 * s + 2, 0:HALF], ACT.Silu).then_inc(e_ready, 1)
                            act.wait_ge(free[s], uses(name, s, at) + 1)
                            A(part(gr, f, 0), t2[:, s, :], ACT.Copy).then_inc(g_high, 1)
                        elif name == "kv":
                            A(by_halves(kvT, i * per + u), ps[:, 4 * s:4 * s + 2, 0:HALF], ACT.Copy).then_inc(free[s], 1)
                        elif name == "q":
                            A(by_halves(qT, i * per + u), ps[:, 4 * s:4 * s + 2, 0:HALF], ACT.Copy)
                            head_root(i * per + u, 4 * s + 2, s, DK).then_inc(free[s], 1)
                            if not (last and u >= per - 2):
                                square(kT, i * per + u + 2, s)

                if tail:
                    with act.Fori(0, units // per) as i:
                        turn(i, False)
                else:
                    with act.Fori(0, units // per - 1) as i:
                        turn(i, False)
                    turn(units // per - 1, True)

            dense("glu")
            root(1)
            apply("up0")
            dense("up0")
            dense("down0")
            root(2)
            apply("kv")
            dense("kv")
            apply("q")
            for s in range(2):
                act.wait_ge(free[s], USES["q"][s])
            for s in range(2):
                square(kT, s, s)
            dense("q", tail=False)

            for s in range(2):
                act.wait_ge(free[s], USES["qtok"][s])
            for s in range(2):
                square(qT, s, s)
            for n in range(2 * (QB + 1)):
                s, v, i = n % 2, n // (QB + 1), n % (QB + 1)
                slot = i % 2
                wait_unit(act, "qtok", s, n // 2)
                if n < H:
                    head_root(H + n, 4 * s, s, DK).then_inc(root_head, 1)
                if v and i < QB:
                    dst = vtok[:, i].rearrange("p h d -> p (h d)")
                else:
                    dst = tok[0:NTOK[i], slot, :]
                    if v or i >= 2:
                        act.wait_ge(tok_put[slot], 16 * (3 + 2 if v else i // 2))
                A(dst, ps[0:NTOK[i], 4 * s + 2:4 * s + 4, :].rearrange("p b c -> p (b c)"), ACT.Copy).then_inc(free[s], 1)
                if n + 2 < H:
                    square(qT, n + 2, s)
                act.wait_ge(free[s], uses("qtok", s, n // 2) + 1)
                o_ = out[6 + v] if i < QB else out[8 + v]
                rows_ = (o_[0, i * P:(i + 1) * P] if i < QB else o_)
                form = {(0, 0): "t h m d -> t (h m d)", (0, 1): "t h d -> t (h d)", (1, 0): "b t h m d -> (b t) (h m d)",
                        (1, 1): "b t h d -> (b t) (h d)"}[(int(i == QB), v)]
                act.dma_start(rows_.rearrange(form), dst).then_inc(tok_put[slot], 16)

            def block_exp(h, i):
                w, par = (i + 1) * P, i % 2
                act.wait_ge(s_max, h * QB + (i + 1))
                act.wait_ge(wp_turned, h * QB + (i + 1))
                for m in range(2):
                    done = A(e01[:, par, m, 0:w], ps[:, 2 * par + m, 0:w], ACT.Exp, bias=l01[:, par, 2 + m:3 + m], scale=SCALE,
                             accum_out=l01[:, par, 4 + m:5 + m])
                done.then_inc(e_done, 1)

            def head_output(h):
                act.wait_ge(pv_full, h + 2)
                A(oT[:, ds(h, 1), 0:SEQ].rearrange("p a t -> p (a t)"), ps[:, 6, :], ACT.Copy).then_inc(head_out, 1)

            def head_pair(k, first=False, final=False):
                for hp in range(2):
                    h = k * 2 + hp
                    for i in range(QB):
                        if i < QB - 1:
                            block_exp(h, i + 1)
                        elif not (final and hp):
                            block_exp(h + 1, 0)
                        if i == 1 and not (first and hp == 0):
                            head_output(h - 1)

            block_exp(0, 0)
            head_pair(0, first=True)
            with act.Fori(1, H // 2 - 1) as k:
                head_pair(k)
            head_pair(H // 2 - 1, final=True)
            head_output(H - 1)

            def page(b, par, u):
                for half in range(2):
                    at = b * PAGES + u
                    act.wait_ge(k_turned, at * 2 + half + 1)
                    if half == 0 and (not isinstance(at, int) or at > 1):
                        act.wait_ge(scored, at - 1)
                    A(kTs[:, u % 2, half], ps[:, ((par * PAGES + u) * 2 + half) % 3, :], ACT.Copy).then_inc(kt_ready, 1)

            def weights(b, par):
                act.wait_ge(m_ready, b)
                q = sc[:, (par - 1) % NBUF]
                A(q, q, ACT.Exp, bias=mq[:, 1, 0:1], scale=SCALE, accum_out=mq[:, 1, 1:2]).then_inc(e_full, 1)

            def sequence(b, par, keys=True, soft=True):
                for u in range(PAGES):
                    if keys:
                        page(b, par, u)
                    if soft and u == 1:
                        weights(b, par)

            sequence(0, 0, soft=False)
            sequence(1, 1)
            with act.Fori(0, (DB - LAG) // NBUF) as i:
                for v in range(NBUF):
                    sequence(i * NBUF + (LAG + v), LAG + v)
            sequence(DB, DB, keys=False)

            act.wait_ge(o_ready, DB + 1)
            split(SLABS["wo"] - DENSE0)
            split(SLABS["wo"] - DENSE0 + 1)
            for s in range(2):
                square(oT, s, s)
            for h in range(H + 2):
                s = h % 2
                if h < H:
                    wait_unit(act, "ohead", s, h // 2)
                    head_root(2 * H + h, 4 * s, s, DV).then_inc(free[s], 1)
                if h + 2 < H:
                    square(oT, h + 2, s)
                if h >= 2:
                    act.wait_ge(head_ready, 2 * H + h + 1)
                    A(hr[:, h - 2, 0, :], oT[:, h - 2, :], ACT.Copy).then_inc(h_high, 1)
            dense("wo")
            root(3)
            apply("up1")
            dense("up1")
            dense("down1", tail=False)
            for i in range(QB + 1):
                s = i % 2
                wait_unit(act, "y", s, i // 2)
                if i >= 2:
                    act.wait_ge(tok_put[s], 16 * ((6, 4)[s] + i // 2))
                A(tok[0:NTOK[i], s, :], ps[0:NTOK[i], 4 * s:4 * s + 2, :].rearrange("p b c -> p (b c)"), ACT.Copy
                  ).then_inc(free[s], 1)
                act.wait_ge(free[s], uses("y", s, i // 2) + 1)
                act.dma_start(out[0][0, i * P:(i + 1) * P] if i < QB else out[1].rearrange("b t d -> (b t) d"),
                              tok[0:NTOK[i], s, :]).then_inc(tok_put[s], 16)

        @block.gpsimd
        def _(pool):
            TT = nc.gpsimd.tensor_tensor
            step = Steps(pool, pool_step)

            nc.gpsimd.memset(ones[:, :], 1.0).then_inc(consts, 1)
            step(nc.gpsimd.memset(ident[:, :], 0.0))
            nc.gpsimd.affine_select(out=ident[:, :], in_=ident[:, :], compare_op=ALU.not_equal, fill=1.0, base=0,
                                    pattern=[[-1, P]], channel_multiplier=1).then_inc(consts, 1)
            nc.gpsimd.memset(eps[:, :], EPS).then_inc(consts, 1)
            pool.wait_ge(consts, 3)
            quarter = ident[:, :].rearrange("p (g c) -> p g c", c=32)[:, :, 0:C9]
            step(TT(add4[:, :], quarter[:, 0], quarter[:, 1], ALU.add))
            for g in (2, 3):
                step(TT(add4[:, :], add4[:, :], quarter[:, g], ALU.add))
            nc.gpsimd.memset(cond[:, :, :].rearrange("p k c -> p (k c)"), 0.0).then_inc(cond_ready, 1)

            def squares(n):
                pool.wait_ge(x_ready, KD * (n - 1) + 1)
                for h in range(2):
                    q = slice(h * HALF, (h + 1) * HALF)
                    done = TT(sqs[:, q], x[:, 0, q], x[:, 0, q], ALU.mult)
                step(done)
                with step.loop(1, KD - 1, 4) as k:
                    pool.wait_ge(x_ready, KD * (n - 1) + 1 + k)
                    for h in range(2):
                        q = slice(h * HALF, (h + 1) * HALF)
                        step(TT(sqt[:, :], tile(x, k)[:, q], tile(x, k)[:, q], ALU.mult))
                        step(TT(sqs[:, q], sqs[:, q], sqt[:, :], ALU.add))
                nc.gpsimd.memset(mark[:, n:n + 1], 0.0).then_inc(sq_ready, 1)

            def cmul_pool(o_re, o_im, a_re, a_im, b_re, b_im, u, v):
                TT(u, a_re, b_re, ALU.mult)
                step(TT(v, a_im, b_im, ALU.mult))
                step(TT(o_re, u, v, ALU.subtract))
                TT(u, a_re, b_im, ALU.mult)
                step(TT(v, a_im, b_re, ALU.mult))
                step(TT(o_im, u, v, ALU.add))

            pool.wait_ge(bbar_ready, 1)
            u_, v_ = (t[:, :].rearrange("p (j q) -> p j q", q=PP) for t in (pA, pB))
            for s in range(CH // 2):
                p_ = [pw[:, CH - 1 - s, r].unsqueeze(2).to_broadcast([P, J, PP]) for r in range(2)]
                cmul_pool(vmat[:, 0, :, s, :], vmat[:, 1, :, s, :], p_[0], p_[1], bbar[:, 0], bbar[:, 1], u_, v_)
            nc.gpsimd.memset(mark[:, 4:5], 0.0).then_inc(v_ready, 1)

            def modulation(n):
                c = COUNT[f"ada{n}"]
                for s in range(2):
                    pool.wait_ge(free[s], ADA_END[n][s])
                step(TT(mod[:, n, 0:c], mod[:, n, 0:c], vec[:, BIAS[n]:BIAS[n] + c].unsqueeze(2).to_broadcast([P, c, C9]), ALU.add))
                g = vec[:, NORM[n]:NORM[n] + KD].unsqueeze(2).to_broadcast([P, KD, C9])
                step(TT(gain[:, n], mod[:, n, KD:2 * KD], g, ALU.mult))
                TT(gain[:, n], gain[:, n], g, ALU.add).then_inc(mod_ready, 1)
                pool.wait_ge(mod_ready, n + 1)

            def sample_part(s, m, k, b0, at, dst):
                pool.wait_ge(t1_ready, at)
                g = by_token(gain[:, m, ds(k, 1), 1:C9].rearrange("p a c -> p (a c)"))
                sh = by_token(cols(m, 0, k, 1, C9))
                step(TT(sample(t1[:, s, :]), sample(t1[:, s, :]), g, ALU.mult))
                TT(dst, sample(t1[:, s, :]), sh, ALU.add).then_inc(t2_sample, 1)

            def apply(name):
                _, m, _h = APPLY[name]
                b0 = KD * ORDER.index(name)
                with step.loop(0, KD // 2, 2) as i:
                    for s in range(2):
                        sample_part(s, m, i * 2 + s, b0, b0 + s + 1 + i * 2, sample(t2[:, s, :]))

            modulation(0)
            for k in range(KD):
                if k >= 2:
                    pool.wait_ge(u_put[k % 2], 16 * (k // 2))
                sample_part(k % 2, 0, k, 0, k + 1, chunks_sample(t2[:, k % 2, :]))
            for s in range(2):
                wait_unit(pool, "ssm_w", s, 1)
            nc.gpsimd.memset(vk[:, :], 0.0).then_inc(kmat_zero, 1)
            modulation(1)
            modulation(2)
            modulation(3)
            modulation(4)
            squares(1)
            apply("up0")
            squares(2)
            apply("kv")
            step(nc.gpsimd.memset(blockd[:, :], 0.0))
            for m in range(2):
                nc.gpsimd.memset(blockd[m * DK:(m + 1) * DK, m * DK:(m + 1) * DK], 1.0)
            step(nc.gpsimd.memset(causal[:, :], 0.0))
            masks = causal[:, :].rearrange("k (r t) -> k r t", t=CH)
            nc.gpsimd.affine_select(out=masks, in_=masks, compare_op=ALU.is_ge, fill=MASKED, base=0,
                                    pattern=[[0, P // CH], [1, CH]], channel_multiplier=-1).then_inc(blocks_ready, 1)
            apply("q")
            pool.wait_ge(head_ready, 2 + 2 * H)
            step(nc.gpsimd.memset(tri[:, :], 0.0))
            step(nc.gpsimd.affine_select(out=tri[:, :], in_=tri[:, :], compare_op=ALU.is_ge, fill=MASKED, base=0,
                                         pattern=[[-1, P]], channel_multiplier=1))
            for s in range(2):
                pool.wait_ge(free[s], USES["attn"][s])
            for c, (signal, n) in enumerate(((e_done, 2), (wp_copied, 2), (wp_turned, 2), (pv_full, 1), (head_out, 1))):
                nc.gpsimd.memset(mark[:, 12 + c:13 + c], 0.0).then_inc(signal, n)

            def head(h, hp):
                nc.gpsimd.tensor_copy(qh[:, hp, :], tile(qT, h)[:, 0:SEQ])
                nc.gpsimd.tensor_copy(kh[:, hp, :], tile(kT, h)[:, 0:SEQ])
                nc.gpsimd.tensor_copy(vh[:, hp], vtok[:, :, ds(h, 1), :].rearrange("p k a d -> p k (a d)")).then_inc(head_in, 1)

            for hp in range(2):
                head(hp, hp)
            with pool.Fori(1, H // 2) as k:
                for hp in range(2):
                    pool.wait_ge(pv_full, k * 2 + hp)
                    head(k * 2 + hp, hp)
            pool.wait_ge(head_out, H + 1)
            for s in range(2):
                pool.wait_ge(tok_put[s], 16 * (6, 4)[s])
            nc.gpsimd.memset(mark[:, 9:10], 0.0).then_inc(v_used, 4)
            step(nc.gpsimd.memset(qn[:, :].rearrange("p b h c -> p (b h c)"), 0.0))
            quarter = ident[:, :].rearrange("p (g c) -> p g c", c=32)
            TT(pick[:, :].rearrange("p (g t) -> p g t", t=CH), quarter[:, :, 0:CH], quarter[:, :, CH:2 * CH], ALU.add)
            TT(sign[:, 1:2], ones[:, 0:1], neglam[:, :], ALU.subtract).then_inc(sinit, 1)

            def new_keys(b, buf):
                for m in range(2):
                    q = slice(m * DK, (m + 1) * DK)
                    for o in range(2):
                        at = o * HQ + m * CH
                        step(nc.gpsimd.tensor_copy(qn[q, buf, o::2, at:at + CH], qT[q, o::2, ds(b * CH + SEQ, CH)]))
                nc.gpsimd.tensor_copy(kn[:, buf], kT[:, :, ds(b * CH + SEQ, CH)]).then_inc(kn_ready, 1)

            def new_values(b):
                if not isinstance(b, int) or b > 0:
                    pool.wait_ge(vn_used, b)
                pool.dma_start(vn[:, :], out[9][ds(b, 1)].rearrange("b t h d -> t (b h d)")).then_inc(vn_full, 16)

            for b in range(NBUF):
                new_keys(b, b)
            new_values(0)
            for b in range(NBUF, DB):
                new_values(b - LAG)
                pool.wait_ge(new_scored, b - NBUF + 1)
                new_keys(b, b % NBUF)
            for b in range(DB - LAG, DB):
                new_values(b)
            for k in range(H):
                pool.wait_ge(h_high, 4 * KD + 1 + k)
                TT(hr[:, k, 1, :], oT[:, k, :], hr[:, k, 0, :].bitcast(F32), ALU.subtract).then_inc(h_ready, 1)
            squares(3)
            apply("up1")

        @block.vector
        def _(dve):
            TT, TS, STT = nc.vector.tensor_tensor, nc.vector.tensor_scalar, nc.vector.scalar_tensor_tensor
            CP, RED, REC = nc.vector.tensor_copy, nc.vector.tensor_reduce, nc.vector.reciprocal
            step = Steps(dve, dve_step)

            dve.wait_ge(in_small, 16 * SMALL)
            CP(v3[64:96, :].rearrange("p (g n) -> p g n", g=2), lst[64:96, :].unsqueeze(2).to_broadcast([32, 2, N])
               ).then_inc(v3_built, 1)
            for k in range(2):
                step(TT(ltmp[:, k, :], lrow[:, 2 * k, :], lrow[:, 2 * k + 1, :], ALU.mult))
            RED(lsum[:, 0:2], ltmp[:, :, :], AX_X, ALU.add)
            wait_unit(dve, "small", 0)
            CP(vec[:, 0:123], ps[:, 0, 0:123])
            CP(vec[:, P:P + 112], ps[:, 0, P:P + 112])
            CP(vec[:, 2 * P:2 * P + 96], ps[:, 0, 2 * P:2 * P + 96]).then_inc(dt_ready, 1)
            CP(h0[:, :, :].rearrange("p r b -> p (r b)"), ps[:, 1, :]).then_inc(dt_ready, 1)
            CP(cT[:, :, :, :].rearrange("p r j q -> p r (j q)"), ps[:, 2:4, :]).then_inc(free[0], 1)
            lr, li = vec[:, 256:288], vec[:, 288:320]
            T_ = lambda n: tiny[:, n, :]
            dve.wait_ge(sincos_out, 1)
            TT(T_(1), lr, T_(0), ALU.mult)
            step(TT(T_(2), li, T_(0), ALU.mult))
            step(TS(T_(3), T_(2), 1 / (2 * math.pi), ROUND, ALU.mult, ALU.add))
            step(TS(T_(3), T_(3), -ROUND, None, ALU.add))
            step(STT(T_(4), T_(3), -TWO_PI_PARTS[0], T_(2), ALU.mult, ALU.add))
            step(STT(T_(4), T_(3), -TWO_PI_PARTS[1], T_(4), ALU.mult, ALU.add))
            step(STT(T_(4), T_(3), -TWO_PI_PARTS[2], T_(4), ALU.mult, ALU.add))
            step(TS(T_(4), T_(4), PI_BELOW, -PI_BELOW, ALU.min, ALU.max))
            step(STT(T_(5), T_(4), -1.0, T_(4), ALU.mult, ALU.max))
            TS(T_(5), T_(5), -1.0, math.pi / 2, ALU.mult, ALU.add).then_inc(sincos_in, 1)
            dve.wait_ge(sincos_out, 2)
            step(TT(neglam[:, :], lsum[:, 2:3], neglam[:, :], ALU.subtract))
            step(TS(neglam[:, :], neglam[:, :], -LAM_INIT, None, ALU.add))
            TS(gaino[:, :], vec[:, 122:123], 1.0 - LAM_INIT, None, ALU.mult)
            dve.wait_ge(sincos_out, 3)
            nc.vector.memset(pw[:, 0, 0, :], 1.0)
            nc.vector.memset(pw[:, 0, 1, :], 0.0)
            TT(pw[:, 1, 0, :], T_(6), T_(8), ALU.mult)
            step(TT(pw[:, 1, 1, :], T_(6), T_(7), ALU.mult))

            def cmul(o_re, o_im, a_re, a_im, b_re, b_im, u, v):
                TT(u, a_re, b_re, ALU.mult)
                step(TT(v, a_im, b_im, ALU.mult))
                step(TT(o_re, u, v, ALU.subtract))
                TT(u, a_re, b_im, ALU.mult)
                step(TT(v, a_im, b_re, ALU.mult))
                step(TT(o_im, u, v, ALU.add))

            for k in (1, 2, 4):
                u, v = (t[:, 0:k * J].rearrange("p (k j) -> p k j", j=J) for t in (tA, tB))
                a_ = [pw[:, k, r].unsqueeze(1).to_broadcast([P, k, J]) for r in range(2)]
                cmul(pw[:, k + 1:2 * k + 1, 0], pw[:, k + 1:2 * k + 1, 1], a_[0], a_[1], pw[:, 1:k + 1, 0], pw[:, 1:k + 1, 1], u, v)
            TS(pws[:, 1], pw[:, CH, 1], -1.0, None, ALU.mult)
            step(CP(pws[:, 0], pw[:, CH, 1]))
            ni = pw[:, 1, 1, :]
            TS(T_(9), pw[:, 1, 0, :], -1.0, None, ALU.add)
            TT(T_(10), lr, lr, ALU.mult)
            step(TT(T_(11), li, li, ALU.mult))
            step(TT(T_(10), T_(10), T_(11), ALU.add))
            step(REC(T_(10), T_(10)))
            TT(T_(11), T_(9), lr, ALU.mult)
            step(TT(T_(12), ni, li, ALU.mult))
            step(TT(T_(11), T_(11), T_(12), ALU.add))
            step(TT(T_(11), T_(11), T_(10), ALU.mult))
            TT(T_(12), ni, lr, ALU.mult)
            step(TT(T_(13), T_(9), li, ALU.mult))
            step(TT(T_(12), T_(12), T_(13), ALU.subtract))
            step(TT(T_(12), T_(12), T_(10), ALU.mult))
            dve.wait_ge(in_b, 16 * 18)
            u, v = (t[:, :].rearrange("p (j q) -> p j q", q=PP) for t in (tA, tB))
            f = [T_(11 + r).unsqueeze(2).to_broadcast([P, J, PP]) for r in range(2)]
            cmul(bbar[:, 0], bbar[:, 1], f[0], f[1], bmat[:, 0], bmat[:, 1], u, v)
            nc.vector.memset(mark[:, 5:6], 0.0).then_inc(bbar_ready, 1)
            with step.loop(0, TAU, 4) as t:
                p_ = [pw[:, ds(t, 1), r].rearrange("p a j -> p (a j)").unsqueeze(2).to_broadcast([P, J, PP]) for r in range(2)]
                o_ = [cpow[:, :, r, ds(t, 1), :].rearrange("p j a q -> p j (a q)") for r in range(2)]
                TT(u, p_[0], cT[:, 0], ALU.mult)
                step(TT(v, p_[1], cT[:, 1], ALU.mult))
                step(TT(o_[0], u, v, ALU.subtract))
                TT(u, p_[0], cT[:, 1], ALU.mult)
                step(TT(v, p_[1], cT[:, 0], ALU.mult))
                step(STT(o_[1], u, -1.0, v, ALU.mult, ALU.subtract))
            nc.vector.memset(mark[:, 6:7], 0.0).then_inc(cpow_ready, 1)

            def root(n):
                dve.wait_ge(free[0], USES[f"norm{n}"][0] + 1)
                step(REC(rstd[:, :], rstd[:, :]))

            root(0)
            for k in range(KD):
                if k >= 2:
                    dve.wait_ge(t2_prompt, k - 1)
                    dve.wait_ge(t2_sample, k - 1)
                TT(t1[:, k % 2, :], x[:, k, :], rstd[:, :], ALU.mult).then_inc(t1_ready, 1)
            u, v = (t[:, :].rearrange("p (j q) -> p j q", q=PP) for t in (tA, tB))
            for s in range(CH // 2, CH):
                p_ = [pw[:, CH - 1 - s, r].unsqueeze(2).to_broadcast([P, J, PP]) for r in range(2)]
                cmul(vmat[:, 0, :, s, :], vmat[:, 1, :, s, :], p_[0], p_[1], bbar[:, 0], bbar[:, 1], u, v)
            nc.vector.memset(mark[:, 0:1], 0.0).then_inc(v_ready, 1)
            for s in range(2):
                dve.wait_ge(free[s], USES["ssm_w"][s])
            for r in range(2):
                CP(hs[:, 0:DB, r, :], h0[:, r, :].rearrange("p (b j) -> p b j", b=DB))
            step(nc.vector.memset(hs[:, DB], 0.0))
            for s in range(2):
                dve.wait_ge(free[s], USES["ada1.1"][s])
            u, v = (t[:, 0:2 * J].rearrange("p (r j) -> p r j", r=2) for t in (tA, tB))
            a8 = pw[:, CH, 0, :].unsqueeze(1).to_broadcast([P, 2, J])
            UN = 4
            with step.loop(0, PCH // UN, 4 * UN) as i:
                for k in range(UN):
                    c = DB + k + i * UN
                    h_ = hs[:, ds(c, 1)].rearrange("p a r j -> p (a r) j")
                    scaled = step.mark(TT(u, h_, a8, ALU.mult))
                    step.mark(TT(v[:, ::-1, :], h_, pws[:, :, :], ALU.mult))
                    step.wait(scaled)
                    driven = step.mark(TT(u, u, drive[:, ds(c, 1)].rearrange("p a r j -> p (a r) j"), ALU.add))
                    step.wait(driven)
                    step(TT(hs[:, ds(c + 1, 1)].rearrange("p a r j -> p (a r) j"), u, v, ALU.add))
            nc.vector.memset(mark[:, 7:8], 0.0).then_inc(hs_ready, 1)
            u, v = (t[:, :].rearrange("p (b r j) -> p b r j", b=DB, r=2) for t in (tA, tB))
            step(TT(u, hs[:, 0:DB], pw[:, CH, 0, :].unsqueeze(1).unsqueeze(1).to_broadcast([P, DB, 2, J]), ALU.mult))
            step(TT(v[:, :, ::-1, :], hs[:, 0:DB], pws[:, :, :].unsqueeze(1).to_broadcast([P, DB, 2, J]), ALU.mult))
            step(TT(u, u, v, ALU.add))
            TT(hfin[:, :].rearrange("p r b j -> p b r j"), u, drive[:, 0:DB], ALU.add).then_inc(hfin_ready, 1)
            for n in range(4):
                s = n % 2
                wait_unit(dve, f"ssm_y{n // 2}", s)
                if n >= 2:
                    dve.wait_ge(y_put[s], 16 * CH)
                for g in range(2):
                    done = CP(ysb[:, s, :].rearrange("p (j g c) -> p g j c", g=2, c=NCH)[:, g].rearrange("p (b j) c -> p b j c", b=2),
                              ps[:, 4 * s + 2 * g:4 * s + 2 * g + 2, 0:4 * NCH].rearrange("p b (j c) -> p b j c", c=NCH))
                done.then_inc(free[s], 1)

            def split(m, late=0, nk=8):
                slot, w = m % 4, m % 2
                dve.wait_ge(slab_high, m + 1 + late)
                f = lambda t: t.rearrange("p k n -> p (k n)")
                TT(f(ws[:, w, 1, 0:nk, :]), f(raw[:, slot, 0:nk, :]), f(ws[:, w, 0, 0:nk, :]).bitcast(F32), ALU.subtract
                   ).then_inc(raw_done[slot], 1)

            def low(k, s, n):
                dve.wait_ge(h_high, n)
                TT(part(hr, k, 1), t2[:, s, :], part(hr, k, 0).bitcast(F32), ALU.subtract).then_inc(h_ready, 1)

            split(0)
            split(1)
            for k in range(KD + 1):
                if k < KD:
                    s = k % 2
                    dve.wait_ge(y_got[s], 32 * (k // 2 + 1))
                    f = lambda t: t[:, s].rearrange("p s c -> p (s c)")
                    if k >= 2:
                        dve.wait_ge(h_high, k - 1)
                    STT(t1[:, s, :], f(uin), vec[:, 112 + k:113 + k], f(yin), ALU.mult, ALU.add).then_inc(yu_ready, 1)
                if k:
                    low(k - 1, (k - 1) % 2, k)

            def apply(name):
                _, m, hb = APPLY[name]
                with dve.Fori(0, KD // 2) as i:
                    for s in range(2):
                        TT(t1[:, s, :], tile(x, i * 2 + s), rstd[:, :], ALU.mult).then_inc(t1_ready, 1)
                    for s in range(2):
                        low(i * 2 + s, s, hb + s + 1 + i * 2)

            def head(src, h, s, g):
                step(REC(t2[:, s, :], t2[:, s, :]))
                t = tile(src, h)
                STT(t, t, g, t2[:, s, :], ALU.mult, ALU.mult).then_inc(head_ready, 1)

            def dense(name, tail=True):
                units, slabs, per = DENSE[name]
                S, n0 = len(slabs), SLABS[name] - DENSE0
                steps_ = per * {"glu": 1, "q": 1}.get(name, 0)

                def turn(i, last):
                    for u in range(per):
                        s = u % 2
                        at = i * (per // 2) + u // 2
                        k = i * per + u
                        for j in range(S):
                            n = u * S + j
                            if not (last and n + 2 >= per * S):
                                split(n0 + n + 2, i * (per * S), slabs[(j + 2) % S][2] if S == 4 and j < 2 else 8)
                        if name == "kv":
                            continue
                        if name == "q":
                            dve.wait_ge(free[s], uses(name, s, at) + 1)
                            head(kT, k, s, vec[:, 120:121])
                            continue
                        wait_unit(dve, name, s, at)
                        if name.startswith("up"):
                            at_e = (KD if name == "up0" else KD + FT) + k + 1
                            dve.wait_ge(e_ready, at_e)
                            TT(halves(t2[:, s, :]), ps[:, 4 * s + 2:4 * s + 4, 0:HALF], halves(t1[:, s, :]), ALU.mult
                               ).then_inc(free[s], 1)
                            dve.wait_ge(free[s], uses(name, s, at) + 1)
                            dve.wait_ge(g_high, (0 if name == "up0" else FT) + k + 1)
                            TT(part(gr, k, 1), t2[:, s, :], part(gr, k, 0).bitcast(F32), ALU.subtract).then_inc(g_ready, 1)
                            continue
                        gate = GATE[name]
                        g, gs = cols(gate, 2, k, 0, 1), by_token(cols(gate, 2, k, 1, C9))
                        xk = tile(x, k)
                        if name == "glu":
                            dve.wait_ge(e_ready, k + 1)
                            TT(halves(t2[:, s, :]), ps[:, 4 * s:4 * s + 2, 0:HALF], halves(t1[:, s, :]), ALU.mult
                               ).then_inc(free[s], 1)
                            dve.wait_ge(free[s], uses(name, s, at) + 1)
                            STT(xk[:, 0:SEQ], t2[:, s, 0:SEQ], g, xk[:, 0:SEQ], ALU.mult, ALU.add)
                            step(TT(sample(t2[:, s, :]), sample(t2[:, s, :]), gs, ALU.mult))
                        else:
                            STT(xk[:, 0:HALF], ps[:, 4 * s, 0:HALF], g, xk[:, 0:HALF], ALU.mult, ALU.add)
                            STT(xk[:, HALF:SEQ], ps[:, 4 * s + 1, 0:SEQ - HALF], g, xk[:, HALF:SEQ], ALU.mult, ALU.add)
                            TT(sample(t2[:, s, :]), ps[:, 4 * s + 1, SEQ - HALF:HALF].rearrange("p (b t) -> p b t", b=DB), gs,
                               ALU.mult).then_inc(free[s], 1)
                            dve.wait_ge(free[s], uses(name, s, at) + 1)
                        TT(xk[:, SEQ:T], xk[:, SEQ:T], t2[:, s, SEQ:T], ALU.add).then_inc(x_ready, 1)

                full_turns = units // per - (0 if tail else 1)
                with step.loop(0, full_turns, steps_) as i:
                    turn(i, False)
                if not tail:
                    turn(units // per - 1, True)

            dense("glu")
            root(1)
            apply("up0")
            dense("up0")
            dense("down0")
            root(2)
            apply("kv")
            dense("kv")
            apply("q")
            nc.vector.memset(mark[:, 8:9], 0.0).then_inc(head_ready, 2)
            dense("q", tail=False)

            for n in range(H):
                dve.wait_ge(root_head, n + 1)
                head(qT, n, n % 2, vec[:, 121:122])
            def block_max(h, i):
                w, par = (i + 1) * P, i % 2
                bank = ps[:, 2 * par:2 * par + 2]
                dve.wait_ge(s_full, h * QB + (i + 1))
                step(TT(bank[:, :, i * P:w], bank[:, :, i * P:w], tri[:, :].unsqueeze(1).to_broadcast([P, 2, P]), ALU.add))
                step(RED(l01[:, par, 0:2], bank[:, :, 0:w], AX_X, ALU.max))
                TS(l01[:, par, 2:4], l01[:, par, 0:2], -SCALE, None, ALU.mult).then_inc(s_max, 1)

            def block_weights(h, i):
                w, par = (i + 1) * P, i % 2
                l_, e0, e1 = l01[:, par], e01[:, par, 0, 0:w], e01[:, par, 1, 0:w]
                dve.wait_ge(e_done, h * QB + (i + 3))
                step(REC(l_[:, 6:8], l_[:, 4:6]))
                step(TT(l_[:, 7:8], l_[:, 7:8], neglam[:, :], ALU.mult))
                step(TS(e1, e1, l_[:, 7:8], None, ALU.mult))
                STT(e0, e0, l_[:, 6:7], e1, ALU.mult, ALU.add).then_inc(w_done, 1)

            def block_turned(h, i):
                w = (i + 1) * P
                dve.wait_ge(wp_turned, h * QB + (i + 3))
                if i == 0:
                    dve.wait_ge(pv_full, h + 1)
                CP(wtT[:, 0:i + 1, i * P:w], ps[:, 4 + i % 2, 0:w].rearrange("p (k q) -> p k q", q=P)).then_inc(wp_copied, 1)

            def head_pair(k, first=False, final=False):
                for hp in range(2):
                    h = k * 2 + hp
                    for i in range(QB):
                        if i < QB - 1:
                            block_max(h, i + 1)
                        elif not (final and hp):
                            block_max(h + 1, 0)
                        block_weights(h, i)
                        if i:
                            block_turned(h, i - 1)
                        elif not (first and hp == 0):
                            block_turned(h - 1, QB - 1)

            dve.wait_ge(head_in, 1)
            block_max(0, 0)
            head_pair(0, first=True)
            with step.loop(1, H // 2 - 2, 2 * QB * 5) as k:
                head_pair(k)
            head_pair(H // 2 - 1, final=True)
            block_turned(H - 1, QB - 1)

            dve.wait_ge(sinit, 1)
            first_map = ident[:, :].rearrange("p (r m t) -> p r m t", m=2, t=CH)[:, :, 0, :]
            step(RED(sign[:, 0:1], first_map, mybir.AxisListType.XY, ALU.add))
            step(TT(sign[:, 0:1], sign[:, 0:1], sign[:, 1:2], ALU.mult))
            step(TT(sign[:, 0:1], sign[:, 0:1], neglam[:, :], ALU.add))
            nc.vector.memset(ps[:, 6, 0:2 * DV], 0.0).then_inc(o_copied, 1)
            nc.vector.memset(mark[:, 10:11], 0.0).then_inc(wt_copied, 1)
            nc.vector.memset(mark[:, 11:12], 0.0).then_inc(o_ready, 1)

            def scores(b, par, q):
                dst = sc[:, par % NBUF, q * BANK:(q + 1) * BANK]
                dve.wait_ge(scored, b * PAGES + 4 * q + 4)
                CP(dst, ps[:, 4 + q % 2, :]).then_inc(s_copied, 1)
                dve.wait_ge(s_copied, b * 4 + q + 1)
                RED(mq[:, 0, q:q + 1], dst, AX_X, ALU.max)

            def new_scores(b, par):
                dst = sc[:, par % NBUF, PAGES * P:]
                dve.wait_ge(new_scored, b + 1)
                step(CP(dst, ps[:, 3, 0:CH]))
                step(RED(mq[:, 0, 4:5], dst, AX_X, ALU.max))
                step(RED(mq[:, 0, 5:6], mq[:, 0, 0:5], AX_X, ALU.max))

            def bias(b):
                if not isinstance(b, int) or b > 0:
                    dve.wait_ge(e_full, b)
                TS(mq[:, 1, 0:1], mq[:, 0, 5:6], -SCALE, None, ALU.mult).then_inc(m_ready, 1)

            def normalize(b, par):
                dve.wait_ge(e_full, b)
                step(REC(mq[:, 1, 2:3], mq[:, 1, 1:2]))
                step(TT(mq[:, 1, 3:4], mq[:, 1, 2:3], sign[:, 0:1], ALU.mult))
                q = sc[:, (par - 1) % NBUF]
                TS(q, q, mq[:, 1, 3:4], None, ALU.mult).then_inc(w_ready, 1)

            def weights(b, q):
                dve.wait_ge(w_turned, (b - LAG) * 5 + q + 1)
                if q == 4:
                    CP(wn[:, :], ps[0:CH, 7, 0:P]).then_inc(wt_copied, 1)
                    return
                if q:
                    dve.wait_ge(v_used, (b - LAG) * PAGES + 4 * q)
                CP(wT[:, q % 2, :], ps[:, 7, :]).then_inc(wt_copied, 1)

            def outputs(b):
                dve.wait_ge(vn_used, b - LAG + 1)
                CP(osb[:, :], ps[:, 6, 0:2 * DV]).then_inc(o_copied, 1)
                dve.wait_ge(o_turned, b - LAG + 1)
                CP(oT[:, :, ds((b - LAG) * CH + SEQ, CH)], ps[:, 3, 4 * CH:12 * CH].rearrange("p (h t) -> p h t", t=CH)
                   ).then_inc(o_ready, 1)

            def sequence(b, par, keys=True, vals=True, soft=True):
                if vals:
                    weights(b, 0)
                if soft:
                    normalize(b, par)
                for q in range(4):
                    if vals:
                        weights(b, q + 1)
                    if keys:
                        scores(b, par, q)
                if keys:
                    new_scores(b, par)
                    bias(b)
                if vals:
                    outputs(b)

            sequence(0, 0, vals=False, soft=False)
            sequence(1, 1, vals=False)
            with step.loop(0, (DB - LAG) // NBUF, 5 * NBUF) as i:
                for v in range(NBUF):
                    sequence(i * NBUF + (LAG + v), LAG + v)
            sequence(DB, DB, keys=False)
            sequence(DB + 1, DB + 1, keys=False, soft=False)
            split(SLABS["wo"] - DENSE0)
            split(SLABS["wo"] - DENSE0 + 1)
            with step.loop(0, H // 2, 2) as i:
                for s in range(2):
                    dve.wait_ge(free[s], uses("ohead", s, i) + 1)
                    head(oT, i * 2 + s, s, gaino[:, 0:1])
            dense("wo")
            root(3)
            apply("up1")
            dense("up1")
            dense("down1", tail=False)


INPUTS = ["x_prompt", "x_sample", "state_ssm_re", "state_ssm_im", "cache_k", "cache_v", "page_table", "c_prompt",
          "c_sample", "norm_mix", "w_ada_mix", "b_ada_mix", "norm_ffn", "w_ada_ffn", "b_ada_ffn", "ffn_w13", "ffn_w2",
          "ssm_lam_re", "ssm_lam_im", "ssm_log_step", "ssm_b_re", "ssm_b_im", "ssm_c_re", "ssm_c_im", "ssm_d",
          "ssm_w_glu", "norm_kv", "w_ada_kv", "b_ada_kv", "w_kv", "k_norm", "w_q", "q_norm", "diff_lambda", "subln", "w_o"]


def kernel(**inputs):
    import numpy as np
    import concourse.bacc as bacc
    from concourse.bass_utils import run_bass_kernel_spmd

    nc = bacc.Bacc("TRN2", target_bir_lowering=False, num_devices=1)
    arrays, args = {}, {}
    for name in INPUTS:
        v = np.ascontiguousarray(inputs[name])
        arrays[f"in_{name}"] = v
        args[name] = nc.dram_tensor(f"in_{name}", v.shape, mybir.dt.from_np(v.dtype), kind="ExternalInput").ap()
    xp, xs = inputs["x_prompt"].shape, inputs["x_sample"].shape
    layers, _, groups, states = inputs["state_ssm_re"].shape
    heads, two, dk = inputs["cache_k"].shape[2:]
    dv = inputs["cache_v"].shape[3]
    shapes = [xp, xs] + [(layers, xp[0], groups, states)] * 2 + [(layers, xs[0], groups, states)] * 2 + [
        (*xp[:2], heads, two, dk), (*xp[:2], heads, dv), (*xs[:2], heads, two, dk), (*xs[:2], heads, dv)]
    outs = [nc.dram_tensor(f"out_{i}", s, F32, kind="ExternalOutput").ap() for i, s in enumerate(shapes)]
    yoco_step(nc, args, outs)
    r = run_bass_kernel_spmd(nc, [arrays], core_ids=[0])
    return tuple(r.results[0][f"out_{i}"] for i in range(len(shapes)))
```
